# Optimizing a Trainium2 kernel written in Bass

```python
import math
import jax
import jax.numpy as jnp
from jax import lax
import numpy as np

D_MODEL = 1024
BATCH = 1
SEQ = 128
DEPTH = 1
DEC_BATCH = 1
DEC_SEQ = 512
PAST_LEN = 128

GRID_W = 64
POS_BASE = 10000.0
N_DIR = 2
CONV_W = 4
LN_EPS = 1e-5
RMS_EPS = 1e-6
H_A = 4
DK_A = 128
DV_A = 128
QK_A = H_A * DK_A
W_A = H_A * DV_A
QKV_A = 2 * QK_A + W_A
CHUNK_A = 64
W_B = 512
NB_B = 4
BW_B = W_B // NB_B
LRU_C = 8.0
H_C = 4
DK_C = 128
DV_C = 128
QK_C = H_C * DK_C
W_C = H_C * DV_C
CHUNK_C = 64
N_GROUPS = 4
E_PER_GROUP = 8
N_EXPERTS = N_GROUPS * E_PER_GROUP
TOP_K = 2
D_EXPERT = 256
DN_ALPHA = (2 * DEPTH) ** 0.25
DN_BETA = (8 * DEPTH) ** -0.25
IN_SIZES = (QKV_A, W_B, W_A, N_DIR * H_A, N_DIR * H_A, W_B, QK_C, QK_C, W_C, W_C, N_DIR * H_C, N_DIR * H_C, 3 * D_MODEL)
N_IN = sum(IN_SIZES)

kernel_name = 'hybrid_bidir_deltanet_rglru_mlstm_hmoe_step'

def _flip(a):
    return jnp.flip(a, axis=1)

def _split(a, sizes):
    parts, start = [], 0
    for s in sizes:
        parts.append(a[..., start:start + s])
        start += s
    return parts

def layer_norm(x, g=None, b=None):
    xf = x.astype(jnp.float32)
    mu = jnp.mean(xf, axis=-1, keepdims=True)
    var = jnp.mean(jnp.square(xf - mu), axis=-1, keepdims=True)
    y = (xf - mu) * lax.rsqrt(var + LN_EPS)
    if g is not None:
        y = y * g + b
    return y.astype(x.dtype)

def rms_norm(x, w):
    xf = x.astype(jnp.float32)
    y = xf * lax.rsqrt(jnp.mean(jnp.square(xf), axis=-1, keepdims=True) + RMS_EPS)
    return (y * w).astype(x.dtype)

def _l2norm(a):
    return a * lax.rsqrt(jnp.sum(jnp.square(a), axis=-1, keepdims=True) + RMS_EPS)

def dwconv(x, w):
    k_w, t = w.shape[0], x.shape[1]
    xp = jnp.pad(x, ((0, 0), ((k_w - 1) // 2, k_w // 2), (0, 0)))
    return sum(xp[:, j:j + t] * w[j] for j in range(k_w))

def grid_pos_embed(n_tokens):
    rows = n_tokens // GRID_W
    r, col = jnp.meshgrid(jnp.arange(rows, dtype=jnp.float32), jnp.arange(GRID_W, dtype=jnp.float32), indexing='ij')
    quarter = D_MODEL // 4
    freqs = jnp.exp(-math.log(POS_BASE) * jnp.arange(quarter, dtype=jnp.float32) / quarter)
    ar = r.reshape(-1, 1) * freqs
    ac = col.reshape(-1, 1) * freqs
    return jnp.concatenate([jnp.sin(ar), jnp.cos(ar), jnp.sin(ac), jnp.cos(ac)], axis=-1)

def _to_chunks(a, chunk):
    b, t = a.shape[:2]
    return jnp.moveaxis(a.reshape(b, t // chunk, chunk, *a.shape[2:]), 2, 3)

def _from_chunks(a):
    b, n, h, c, d = a.shape
    return jnp.moveaxis(a, 3, 2).reshape(b, n * c, h, d)

def gated_delta_chunked(q, k, v, g, beta, s0):
    c = CHUNK_A
    qc, kc, vc, gc, bc = (_to_chunks(a, c) for a in (q, k, v, g, beta))
    G = jnp.cumsum(gc, axis=-1)
    causal = jnp.tril(jnp.ones((c, c), dtype=bool))
    strict = jnp.tril(jnp.ones((c, c), dtype=bool), -1)
    decay = jnp.exp(jnp.where(causal, G[..., :, None] - G[..., None, :], -jnp.inf))
    kk = jnp.einsum('bnhid,bnhjd->bnhij', kc, kc)
    strict_l = jnp.where(strict, bc[..., :, None] * kk * decay, 0.0)
    eye = jnp.eye(c, dtype=strict_l.dtype)
    rhs = jnp.concatenate([vc * bc[..., None], kc * (bc * jnp.exp(G))[..., None]], axis=-1)
    sol = lax.linalg.triangular_solve(eye + strict_l, rhs, left_side=True, lower=True)
    dv = v.shape[-1]
    u_v, u_k = sol[..., :dv], sol[..., dv:]
    qk = jnp.where(causal, jnp.einsum('bnhid,bnhjd->bnhij', qc, kc) * decay, 0.0)
    q_dec = qc * jnp.exp(G)[..., None]
    k_dec = kc * jnp.exp(G[..., -1:] - G)[..., None]
    g_end = jnp.exp(G[..., -1])

    def step(s, xs):
        uv, uk, qk_n, qd, kd, ge = xs
        u = uv - jnp.einsum('bhik,bhkv->bhiv', uk, s)
        o = jnp.einsum('bhik,bhkv->bhiv', qd, s) + jnp.einsum('bhij,bhjv->bhiv', qk_n, u)
        s = s * ge[..., None, None] + jnp.einsum('bhik,bhiv->bhkv', kd, u)
        return s, o

    xs = tuple(jnp.moveaxis(a, 1, 0) for a in (u_v, u_k, qk, q_dec, k_dec, g_end))
    s_end, o = lax.scan(step, s0, xs)
    return _from_chunks(jnp.moveaxis(o, 0, 1)), s_end

def delta_mixer(qkv, z, beta_pre, alpha_pre, a_log, dt_bias, norm_w, s0):
    f32 = jnp.float32
    bsz, t, _ = qkv.shape
    qkv = qkv.astype(f32)
    q = _l2norm(qkv[..., :QK_A].reshape(bsz, t, H_A, DK_A)) * DK_A ** -0.5
    k = _l2norm(qkv[..., QK_A:2 * QK_A].reshape(bsz, t, H_A, DK_A))
    v = qkv[..., 2 * QK_A:].reshape(bsz, t, H_A, DV_A)
    beta = jax.nn.sigmoid(beta_pre.astype(f32).reshape(bsz, t, N_DIR, H_A))
    g = -jnp.exp(a_log) * jax.nn.softplus(alpha_pre.astype(f32).reshape(bsz, t, N_DIR, H_A) + dt_bias)
    s0 = s0.astype(f32)
    o_f, s_f = gated_delta_chunked(q, k, v, g[:, :, 0], beta[:, :, 0], s0[:, 0])
    o_b, s_b = gated_delta_chunked(_flip(q), _flip(k), _flip(v), _flip(g[:, :, 1]), _flip(beta[:, :, 1]), s0[:, 1])
    o = o_f + _flip(o_b)
    o = rms_norm(o, norm_w) * jax.nn.silu(z.astype(f32).reshape(bsz, t, H_A, DV_A))
    return o.reshape(bsz, t, W_A).astype(z.dtype), jnp.stack([s_f, s_b], axis=1)

def _linear_combine(e1, e2):
    a1, b1 = e1
    a2, b2 = e2
    return a1 * a2, a2 * b1 + b2

def rglru(x, w_a, b_a, w_x, b_x, lam, h0):
    bsz, t, _ = x.shape
    xb = x.reshape(bsz, t, NB_B, BW_B)
    r = jax.nn.sigmoid(jnp.einsum('btni,nij->btnj', xb, w_a).reshape(bsz, t, W_B) + b_a)
    gi = jax.nn.sigmoid(jnp.einsum('btni,nij->btnj', xb, w_x).reshape(bsz, t, W_B) + b_x)
    log_a = -LRU_C * r * jax.nn.softplus(-lam)
    a = jnp.exp(log_a)
    b = jnp.sqrt(-jnp.expm1(2.0 * log_a)) * (gi * x)
    a_cum, h = lax.associative_scan(_linear_combine, (a, b), axis=1)
    h = h + a_cum * h0[:, None, :]
    return h, h[:, -1]

def lru_mixer(xc, gate_pre, p, h0):
    f32 = jnp.float32
    xc = xc.astype(f32)
    h0 = h0.astype(f32)
    h_f, s_f = rglru(xc, p['lru_wa'][0], p['lru_ba'][0], p['lru_wx'][0], p['lru_bx'][0], p['lru_lambda'][0], h0[:, 0])
    h_b, s_b = rglru(_flip(xc), p['lru_wa'][1], p['lru_ba'][1], p['lru_wx'][1], p['lru_bx'][1], p['lru_lambda'][1], h0[:, 1])
    y = (h_f + _flip(h_b)).astype(gate_pre.dtype) * jax.nn.gelu(gate_pre)
    return y, jnp.stack([s_f, s_b], axis=1)

def mlstm_chunked(q, k, v, i_pre, log_f, c0, n0, m0):
    c = CHUNK_C
    qc, kc, vc, ic, fc = (_to_chunks(a, c) for a in (q, k, v, i_pre, log_f))
    F = jnp.cumsum(fc, axis=-1)
    causal = jnp.tril(jnp.ones((c, c), dtype=bool))
    dmat = jnp.where(causal, F[..., :, None] - F[..., None, :] + ic[..., None, :], -jnp.inf)
    m_intra = jnp.max(dmat, axis=-1)
    qk = jnp.einsum('bnhid,bnhjd->bnhij', qc, kc)
    d_end = F[..., -1:] - F + ic
    m_end = jnp.max(d_end, axis=-1)

    def step(carry, xs):
        cs, ns, ms = carry
        f_n, d_n, mi, qk_n, q_n, k_n, v_n, de, me = xs
        inter = f_n + ms[..., None]
        mt = jnp.maximum(inter, mi)
        w_int = jnp.exp(inter - mt)
        pm = jnp.exp(d_n - mt[..., None]) * qk_n
        num = w_int[..., None] * jnp.einsum('bhik,bhkv->bhiv', q_n, cs) + jnp.einsum('bhij,bhjv->bhiv', pm, v_n)
        den = w_int * jnp.einsum('bhik,bhk->bhi', q_n, ns) + jnp.sum(pm, axis=-1)
        h = num / jnp.maximum(jnp.abs(den), jnp.exp(-mt))[..., None]
        inter_end = f_n[..., -1] + ms
        m_new = jnp.maximum(inter_end, me)
        w_tok = jnp.exp(de - m_new[..., None])
        s_int = jnp.exp(inter_end - m_new)
        c_new = s_int[..., None, None] * cs + jnp.einsum('bhi,bhik,bhiv->bhkv', w_tok, k_n, v_n)
        n_new = s_int[..., None] * ns + jnp.einsum('bhi,bhik->bhk', w_tok, k_n)
        return (c_new, n_new, m_new), h

    xs = tuple(jnp.moveaxis(a, 1, 0) for a in (F, dmat, m_intra, qk, qc, kc, vc, d_end, m_end))
    (c_e, n_e, m_e), h = lax.scan(step, (c0, n0, m0), xs)
    return _from_chunks(jnp.moveaxis(h, 0, 1)), (c_e, n_e, m_e)

def mlstm_mixer(q, k, v, o_pre, i_pre, f_pre, b_i, b_f, norm_w, c0, n0, m0):
    f32 = jnp.float32
    bsz, t, _ = q.shape
    q = q.astype(f32).reshape(bsz, t, H_C, DK_C)
    k = k.astype(f32).reshape(bsz, t, H_C, DK_C) * DK_C ** -0.5
    v = v.astype(f32).reshape(bsz, t, H_C, DV_C)
    i_t = i_pre.astype(f32).reshape(bsz, t, N_DIR, H_C) + b_i
    lf = jax.nn.log_sigmoid(f_pre.astype(f32).reshape(bsz, t, N_DIR, H_C) + b_f)
    c0, n0, m0 = c0.astype(f32), n0.astype(f32), m0.astype(f32)
    h_f, st_f = mlstm_chunked(q, k, v, i_t[:, :, 0], lf[:, :, 0], c0[:, 0], n0[:, 0], m0[:, 0])
    h_b, st_b = mlstm_chunked(_flip(q), _flip(k), _flip(v), _flip(i_t[:, :, 1]), _flip(lf[:, :, 1]), c0[:, 1], n0[:, 1], m0[:, 1])
    h = layer_norm(h_f + _flip(h_b)) * norm_w.reshape(H_C, DV_C)
    y = jax.nn.sigmoid(o_pre) * h.reshape(bsz, t, W_C).astype(o_pre.dtype)
    states = tuple(jnp.stack([a, b], axis=1) for a, b in zip(st_f, st_b))
    return y, states

def token_mixer(h, p, init_state):
    s_delta, s_lru, s_c, s_n, s_m = init_state
    proj = h @ p['w_in']
    qkv_a, x_b, z_a, beta_a, alpha_a, g_b, q_c, k_c, v_c, o_c, i_c, f_c, gates = _split(proj, IN_SIZES)
    y_a, st_a = delta_mixer(jax.nn.silu(dwconv(qkv_a, p['conv_a'])), z_a, beta_a, alpha_a,
                            p['delta_a_log'], p['delta_dt_bias'], p['delta_norm'], s_delta)
    y_b, st_b = lru_mixer(dwconv(x_b, p['conv_b_w']) + p['conv_b_b'], g_b, p, s_lru)
    y_c, st_c = mlstm_mixer(q_c, k_c, v_c, o_c, i_c, f_c, p['mlstm_bi'], p['mlstm_bf'], p['mlstm_norm'], s_c, s_n, s_m)
    gate_a, gate_b, gate_c = jnp.split(jax.nn.sigmoid(gates), 3, axis=-1)
    merged = gate_a * (y_a @ p['w_pa']) + gate_b * (y_b @ p['w_pb']) + gate_c * (y_c @ p['w_pc'])
    return merged @ p['w_out'], (st_a, st_b, *st_c)

def hier_moe(h, p):
    f32 = jnp.float32
    bsz, t, _ = h.shape
    lg = (h @ p['w_rg'] + p['b_rg']).astype(f32)
    p_grp = jnp.max(jax.nn.softmax(lg, axis=-1), axis=-1, keepdims=True)
    g_sel = jnp.argmax(lg, axis=-1)
    le = (h @ p['w_re'] + p['b_re']).astype(f32).reshape(bsz, t, N_GROUPS, E_PER_GROUP)
    le_sel = jnp.einsum('btge,btg->bte', le, jax.nn.one_hot(g_sel, N_GROUPS, dtype=f32))
    top_v, top_i = lax.top_k(le_sel, TOP_K)
    w_top = jax.nn.softmax(top_v, axis=-1) * p_grp
    e_idx = g_sel[..., None] * E_PER_GROUP + top_i
    gate = jnp.einsum('btk,btke->bte', w_top, jax.nn.one_hot(e_idx, N_EXPERTS, dtype=f32)).astype(h.dtype)
    hid = jax.nn.silu(jnp.einsum('btd,edf->btef', h, p['w_e1'])) * jnp.einsum('btd,edf->btef', h, p['w_e3'])
    return jnp.einsum('btef,efd->btd', hid * gate[..., None], p['w_e2'])

def trunk_layer(x, mod, p, init_state):
    shift1, scale1, gate1, shift2, scale2, gate2 = (mod[:, i, None, :] for i in range(6))
    h = layer_norm(x) * (1.0 + scale1) + shift1
    mixed, final_state = token_mixer(h, p, init_state)
    x = layer_norm(DN_ALPHA * x + gate1 * mixed, p['ln1_g'], p['ln1_b'])
    h = layer_norm(x) * (1.0 + scale2) + shift2
    x = layer_norm(DN_ALPHA * x + gate2 * hier_moe(h, p), p['ln2_g'], p['ln2_b'])
    return x, final_state

def zero_states(nb):
    f32 = jnp.float32
    return (jnp.zeros((nb, N_DIR, H_A, DK_A, DV_A), f32), jnp.zeros((nb, N_DIR, W_B), f32),
            jnp.zeros((nb, N_DIR, H_C, DK_C, DV_C), f32), jnp.zeros((nb, N_DIR, H_C, DK_C), f32),
            jnp.zeros((nb, N_DIR, H_C), f32))

def setup_inputs(seed: int = 0) -> dict:
    key = jax.random.key(seed)
    k = jax.random.split(key, 48)
    f32 = jnp.float32

    def nrm(i, shape, scale=1.0):
        return scale * jax.random.normal(k[i], shape, f32)

    def uni(i, shape, lo, hi):
        return jax.random.uniform(k[i], shape, f32, lo, hi)

    dt = jnp.exp(uni(14, (DEPTH, N_DIR, H_A), math.log(1e-3), math.log(1e-1)))
    a_lru = uni(22, (DEPTH, N_DIR, W_B), 0.9, 0.999) ** (1.0 / LRU_C)
    return {
        'x_prompt': nrm(0, (BATCH, SEQ, D_MODEL)),
        'x_sample': nrm(1, (DEC_BATCH, DEC_SEQ, D_MODEL)),
        'state_delta': nrm(2, (DEC_BATCH, DEPTH, N_DIR, H_A, DK_A, DV_A), 0.05),
        'state_lru': nrm(3, (DEC_BATCH, DEPTH, N_DIR, W_B), 0.5),
        'state_mlstm_C': nrm(4, (DEC_BATCH, DEPTH, N_DIR, H_C, DK_C, DV_C), 0.05),
        'state_mlstm_n': nrm(5, (DEC_BATCH, DEPTH, N_DIR, H_C, DK_C), 0.1),
        'state_mlstm_m': 1.0 + nrm(6, (DEC_BATCH, DEPTH, N_DIR, H_C), 0.5),
        'c': nrm(7, (DEC_BATCH, D_MODEL)),
        'c_ctx': nrm(8, (D_MODEL,)),
        'w_mod': nrm(9, (DEPTH, D_MODEL, 6 * D_MODEL), 0.5 * D_MODEL ** -0.5),
        'b_mod': nrm(10, (DEPTH, 6 * D_MODEL), 0.01),
        'w_in': nrm(11, (DEPTH, D_MODEL, N_IN), D_MODEL ** -0.5),
        'conv_a': nrm(12, (DEPTH, CONV_W, QKV_A), CONV_W ** -0.5),
        'delta_a_log': jnp.log(uni(13, (DEPTH, N_DIR, H_A), 1.0, 16.0)),
        'delta_dt_bias': dt + jnp.log(-jnp.expm1(-dt)),
        'delta_norm': 1.0 + nrm(15, (DEPTH, DV_A), 0.02),
        'conv_b_w': nrm(16, (DEPTH, CONV_W, W_B), CONV_W ** -0.5),
        'conv_b_b': nrm(17, (DEPTH, W_B), 0.01),
        'lru_wa': nrm(18, (DEPTH, N_DIR, NB_B, BW_B, BW_B), BW_B ** -0.5),
        'lru_ba': nrm(19, (DEPTH, N_DIR, W_B), 0.01),
        'lru_wx': nrm(20, (DEPTH, N_DIR, NB_B, BW_B, BW_B), BW_B ** -0.5),
        'lru_bx': nrm(21, (DEPTH, N_DIR, W_B), 0.01),
        'lru_lambda': jnp.log(a_lru) - jnp.log1p(-a_lru),
        'mlstm_bi': nrm(23, (DEPTH, N_DIR, H_C), 0.1),
        'mlstm_bf': uni(24, (DEPTH, N_DIR, H_C), 3.0, 6.0),
        'mlstm_norm': 1.0 + nrm(25, (DEPTH, W_C), 0.02),
        'w_pa': nrm(26, (DEPTH, W_A, D_MODEL), W_A ** -0.5),
        'w_pb': nrm(27, (DEPTH, W_B, D_MODEL), W_B ** -0.5),
        'w_pc': nrm(28, (DEPTH, W_C, D_MODEL), W_C ** -0.5),
        'w_out': nrm(29, (DEPTH, D_MODEL, D_MODEL), DN_BETA * D_MODEL ** -0.5),
        'ln1_g': 1.0 + nrm(30, (DEPTH, D_MODEL), 0.02),
        'ln1_b': nrm(31, (DEPTH, D_MODEL), 0.02),
        'ln2_g': 1.0 + nrm(32, (DEPTH, D_MODEL), 0.02),
        'ln2_b': nrm(33, (DEPTH, D_MODEL), 0.02),
        'w_rg': nrm(34, (DEPTH, D_MODEL, N_GROUPS), D_MODEL ** -0.5),
        'b_rg': nrm(35, (DEPTH, N_GROUPS), 0.01),
        'w_re': nrm(36, (DEPTH, D_MODEL, N_EXPERTS), D_MODEL ** -0.5),
        'b_re': nrm(37, (DEPTH, N_EXPERTS), 0.01),
        'w_e1': nrm(38, (DEPTH, N_EXPERTS, D_MODEL, D_EXPERT), D_MODEL ** -0.5),
        'w_e3': nrm(39, (DEPTH, N_EXPERTS, D_MODEL, D_EXPERT), D_MODEL ** -0.5),
        'w_e2': nrm(40, (DEPTH, N_EXPERTS, D_EXPERT, D_MODEL), DN_BETA * D_EXPERT ** -0.5),
    }

def reference(x_prompt, x_sample, state_delta, state_lru, state_mlstm_C, state_mlstm_n, state_mlstm_m, c, c_ctx,
              w_mod, b_mod, w_in, conv_a, delta_a_log, delta_dt_bias, delta_norm, conv_b_w, conv_b_b,
              lru_wa, lru_ba, lru_wx, lru_bx, lru_lambda, mlstm_bi, mlstm_bf, mlstm_norm,
              w_pa, w_pb, w_pc, w_out, ln1_g, ln1_b, ln2_g, ln2_b, w_rg, b_rg, w_re, b_re, w_e1, w_e3, w_e2):
    layers = [dict(w_in=w_in[l], conv_a=conv_a[l], delta_a_log=delta_a_log[l], delta_dt_bias=delta_dt_bias[l],
                   delta_norm=delta_norm[l], conv_b_w=conv_b_w[l], conv_b_b=conv_b_b[l], lru_wa=lru_wa[l],
                   lru_ba=lru_ba[l], lru_wx=lru_wx[l], lru_bx=lru_bx[l], lru_lambda=lru_lambda[l],
                   mlstm_bi=mlstm_bi[l], mlstm_bf=mlstm_bf[l], mlstm_norm=mlstm_norm[l], w_pa=w_pa[l],
                   w_pb=w_pb[l], w_pc=w_pc[l], w_out=w_out[l], ln1_g=ln1_g[l], ln1_b=ln1_b[l], ln2_g=ln2_g[l],
                   ln2_b=ln2_b[l], w_rg=w_rg[l], b_rg=b_rg[l], w_re=w_re[l], b_re=b_re[l], w_e1=w_e1[l],
                   w_e3=w_e3[l], w_e2=w_e2[l]) for l in range(DEPTH)]

    def modulation(cond, l):
        return (jax.nn.silu(cond) @ w_mod[l] + b_mod[l]).reshape(-1, 6, D_MODEL)

    xp = x_prompt
    zero = zero_states(x_prompt.shape[0])
    ctx_states = []
    for l in range(DEPTH):
        xp, st = trunk_layer(xp, modulation(c_ctx[None, :], l), layers[l], zero)
        ctx_states.append(st)
    new_delta, new_lru, new_mc, new_mn, new_mm = (jnp.stack([st[i] for st in ctx_states], axis=1) for i in range(5))

    xs = x_sample + grid_pos_embed(x_sample.shape[1]).astype(x_sample.dtype)
    for l in range(DEPTH):
        cached = (state_delta[:, l], state_lru[:, l], state_mlstm_C[:, l], state_mlstm_n[:, l], state_mlstm_m[:, l])
        xs, _ = trunk_layer(xs, modulation(c, l), layers[l], cached)

    return (xp, xs, new_delta, new_lru, new_mc, new_mn, new_mm)


_drawn_inputs = setup_inputs


def setup_inputs(seed=0):
    import zlib

    import numpy as np

    out = dict(_drawn_inputs(seed))
    spreads = {}
    factors = {'state_delta': 8.0,
     'state_lru': 6.037,
     'state_mlstm_C': 8.0,
     'state_mlstm_n': 8.0,
     'state_mlstm_m': 8.0,
     'delta_norm': 64.0,
     'lru_ba': 37.768,
     'lru_bx': 8.0,
     'mlstm_norm': 64.0,
     'ln1_g': 7.334,
     'ln1_b': 7.674,
     'ln2_g': 7.454,
     'ln2_b': 21.167,
     'b_rg': 64.0,
     'b_re': 64.0,
     'w_rg': 3.917,
     'w_re': 3.945,
     'w_e1': 3.678,
     'w_e3': 3.451,
     'w_e2': 3.429}
    for name, (base, spread) in spreads.items():
        noise = np.random.default_rng([zlib.crc32(name.encode()), seed]).standard_normal(out[name].shape)
        drawn = base * np.exp(spread * noise) if base else spread * noise
        out[name] = jnp.asarray(drawn.astype(out[name].dtype))
    for name, factor in factors.items():
        out[name] = (out[name] * factor).astype(out[name].dtype)
    return out
```

```python
import math

import concourse.bass as bass
from concourse import mybir

F32 = mybir.dt.float32
I32 = mybir.dt.int32
ALU = mybir.AluOpType
ACT = mybir.ActivationFunctionType
AX = mybir.AxisListType.X

P = 128
D = 1024
KD = D // P
T_CTX, T_LAT = 128, 512
T = T_CTX + T_LAT
NT = T // P
H = 4
HD = 128
LN_EPS, RMS_EPS = 1e-5, 1e-6
ALPHA = 2.0 ** 0.25
NG, EPG = 4, 8
NE = NG * EPG
DE = 256
CW = T + 2
LAT = T_CTX + 2
RAW = CW + 3
NEG = -1.0e30
LEVELS = 7

C_ID, C_TRI, C_ONE, C_NEG, C_SU, C_IOTA, C_COL = 0, 128, 384, 512, 768, 896, 1536
C_TOK1, C_TOKP = C_COL + 8, C_COL + 16
N_CONST = C_COL + 32
COLS = [LN_EPS, RMS_EPS, 128 * RMS_EPS, 0.0, 1.0, 0.5]
E_LN, E_RMS, E_RMS128, E_ZERO, E_ONE, E_HALF = [C_COL + i for i in range(6)]
V_BMOD, V_CONVA, V_CONVB, V_CONVBB, V_BA, V_BX, V_LAM, V_DN, V_MN, V_SLRU, V_SN = 0, 48, 96, 112, 116, 124, 132, 140, 141, 145, 153
N_VEC = 161
R_ALOG, R_DT, R_BI, R_BF, R_M, R_BRG, R_BRE = 0, 8, 16, 24, 32, 40, 44
N_ROW = 76
NB_MOD, NB_IN, NB_G = 12, 10, 8
RING = 2


def tok(tt):
    return slice(tt * P, tt * P + P)


def ctok(tt):
    lo = 0 if tt == 0 else LAT + (tt - 1) * P
    return slice(lo, lo + P)


BLOCKS = [("mod", n) for n in range(4)]
BLOCKS += [("in", 0), ("mod", 4), ("in", 1), ("mod", 5), ("in", 2), ("mod", 6), ("mod", 7), ("in", 3), ("mod", 8),
           ("mod", 9), ("in", 4), ("mod", 10), ("in", 5), ("mod", 11)]
BLOCKS += [("in", n) for n in range(6, 10)]


class Steps:

    def __init__(self, nc, name, labels):
        self.sem = nc.alloc_semaphore(name)
        self.at = {x: n + 1 for n, x in enumerate(labels)}
        self.n, self.count = 0, len(labels)
        assert len(self.at) == len(labels), name

    def step(self, *label):
        self.n += 1
        assert self.at[label] == self.n, (label, self.at[label], self.n)
        return self.sem

    def after(self, *label):
        return self.at[label]


class LoopSteps(Steps):

    def credit(self, e):
        e.sem_inc(self.sem, self.count)

    def turn(self):
        self.n = 0

    def after(self, *label, turn):
        return (turn + 1) * self.count + self.at[label]


def program(nc, A, O, dbg=None, stop=99):
    cursor = [0]

    def sb(name, shape, dt=F32):
        n = 4
        for s in shape[1:]:
            n *= s
        off = cursor[0]
        cursor[0] = off + (n + 31) // 32 * 32
        assert cursor[0] <= 229344, (name, cursor[0])
        return nc.alloc_sbuf_tensor_at(name, list(shape), dt, offset=off)

    cursor[0] = (nc.sbuf_base + 63) // 64 * 64
    bank = [nc.alloc_psum_tensor(f"bank{i}", [P, 512], F32) for i in range(8)]

    def bc(ap, *shape):
        return ap.to_broadcast(list(shape))

    def heads(ap, n=HD):
        return ap.rearrange("p (h i) -> p h i", h=H)

    cst = sb("cst", [P, N_CONST])
    lev = sb("lev", [P, 2, LEVELS, P], I32)
    vec = sb("vec", [P, N_VEC])
    row = sb("row", [P, N_ROW])
    cond = sb("cond", [P, KD, 2])
    modc = sb("modc", [P, 48, 2])
    smg = sb("smg", [P, NT, 32])
    hT_off = cursor[0]
    hT = sb("hT", [P, KD, T])
    yA_off = cursor[0]
    yA = sb("yA", [P, H, T])
    yB = sb("yB", [P, H, T])
    yC = sb("yC", [P, H, T])
    ident = cst[:, C_ID:C_ID + P]
    tri = [cst[:, C_TRI + P * d:C_TRI + P * d + P] for d in range(2)]
    ones = cst[:, C_ONE:C_ONE + P]
    neg = [cst[:, C_NEG + P * d:C_NEG + P * d + P] for d in range(2)]
    col = lambda c: cst[:, c:c + 1]
    ring = sb("ring", [P, RING, 4096])

    landed = [nc.alloc_semaphore(f"block_landed{i}") for i in range(RING)]
    used = nc.alloc_semaphore("mod_block_used")
    stored = nc.alloc_semaphore("stored")
    stores = [0]
    N_BLOCK = len(BLOCKS)

    def load_block(sp, n, sem=None, value=0):
        if n < N_BLOCK:
            if n >= RING:
                sp.wait_ge(sem, value)
            sp.dma_start(ring[:, n % RING, :], A["blocks"][n]).then_inc(landed[n % RING], 16)

    def block_ready(pe, n):
        pe.wait_ge(landed[n % RING], 16 * (n // RING + 1))

    def store(sp, out, in_):
        stores[0] += 16
        sp.dma_start(out, in_).then_inc(stored, 16)

    def mod_block(pe, n, m, w_bank):
        block_ready(pe, n)
        for j in range(4):
            for k in range(KD):
                mm = pe.matmul(w_bank[:, 8 * m + 2 * j:8 * m + 2 * j + 2],
                               ring[:, n % RING, 512 * k + P * j:512 * k + P * j + P], cond[:, k, :],
                               start=(k == 0), stop=(k == KD - 1))
        mm.then_inc(used, 1)

    base0 = cursor[0]

    x_sb = sb("x_sb", [P, NT, D])
    pos_sb = sb("pos_sb", [P, NT - 1, D])
    cond_t = sb("cond_t", [P, KD, 2])
    stats = sb("stats", [P, NT, 2, 6])
    mv = sb("mv", [P, NT, 2])
    rstd = sb("rstd", [P, NT])
    got_cst = nc.alloc_semaphore("got_constants")
    got_x = [nc.alloc_semaphore(f"got_x{i}") for i in range(NT)]
    got_pos = nc.alloc_semaphore("got_pos")
    vs = Steps(nc, "ln1_vector", [("cond", 0)] + [(k, t) for t in range(NT) for k in ("stat0", "stat1", "mv")]
               + [(k, t) for t in range(NT) for k in ("rec", "xn")] + [("modc", 0), ("scale1", 0)]
               + [("h", k) for k in range(KD)])
    as_ = Steps(nc, "ln1_scalar", [("tanh", 0)] + [("sqrt", t) for t in range(NT)] + [("hc", k) for k in range(KD)])
    ps = Steps(nc, "ln1_tensor", [("xt", k) for k in range(KD)])
    gs = Steps(nc, "ln1_gpsimd", [("pos", t) for t in range(1, NT)])

    with nc.Block("ln1", no_gpsimd_drain=True) as block:
        @block.sync
        def _(sp):
            sp.dma_start(cond[:], A["cond"]).then_inc(got_cst, 16)
            sp.dma_start(vec[:], A["vecs"]).then_inc(got_cst, 16)
            sp.dma_start(cst[:], A["consts"]).then_inc(got_cst, 16)
            sp.dma_start(row[:], A["rows"].partition_broadcast(P)).then_inc(got_cst, 16)
            load_block(sp, 0)
            sp.dma_start(x_sb[:, 0, :], A["xp"]).then_inc(got_x[0], 16)
            load_block(sp, 1)
            for t in range(1, NT):
                sp.dma_start(x_sb[:, t, :], A["xs"][(t - 1) * P:t * P, :]).then_inc(got_x[t], 16)
            sp.dma_start(pos_sb[:], A["pos"].rearrange("(t p) d -> p t d", p=P)).then_inc(got_pos, 16)
            sp.dma_start(lev[:], A["levels"]).then_inc(got_cst, 16)
            for n in range(4):
                load_block(sp, n + RING, used, n + 1)

        @block.gpsimd
        def _(pool):
            pool.wait_ge(got_pos, 16)
            for t in range(1, NT):
                pool.wait_ge(got_x[t], 16)
                pool.tensor_tensor(x_sb[:, t, :], x_sb[:, t, :], pos_sb[:, t - 1, :], ALU.add).then_inc(gs.step("pos", t), 1)

        @block.scalar
        def _(act):
            act.wait_ge(got_cst, 80)
            act.activation(cond_t[:], cond[:], ACT.Tanh, scale=0.5).then_inc(as_.step("tanh", 0), 1)
            for t in range(NT):
                act.wait_ge(vs.sem, vs.after("mv", t))
                act.activation(rstd[:, t:t + 1], mv[:, t, 1:2], ACT.Sqrt, bias=col(E_LN)).then_inc(as_.step("sqrt", t), 1)
            for k in range(KD):
                act.wait_ge(ps.sem, ps.after("xt", k))
                act.wait_ge(vs.sem, vs.after("scale1", 0))
                act.activation(hT[:, k, 0:P], bank[4 + k % 2][:, 0:P], ACT.Identity, scale=modc[:, 8 + k, 0:1],
                               bias=modc[:, k, 0:1]).then_inc(as_.step("hc", k), 1)

        @block.vector
        def _(dve):
            dve.wait_ge(got_cst, 80)
            dve.wait_ge(as_.sem, as_.after("tanh", 0))
            dve.scalar_tensor_tensor(cond[:], cond_t[:], 1.0, cond[:], ALU.add, ALU.mult).then_inc(vs.step("cond", 0), 1)
            for t in range(NT):
                dve.wait_ge(got_x[t], 16)
                if t:
                    dve.wait_ge(gs.sem, gs.after("pos", t))
                for i in range(2):
                    dve.bn_stats(stats[:, t, i, :], x_sb[:, t, 512 * i:512 * i + 512]).then_inc(vs.step(f"stat{i}", t), 1)
                dve.wait_ge(vs.sem, vs.after("stat1", t))
                dve.bn_aggr(mv[:, t, :], stats[:, t, :, :]).then_inc(vs.step("mv", t), 1)
            for t in range(NT):
                dve.wait_ge(as_.sem, as_.after("sqrt", t))
                dve.reciprocal(rstd[:, t:t + 1], rstd[:, t:t + 1]).then_inc(vs.step("rec", t), 1)
                dve.wait_ge(vs.sem, vs.after("rec", t))
                dve.tensor_scalar(x_sb[:, t, :], x_sb[:, t, :], mv[:, t, 0:1], rstd[:, t:t + 1], ALU.subtract,
                                  ALU.mult).then_inc(vs.step("xn", t), 1)
            dve.wait_ge(used, 4)
            dve.scalar_tensor_tensor(modc[:, 0:16, :], bank[7][:, 0:32].rearrange("p (m c) -> p m c", c=2), 0.5,
                                     bc(vec[:, V_BMOD:V_BMOD + 16].unsqueeze(2), P, 16, 2),
                                     ALU.mult, ALU.add).then_inc(vs.step("modc", 0), 1)
            dve.wait_ge(vs.sem, vs.after("modc", 0))
            dve.tensor_scalar(modc[:, 8:16, :], modc[:, 8:16, :], 1.0, None, ALU.add).then_inc(vs.step("scale1", 0), 1)
            dve.wait_ge(vs.sem, vs.after("scale1", 0))
            for k in range(KD):
                dve.wait_ge(ps.sem, ps.after("xt", k))
                dve.tensor_scalar(hT[:, k, P:T], bank[k % 2][:, :], modc[:, 8 + k, 1:2], modc[:, k, 1:2], ALU.mult,
                                  ALU.add).then_inc(vs.step("h", k), 1)

        @block.tensor
        def _(pe):
            pe.wait_ge(vs.sem, vs.after("cond", 0))
            for n in range(4):
                mod_block(pe, n, n, bank[7])
            pe.wait_ge(vs.sem, vs.after("xn", NT - 1))
            for k in range(KD):
                if k >= 2:
                    pe.wait_ge(vs.sem, vs.after("h", k - 2))
                    pe.wait_ge(as_.sem, as_.after("hc", k - 2))
                for t in range(1, NT):
                    pe.transpose(bank[k % 2][:, (t - 1) * P:t * P], x_sb[:, t, k * P:k * P + P], ident)
                mm = pe.transpose(bank[4 + k % 2][:, 0:P], x_sb[:, 0, k * P:k * P + P], ident)
                mm.then_inc(ps.step("xt", k), 1)


    cursor[0] = base0
    qkv = sb("qkv", [P, 12, CW])
    stage1_keep = cursor[0]
    xc = sb("xc", [P, 4, CW])
    rawc = sb("rawc", [P, 2, RAW])
    yc_half = sb("yc_half", [P, 2, CW])
    tch = sb("tch", [P, 2, CW])
    w_small = sb("w_small", [P, KD, 32])
    tr = sb("tr", [P, T])
    tg = sb("tg", [P, T])
    th = sb("th", [P, T])
    A4 = sb("A4", [P, 4, T])
    Q4 = sb("Q4", [P, 4, T])
    G4 = sb("G4", [P, 4, T])
    HF = yC
    spx = sb("spx", [P, 88])
    spn = sb("spn", [P, 88])
    ea = sb("ea", [P, 8])
    bah = sb("bah", [P, 16])
    cah = sb("cah", [P, 48])
    hn = sb("hn", [P, 2, 8])
    nlru = sb("nlru", [P, 8])
    C1 = 24
    CONV = [c for c in range(C1) if c // 4 in (0, 2, 3, 4)]
    kth = {c: i for i, c in enumerate(CONV)}
    w_lru = sb("w_lru", [P, 2, 2, 4, P])
    got_lru = nc.alloc_semaphore("got_w_lru")
    got_ws = nc.alloc_semaphore("got_w_small")

    def dve_chunk(c):
        out = [("ctx", c)]
        if c in kth:
            out += [("conv", c, j) for j in range(4)]
            if c >= 8:
                out += [("silu", c)]
        return out

    def dve_unit(u):
        return [(k, u) for k in ("gx0", "gx1", "den", "rec", "q")]

    def dve_dir(d):
        out = [("b", d)] + [("scan", d, b, i) for b in range(4) for i in range(2)] + [("state", d)]
        return out + ([("sum", 0)] if d else [])

    lab_v = [("pad", 0), ("prep", 0), ("prep", 1), ("prep", 2), ("sm", 0), ("sm", 1), ("sm", 2), ("sm", 3), ("sm", 4), ("sm", 5)]
    lab_v += [("sm", i) for i in range(6, 12)]
    for c in range(C1):
        lab_v += dve_chunk(c)
        if c in (12, 17):
            lab_v += dve_dir(0 if c == 12 else 1)
        if 8 <= c < 16:
            lab_v += dve_unit(c - 8)
    lab_v += [("y", 0), ("y", 1), ("modc", 0), ("modc", 1)]
    lab_a = [("ea", 0), ("sm", 0), ("sm", 1), ("sm", 2)]
    for c in range(C1):
        lab_a += [("evac", c)] + ([("tanh", c)] if c in kth and c >= 8 else [])
        if 8 <= c < 16:
            lab_a += [(k, c - 8) for k in ("tr0", "tr1", "tg0", "tg1", "a", "th")]
        if c in (11, 15):
            lab_a += [("sqrt", c // 12)]
    lab_a += [("gelu", 0)]
    lab_p = [("small", 0)]
    for c in range(C1):
        lab_p += [("chunk", c)]
        if 7 <= c < 15:
            lab_p += [("lru", c - 7)]
    v1 = Steps(nc, "proj1_vector", lab_v)
    a1 = Steps(nc, "proj1_scalar", lab_a)
    p1 = Steps(nc, "proj1_tensor", lab_p)
    g1 = Steps(nc, "proj1_gpsimd", [("g", i) for i in range(3)])
    first_in = {n: i for i, (kind, n) in enumerate(BLOCKS) if kind == "in"}

    with nc.Block("proj1", no_gpsimd_drain=True) as block:
        @block.sync
        def _(sp):
            sp.dma_start(w_small[:], A["w_small"]).then_inc(got_ws, 16)
            for n in range(4, 18):
                kind, m = BLOCKS[n]
                last = (used, m + 1) if kind == "mod" else (p1.sem, p1.after("chunk", 4 * m + 3))
                load_block(sp, n + RING, *last)
            sp.wait_ge(v1.sem, v1.after("state", 1))
            store(sp, O["lru"], nlru[:])
            sp.wait_ge(stored, stores[0])

        @block.tensor
        def _(pe):
            pe.wait_ge(got_ws, 16)
            for t in range(NT):
                for k in range(KD):
                    mm = pe.matmul(bank[6][:, 32 * t:32 * t + 32], hT[:, k, tok(t)], w_small[:, k, :],
                                   start=(k == 0), stop=(k == KD - 1))
            mm.then_inc(p1.step("small", 0), 1)
            for n in range(4, 18):
                kind, m = BLOCKS[n]
                if kind == "mod":
                    mod_block(pe, n, m, bank[7])
                    continue
                block_ready(pe, n)
                for j in range(4):
                    c = 4 * m + j
                    if c >= 2:
                        pe.wait_ge(a1.sem, a1.after("evac", c - 2))
                        pe.wait_ge(v1.sem, v1.after("ctx", c - 2))
                    lat, ctx = bank[2 * (c % 2)], bank[2 * (c % 2) + 1]
                    for k in range(KD):
                        w = ring[:, n % RING, 512 * k + P * j:512 * k + P * j + P]
                        pe.matmul(lat[:, :], w, hT[:, k, P:T], start=(k == 0), stop=(k == KD - 1))
                        mm = pe.matmul(ctx[:, 0:P], w, hT[:, k, 0:P], start=(k == 0), stop=(k == KD - 1))
                    mm.then_inc(p1.step("chunk", c), 1)
                    if 7 <= c < 15:
                        u = c - 7
                        d, b = u // 4, u % 4
                        if u == 0:
                            pe.wait_ge(v1.sem, v1.after("conv", 3, 3))
                            pe.wait_ge(v1.sem, v1.after("sm", 0))
                            pe.wait_ge(got_lru, 16)
                        else:
                            pe.wait_ge(a1.sem, a1.after("tg1", u - 1))
                        for g in range(2):
                            w = w_lru[:, g, d, b, :]
                            pe.matmul(bank[4 + g][:, :], w, xc[:, b, LAT:CW], start=True, stop=True)
                            mm = pe.matmul(bank[6][:, P * g:P * g + P], w, xc[:, b, 0:P], start=True, stop=True)
                        mm.then_inc(p1.step("lru", u), 1)

        @block.scalar
        def _(act):
            act.dma_start(w_lru[:], A["w_lru"]).then_inc(got_lru, 16)
            act.activation(ea[:], row[:, R_ALOG:R_ALOG + 8], ACT.Exp).then_inc(a1.step("ea", 0), 1)
            act.wait_ge(v1.sem, v1.after("sm", 5))
            act.activation(spn[:], spn[:], ACT.Exp).then_inc(a1.step("sm", 0), 1)
            act.activation(smg[:, :, 0:8], smg[:, :, 0:8], ACT.Tanh, scale=0.5).then_inc(a1.step("sm", 1), 1)
            act.wait_ge(a1.sem, a1.after("sm", 0))
            act.activation(spn[:], spn[:], ACT.Ln, bias=col(E_ONE)).then_inc(a1.step("sm", 2), 1)
            for c in range(C1):
                act.wait_ge(p1.sem, p1.after("chunk", c))
                lat = bank[2 * (c % 2)]
                if c in kth:
                    i = kth[c]
                    if i >= 2:
                        act.wait_ge(v1.sem, v1.after("conv", CONV[i - 2], 3))
                    else:
                        act.wait_ge(v1.sem, v1.after("pad", 0))
                    dst = rawc[:, i % 2, 1 + LAT:1 + CW]
                else:
                    dst = (yB if c < 8 else yA)[:, c % 4, P:T]
                act.activation(dst, lat[:, :], ACT.Copy).then_inc(a1.step("evac", c), 1)
                if c in kth and c >= 8:
                    act.wait_ge(v1.sem, v1.after("conv", c, 3))
                    if kth[c] >= 6:
                        act.wait_ge(v1.sem, v1.after("silu", CONV[kth[c] - 2]))
                    act.activation(tch[:, kth[c] % 2, :], yc_half[:, kth[c] % 2, :], ACT.Tanh).then_inc(a1.step("tanh", c), 1)
                if 8 <= c < 16:
                    u = c - 8
                    act.wait_ge(p1.sem, p1.after("lru", u))
                    if u == 0:
                        act.wait_ge(v1.sem, v1.after("sm", 11))
                    else:
                        act.wait_ge(v1.sem, v1.after("gx1", u - 1))
                        act.wait_ge(v1.sem, v1.after("q", u - 1))
                    for t_, g, n_ in ((tr, 0, "tr"), (tg, 1, "tg")):
                        act.activation(t_[:, P:T], bank[4 + g][:, :], ACT.Tanh, scale=0.5,
                                       bias=bah[:, 8 * g + u:8 * g + u + 1]).then_inc(a1.step(n_ + "0", u), 1)
                        act.activation(t_[:, 0:P], bank[6][:, P * g:P * g + P], ACT.Tanh, scale=0.5,
                                       bias=bah[:, 8 * g + u:8 * g + u + 1]).then_inc(a1.step(n_ + "1", u), 1)
                    act.wait_ge(a1.sem, a1.after("tr1", u))
                    if u >= 4:
                        act.wait_ge(v1.sem, v1.after("scan", 0, u - 4, 1))
                    act.activation(A4[:, u % 4, :], tr[:], ACT.Exp, scale=hn[:, 1, u:u + 1],
                                   bias=hn[:, 1, u:u + 1]).then_inc(a1.step("a", u), 1)
                    act.activation(th[:], tr[:], ACT.Tanh, scale=hn[:, 0, u:u + 1],
                                   bias=hn[:, 0, u:u + 1]).then_inc(a1.step("th", u), 1)
                if c in (11, 15):
                    act.wait_ge(v1.sem, v1.after("q", c - 8))
                    act.activation(Q4[:], Q4[:], ACT.Sqrt, scale=0.5).then_inc(a1.step("sqrt", c // 12), 1)
            act.wait_ge(g1.sem, g1.after("g", 2))
            act.activation(G4[:], G4[:], ACT.Tanh, scale=math.sqrt(2.0 / math.pi)).then_inc(a1.step("gelu", 0), 1)

        @block.gpsimd
        def _(pool):
            pool.wait_ge(a1.sem, a1.after("evac", 7))
            pool.wait_ge(v1.sem, v1.after("ctx", 7))
            pool.wait_ge(v1.sem, v1.after("scan", 1, 3, 1))
            pool.tensor_tensor(G4[:], yB[:], yB[:], ALU.mult).then_inc(g1.step("g", 0), 1)
            pool.wait_ge(g1.sem, g1.after("g", 0))
            pool.tensor_scalar(G4[:], G4[:], 0.044715, 1.0, ALU.mult, ALU.add).then_inc(g1.step("g", 1), 1)
            pool.wait_ge(g1.sem, g1.after("g", 1))
            pool.tensor_tensor(G4[:], G4[:], yB[:], ALU.mult).then_inc(g1.step("g", 2), 1)

        @block.vector
        def _(dve):
            dve.memset(rawc[:], 0.0).then_inc(v1.step("pad", 0), 1)
            dve.tensor_scalar(cah[:], vec[:, V_CONVA:V_CONVA + 48], 0.5, None, ALU.mult).then_inc(v1.step("prep", 0), 1)
            dve.tensor_scalar(bah[:], vec[:, V_BA:V_BA + 16], 0.5, None, ALU.mult).then_inc(v1.step("prep", 1), 1)
            dve.tensor_scalar(spx[:, 80:88], vec[:, V_LAM:V_LAM + 8], -1.0, None, ALU.mult).then_inc(v1.step("prep", 2), 1)
            dve.wait_ge(p1.sem, p1.after("small", 0))
            dve.tensor_copy(smg[:], bank[6][:, 0:160].rearrange("p (t s) -> p t s", s=32)).then_inc(v1.step("sm", 0), 1)
            dve.wait_ge(v1.sem, v1.after("sm", 0))
            dve.tensor_tensor(spx[:, 0:40].rearrange("p (t s) -> p t s", s=8), smg[:, :, 8:16],
                              bc(row[:, R_DT:R_DT + 8].unsqueeze(1), P, NT, 8), ALU.add).then_inc(v1.step("sm", 1), 1)
            dve.tensor_tensor(spx[:, 40:80].rearrange("p (t s) -> p t s", s=8), smg[:, :, 24:32],
                              bc(row[:, R_BF:R_BF + 8].unsqueeze(1), P, NT, 8), ALU.add).then_inc(v1.step("sm", 2), 1)
            dve.tensor_tensor(smg[:, :, 16:24], smg[:, :, 16:24],
                              bc(row[:, R_BI:R_BI + 8].unsqueeze(1), P, NT, 8), ALU.add).then_inc(v1.step("sm", 3), 1)
            dve.wait_ge(v1.sem, v1.after("sm", 2))
            dve.tensor_scalar(spx[:, 40:80], spx[:, 40:80], -1.0, None, ALU.mult).then_inc(v1.step("sm", 4), 1)
            dve.wait_ge(v1.sem, v1.after("sm", 4))
            dve.scalar_tensor_tensor(spn[:], spx[:], -1.0, spx[:], ALU.mult, ALU.min).then_inc(v1.step("sm", 5), 1)
            dve.wait_ge(a1.sem, a1.after("sm", 2))
            dve.scalar_tensor_tensor(spx[:], spx[:], 0.0, spn[:], ALU.max, ALU.add).then_inc(v1.step("sm", 6), 1)
            dve.wait_ge(v1.sem, v1.after("sm", 6))
            dve.scalar_tensor_tensor(smg[:, :, 8:16], spx[:, 0:40].rearrange("p (t s) -> p t s", s=8), -1.0,
                                     bc(ea[:].unsqueeze(1), P, NT, 8), ALU.mult, ALU.mult).then_inc(v1.step("sm", 7), 1)
            dve.tensor_scalar(smg[:, :, 24:32], spx[:, 40:80].rearrange("p (t s) -> p t s", s=8), -1.0, None,
                              ALU.mult).then_inc(v1.step("sm", 8), 1)
            dve.tensor_scalar(hn[:, 0, :], spx[:, 80:88], 4.0, None, ALU.mult).then_inc(v1.step("sm", 9), 1)
            dve.tensor_scalar(hn[:, 1, :], spx[:, 80:88], -4.0, None, ALU.mult).then_inc(v1.step("sm", 10), 1)
            dve.tensor_scalar(smg[:, :, 0:8], smg[:, :, 0:8], 0.5, 0.5, ALU.mult, ALU.add).then_inc(v1.step("sm", 11), 1)

            def chunk(c):
                dve.wait_ge(p1.sem, p1.after("chunk", c))
                ctx = bank[2 * (c % 2) + 1]
                if c not in kth:
                    dve.tensor_copy((yB if c < 8 else yA)[:, c % 4, 0:P], ctx[:, 0:P]).then_inc(v1.step("ctx", c), 1)
                    return
                i = kth[c]
                s_ = i % 2
                dve.tensor_copy(rawc[:, s_, 1:1 + P], ctx[:, 0:P]).then_inc(v1.step("ctx", c), 1)
                dve.wait_ge(v1.sem, v1.after("ctx", c))
                dve.wait_ge(a1.sem, a1.after("evac", c))
                if c < 4:
                    dst = xc[:, c, :]
                    w = [vec[:, V_CONVB + 4 * j + c:V_CONVB + 4 * j + c + 1] for j in range(4)]
                    dve.tensor_scalar(dst, rawc[:, s_, 0:CW], w[0], vec[:, V_CONVBB + c:V_CONVBB + c + 1], ALU.mult,
                                      ALU.add).then_inc(v1.step("conv", c, 0), 1)
                else:
                    dst = yc_half[:, s_, :]
                    w = [cah[:, 12 * j + c - 8:12 * j + c - 7] for j in range(4)]
                    if i >= 6:
                        dve.wait_ge(a1.sem, a1.after("tanh", CONV[i - 2]))
                    dve.tensor_scalar(dst, rawc[:, s_, 0:CW], w[0], None, ALU.mult).then_inc(v1.step("conv", c, 0), 1)
                for j in range(1, 4):
                    dve.wait_ge(v1.sem, v1.after("conv", c, j - 1))
                    dve.scalar_tensor_tensor(dst, rawc[:, s_, j:j + CW], w[j], dst, ALU.mult,
                                             ALU.add).then_inc(v1.step("conv", c, j), 1)
                if c >= 8:
                    dve.wait_ge(a1.sem, a1.after("tanh", c))
                    dve.scalar_tensor_tensor(qkv[:, c - 8, :], tch[:, s_, :], 1.0, dst, ALU.add,
                                             ALU.mult).then_inc(v1.step("silu", c), 1)

            def unit(u):
                b = u % 4
                dve.wait_ge(a1.sem, a1.after("tg1", u))
                dve.scalar_tensor_tensor(G4[:, b, 0:P], tg[:, 0:P], 1.0, xc[:, b, 0:P], ALU.add,
                                         ALU.mult).then_inc(v1.step("gx0", u), 1)
                dve.scalar_tensor_tensor(G4[:, b, P:T], tg[:, P:T], 1.0, xc[:, b, LAT:CW], ALU.add,
                                         ALU.mult).then_inc(v1.step("gx1", u), 1)
                dve.wait_ge(a1.sem, a1.after("th", u))
                dve.tensor_scalar(tr[:], th[:], 1.0, None, ALU.add).then_inc(v1.step("den", u), 1)
                dve.wait_ge(v1.sem, v1.after("den", u))
                dve.reciprocal(tr[:], tr[:]).then_inc(v1.step("rec", u), 1)
                dve.wait_ge(v1.sem, v1.after("rec", u))
                dve.tensor_tensor(Q4[:, b, :], th[:], tr[:], ALU.mult).then_inc(v1.step("q", u), 1)

            def direction(d):
                dve.wait_ge(a1.sem, a1.after("sqrt", d))
                dve.tensor_tensor(G4[:], G4[:], Q4[:], ALU.mult).then_inc(v1.step("b", d), 1)
                dve.wait_ge(v1.sem, v1.after("b", d))
                dve.wait_ge(a1.sem, a1.after("a", 4 * d + 3))
                out = Q4 if d else HF
                for b in range(4):
                    h0 = vec[:, V_SLRU + 4 * d + b:V_SLRU + 4 * d + b + 1]
                    for i, (lo, hi, init) in enumerate(((0, P, 0.0), (P, T, h0))):
                        sl = slice(lo, hi) if d == 0 else slice(hi - 1, lo - 1 if lo else None, -1)
                        dve.tensor_tensor_scan(out[:, b, sl], A4[:, b, sl], G4[:, b, sl], init, ALU.mult,
                                               ALU.add).then_inc(v1.step("scan", d, b, i), 1)
                dve.wait_ge(v1.sem, v1.after("scan", d, 3, 1))
                dve.tensor_copy(nlru[:, 4 * d:4 * d + 4], out[:, :, 0 if d else P - 1]).then_inc(v1.step("state", d), 1)
                if d:
                    dve.tensor_tensor(HF[:], HF[:], Q4[:], ALU.add).then_inc(v1.step("sum", 0), 1)

            for c in range(C1):
                chunk(c)
                if c in (12, 17):
                    direction(0 if c == 12 else 1)
                if 8 <= c < 16:
                    unit(c - 8)
            dve.wait_ge(a1.sem, a1.after("gelu", 0))
            dve.scalar_tensor_tensor(G4[:], G4[:], 1.0, yB[:], ALU.add, ALU.mult).then_inc(v1.step("y", 0), 1)
            dve.wait_ge(v1.sem, v1.after("y", 0))
            dve.scalar_tensor_tensor(yB[:], G4[:], 0.5, HF[:], ALU.mult, ALU.mult).then_inc(v1.step("y", 1), 1)
            dve.wait_ge(used, NB_MOD)
            dve.scalar_tensor_tensor(modc[:, 16:48, :], bank[7][:, 32:96].rearrange("p (m c) -> p m c", c=2), 0.5,
                                     bc(vec[:, V_BMOD + 16:V_BMOD + 48].unsqueeze(2), P, 32, 2),
                                     ALU.mult, ALU.add).then_inc(v1.step("modc", 0), 1)
            dve.wait_ge(v1.sem, v1.after("modc", 0))
            dve.tensor_scalar(modc[:, 32:40, :], modc[:, 32:40, :], 1.0, None, ALU.add).then_inc(v1.step("modc", 1), 1)
    if stop <= 1:
        return dict(locals())

    cursor[0] = stage1_keep
    k_tm = sb("k_tm", [P, NT, H * HD])
    v_tm = sb("v_tm", [P, NT, H * HD])
    stage2_keep = cursor[0]
    sq = sb("sq", [P, 2, CW])
    rs = sb("rs", [P, 2, CW])
    HC = CW // 2
    v2 = Steps(nc, "delta_prep_vector", [(k, i) for i in range(8) for k in ("rec", "norm")] + [("k", t) for t in range(NT)])
    a2 = Steps(nc, "delta_prep_scalar", [("v", t) for t in range(2)] + [("sqrt", i, j) for i in range(8) for j in range(2)]
               + [("v", t) for t in range(2, NT)])
    p2 = Steps(nc, "delta_prep_tensor", [("v", 0), ("v", 1)] + [("sum", i) for i in range(8)] + [("v", t) for t in range(2, NT)]
               + [("k", t) for t in range(NT)])
    g2 = Steps(nc, "delta_prep_gpsimd", [("sq", i) for i in range(8)])
    with nc.Block("delta_prep", no_gpsimd_drain=True) as block:
        @block.gpsimd
        def _(pool):
            for i in range(8):
                if i >= 2:
                    pool.wait_ge(p2.sem, p2.after("sum", i - 2))
                pool.tensor_tensor(sq[:, i % 2, :], qkv[:, i, :], qkv[:, i, :], ALU.mult).then_inc(g2.step("sq", i), 1)

        @block.tensor
        def _(pe):
            def v_tile(t):
                if t >= 2:
                    pe.wait_ge(a2.sem, a2.after("v", t - 2))
                for h in range(H):
                    mm = pe.transpose(bank[4 + t % 2][:, P * h:P * h + P], qkv[:, 8 + h, ctok(t)], ident)
                mm.then_inc(p2.step("v", t), 1)

            v_tile(0)
            v_tile(1)
            for i in range(8):
                pe.wait_ge(g2.sem, g2.after("sq", i))
                if i >= 2:
                    pe.wait_ge(a2.sem, a2.after("sqrt", i - 2, 1))
                for j in range(2):
                    mm = pe.matmul(bank[2 * (i % 2) + j][:, 0:HC], ones, sq[:, i % 2, HC * j:HC * j + HC], start=True, stop=True)
                mm.then_inc(p2.step("sum", i), 1)
            for t in range(2, NT):
                v_tile(t)
            pe.wait_ge(v2.sem, v2.after("norm", 7))
            for t in range(NT):
                if t >= 2:
                    pe.wait_ge(v2.sem, v2.after("k", t - 2))
                for h in range(H):
                    mm = pe.transpose(bank[6 + t % 2][:, P * h:P * h + P], qkv[:, 4 + h, ctok(t)], ident)
                mm.then_inc(p2.step("k", t), 1)

        @block.scalar
        def _(act):
            def v_tile(t):
                act.wait_ge(p2.sem, p2.after("v", t))
                act.activation(v_tm[:, t, :], bank[4 + t % 2][:, :], ACT.Copy).then_inc(a2.step("v", t), 1)

            v_tile(0)
            v_tile(1)
            for i in range(8):
                act.wait_ge(p2.sem, p2.after("sum", i))
                if i >= 2:
                    act.wait_ge(v2.sem, v2.after("norm", i - 2))
                for j in range(2):
                    act.activation(rs[:, i % 2, HC * j:HC * j + HC], bank[2 * (i % 2) + j][:, 0:HC], ACT.Sqrt,
                                   scale=128.0 if i < 4 else 1.0,
                                   bias=col(E_RMS128 if i < 4 else E_RMS)).then_inc(a2.step("sqrt", i, j), 1)
            for t in range(2, NT):
                v_tile(t)

        @block.vector
        def _(dve):
            for i in range(8):
                dve.wait_ge(a2.sem, a2.after("sqrt", i, 1))
                dve.reciprocal(rs[:, i % 2, :], rs[:, i % 2, :]).then_inc(v2.step("rec", i), 1)
                dve.wait_ge(v2.sem, v2.after("rec", i))
                dve.tensor_tensor(qkv[:, i, :], qkv[:, i, :], rs[:, i % 2, :], ALU.mult).then_inc(v2.step("norm", i), 1)
            for t in range(NT):
                dve.wait_ge(p2.sem, p2.after("k", t))
                dve.tensor_copy(k_tm[:, t, :], bank[6 + t % 2][:, :]).then_inc(v2.step("k", t), 1)

    cursor[0] = stage2_keep + 64
    o_f = yC
    o_b = sb("o_b", [P, H, T])

    def two(name, w=H * HD):
        return [sb(f"{name}{d}", [P, w]) for d in range(2)]

    n_, w_, f_, qk_, qd_, kd_, vb_, d_, dt_, s_ = (two(x) for x in ("dl_n", "dl_w", "dl_f", "dl_qk", "dl_qd", "dl_kd",
                                                                    "dl_vb", "dl_d", "dl_dt", "dl_s"))
    gc = two("dl_gc", 12)
    eg = two("dl_eg", 12)
    nb = two("dl_nb", 8)
    got_s = nc.alloc_semaphore("got_delta_state")

    def tile_of(g, d):
        return g if d == 0 or g == 0 else NT - g

    def both(*names):
        return [(x, g, d) for g in range(NT) for x in names for d in range(2)]

    inv = range(1, LEVELS)
    lv3 = both("gtri", "gc", "kd", "nb", "t1", "n0", "nbe", "n1", "qk", "p0", "p1", *[("x", l) for l in inv],
               "w0", "w1", "o", "s0", "s1")
    la3 = both("eg", "egb", "dec", "qdec", *[(x, l) for l in inv for x in ("f", "d") if (x, l) != ("d", LEVELS - 1)], "u")
    lp3 = both("gcol", "gb", "kk", "nt", *[(x, l) for l in inv for x in ("f", "x", "d") if (x, l) != ("d", LEVELS - 1)],
               "ks", "u", "o")
    lg3 = both("init", "m1", "m2", "kd", "vb", "qd")
    v3, a3 = Steps(nc, "delta_vector", [("z", 0), ("z", 1)] + lv3), Steps(nc, "delta_scalar", la3)
    p3, g3 = Steps(nc, "delta_tensor", lp3), Steps(nc, "delta_gpsimd", lg3)
    with nc.Block("delta", no_gpsimd_drain=True) as block:
        @block.sync
        def _(sp):
            for d in range(2):
                sp.wait_ge(v3.sem, v3.after("s1", 0, d))
                store(sp, O["delta"][d], s_[d][:])
            sp.wait_ge(stored, stores[0])
            for d in range(2):
                sp.dma_start(s_[d][:], A["s_delta"][d]).then_inc(got_s, 16)
            sp.wait_ge(got_s, 32)

        @block.tensor
        def _(pe):
            def kt(g, d, h):
                return qkv[:, 4 + h, ctok(tile_of(g, d))]

            def hd(t, h):
                return t[:, P * h:P * h + P]

            for g in range(NT):
                for d in range(2):
                    if g:
                        pe.wait_ge(v3.sem, v3.after("w0", g - 1, d))
                    t = tile_of(g, d)
                    g4 = smg[:, t, 8 + 4 * d:12 + 4 * d]
                    pe.matmul(bank[4 * d][:, 0:4], tri[d], g4, start=True, stop=True)
                    pe.matmul(bank[4 * d][:, 4:8], ones, g4, start=True, stop=True).then_inc(p3.step("gcol", g, d), 1)
                for d in range(2):
                    pe.wait_ge(v3.sem, v3.after("gtri", g, d))
                    if g:
                        pe.wait_ge(a3.sem, a3.after("u", g - 1, d))
                    pe.matmul(bank[4 * d + 1][:, :], ones, n_[d][:], start=True, stop=True).then_inc(p3.step("gb", g, d), 1)
                for d in range(2):
                    if g:
                        pe.wait_ge(v3.sem, v3.after("o", g - 1, d))
                        pe.wait_ge(v3.sem, v3.after("s1", g - 1, d))
                    for h in range(H):
                        pe.matmul(hd(bank[4 * d + 2], h), kt(g, d, h), kt(g, d, h), start=True, stop=True)
                    for h in range(H):
                        mm = pe.matmul(hd(bank[4 * d + 3], h), kt(g, d, h), qkv[:, h, ctok(tile_of(g, d))], start=True, stop=True)
                    mm.then_inc(p3.step("kk", g, d), 1)
                for d in range(2):
                    pe.wait_ge(v3.sem, v3.after("n1", g, d))
                    pe.wait_ge(v3.sem, v3.after("gc", g, d))
                    for h in range(H):
                        mm = pe.transpose(hd(bank[4 * d], h), hd(n_[d], h), ident)
                    mm.then_inc(p3.step("nt", g, d), 1)
                for l in inv:
                    for d in range(2):
                        if l == 1:
                            pe.wait_ge(v3.sem, v3.after("p1", g, d))
                            pe.wait_ge(a3.sem, a3.after("egb", g, d))
                        else:
                            pe.wait_ge(v3.sem, v3.after(("x", l - 1), g, d))
                        for h in range(H):
                            mm = pe.matmul(hd(bank[4 * d + 1], h), hd(n_[d], h), hd(dt_[d], h), start=True, stop=True)
                        mm.then_inc(p3.step(("f", l), g, d), 1)
                    for d in range(2):
                        pe.wait_ge(a3.sem, a3.after(("f", l), g, d))
                        if l > 1:
                            pe.wait_ge(a3.sem, a3.after(("d", l - 1), g, d))
                        for h in range(H):
                            mm = pe.matmul(hd(bank[4 * d + 2], h), hd(d_[d], h), hd(f_[d], h), start=True, stop=True)
                        mm.then_inc(p3.step(("x", l), g, d), 1)
                    if l < LEVELS - 1:
                        for d in range(2):
                            pe.wait_ge(v3.sem, v3.after(("x", l), g, d))
                            if l == 1:
                                pe.wait_ge(v3.sem, v3.after("qk", g, d))
                            for h in range(H):
                                mm = pe.transpose(hd(bank[4 * d + 3], h), hd(dt_[d], h), ident)
                            mm.then_inc(p3.step(("d", l), g, d), 1)
                for d in range(2):
                    if g == 0:
                        pe.wait_ge(v3.sem, v3.after("z", d))
                    elif g == 1:
                        pe.wait_ge(got_s, 32)
                    for h in range(H):
                        mm = pe.matmul(hd(bank[4 * d], h), kt(g, d, h), hd(s_[d], h), start=True, stop=True)
                    mm.then_inc(p3.step("ks", g, d), 1)
                for d in range(2):
                    pe.wait_ge(v3.sem, v3.after("w1", g, d))
                    for h in range(H):
                        mm = pe.matmul(hd(bank[4 * d + 1], h), hd(dt_[d], h), hd(w_[d], h), start=True, stop=True)
                    mm.then_inc(p3.step("u", g, d), 1)
                for d in range(2):
                    pe.wait_ge(a3.sem, a3.after("u", g, d))
                    pe.wait_ge(g3.sem, g3.after("qd", g, d))
                    for h in range(H):
                        pe.matmul(hd(bank[4 * d + 2], h), hd(s_[d], h), hd(qd_[d], h), start=True, stop=False)
                        pe.matmul(hd(bank[4 * d + 2], h), hd(d_[d], h), hd(qk_[d], h), start=False, stop=True)
                    for h in range(H):
                        mm = pe.matmul(hd(bank[4 * d + 3], h), hd(kd_[d], h), hd(d_[d], h), start=True, stop=True)
                    mm.then_inc(p3.step("o", g, d), 1)

        @block.scalar
        def _(act):
            for g in range(NT):
                for d in range(2):
                    act.wait_ge(v3.sem, v3.after("kd", g, d))
                    if g:
                        act.wait_ge(v3.sem, v3.after("s0", g - 1, d))
                    act.activation(eg[d][:], gc[d][:], ACT.Exp).then_inc(a3.step("eg", g, d), 1)
                for d in range(2):
                    act.wait_ge(p3.sem, p3.after("gb", g, d))
                    act.wait_ge(v3.sem, v3.after("t1", g, d))
                    if g:
                        act.wait_ge(p3.sem, p3.after("o", g - 1, d))
                    act.activation(qd_[d][:], bank[4 * d + 1][:, :], ACT.Exp).then_inc(a3.step("egb", g, d), 1)
                for d in range(2):
                    act.wait_ge(g3.sem, g3.after("m1", g, d))
                    act.activation(f_[d][:], f_[d][:], ACT.Exp).then_inc(a3.step("dec", g, d), 1)
                for d in range(2):
                    act.wait_ge(g3.sem, g3.after("m2", g, d))
                    act.activation(qk_[d][:], qk_[d][:], ACT.Exp).then_inc(a3.step("qdec", g, d), 1)
                for l in inv:
                    for d in range(2):
                        act.wait_ge(p3.sem, p3.after(("f", l), g, d))
                        act.activation(f_[d][:], bank[4 * d + 1][:, :], ACT.Copy).then_inc(a3.step(("f", l), g, d), 1)
                    if l < LEVELS - 1:
                        for d in range(2):
                            act.wait_ge(p3.sem, p3.after(("d", l), g, d))
                            act.activation(d_[d][:], bank[4 * d + 3][:, :], ACT.Copy).then_inc(a3.step(("d", l), g, d), 1)
                for d in range(2):
                    act.wait_ge(p3.sem, p3.after("u", g, d))
                    act.activation(d_[d][:], bank[4 * d + 1][:, :], ACT.Copy).then_inc(a3.step("u", g, d), 1)

        @block.gpsimd
        def _(pool):
            for g in range(NT):
                for d in range(2):
                    if g:
                        pool.wait_ge(p3.sem, p3.after("o", g - 1, d))
                    pool.tensor_copy(heads(d_[d][:]), bc(ident.unsqueeze(1), P, H, P)).then_inc(g3.step("init", g, d), 1)
                for d in range(2):
                    pool.wait_ge(v3.sem, v3.after("t1", g, d))
                    pool.tensor_tensor(heads(f_[d][:]), heads(w_[d][:]), bc(neg[d].unsqueeze(1), P, H, P),
                                       ALU.add).then_inc(g3.step("m1", g, d), 1)
                for d in range(2):
                    pool.tensor_tensor(heads(qk_[d][:]), bc(neg[1 - d].unsqueeze(1), P, H, P), heads(w_[d][:]),
                                       ALU.subtract).then_inc(g3.step("m2", g, d), 1)
                for d in range(2):
                    pool.wait_ge(a3.sem, a3.after("eg", g, d))
                    pool.tensor_tensor(heads(kd_[d][:]), heads(k_tm[:, tile_of(g, d), :]),
                                       bc(eg[d][:, 8:12].unsqueeze(2), P, H, HD), ALU.mult).then_inc(g3.step("kd", g, d), 1)
                for d in range(2):
                    t = tile_of(g, d)
                    pool.tensor_tensor(heads(vb_[d][:]), heads(v_tm[:, t, :]),
                                       bc(smg[:, t, 4 * d:4 * d + 4].unsqueeze(2), P, H, HD), ALU.mult).then_inc(g3.step("vb", g, d), 1)
                for d in range(2):
                    pool.wait_ge(a3.sem, a3.after("egb", g, d))
                    pool.tensor_tensor(heads(qd_[d][:]), heads(qd_[d][:]), qkv[:, 0:4, ctok(tile_of(g, d))],
                                       ALU.mult).then_inc(g3.step("qd", g, d), 1)

        @block.vector
        def _(dve):
            for d in range(2):
                dve.memset(s_[d][:], 0.0).then_inc(v3.step("z", d), 1)
            for g in range(NT):
                for d in range(2):
                    g4 = smg[:, tile_of(g, d), 8 + 4 * d:12 + 4 * d]
                    dve.tensor_tensor(heads(n_[d][:]), bc(tri[d].unsqueeze(1), P, H, P), bc(g4.unsqueeze(2), P, H, P),
                                      ALU.mult).then_inc(v3.step("gtri", g, d), 1)
                for d in range(2):
                    dve.wait_ge(p3.sem, p3.after("gcol", g, d))
                    dve.tensor_copy(gc[d][:, 0:8], bank[4 * d][:, 0:8]).then_inc(v3.step("gc", g, d), 1)
                for d in range(2):
                    dve.wait_ge(v3.sem, v3.after("gc", g, d))
                    dve.tensor_tensor(gc[d][:, 8:12], gc[d][:, 4:8], gc[d][:, 0:4], ALU.subtract).then_inc(v3.step("kd", g, d), 1)
                for d in range(2):
                    dve.tensor_scalar(nb[d][:, 0:4], smg[:, tile_of(g, d), 4 * d:4 * d + 4], -1.0, None,
                                      ALU.mult).then_inc(v3.step("nb", g, d), 1)
                for d in range(2):
                    dve.wait_ge(p3.sem, p3.after("gb", g, d))
                    dve.tensor_tensor(heads(w_[d][:]), bc(gc[d][:, 0:4].unsqueeze(2), P, H, P), heads(bank[4 * d + 1][:, :]),
                                      ALU.subtract).then_inc(v3.step("t1", g, d), 1)
                for d in range(2):
                    dve.wait_ge(p3.sem, p3.after("kk", g, d))
                    dve.wait_ge(a3.sem, a3.after("dec", g, d))
                    dve.tensor_tensor(n_[d][:], bank[4 * d + 2][:, :], f_[d][:], ALU.mult).then_inc(v3.step("n0", g, d), 1)
                for d in range(2):
                    dve.wait_ge(a3.sem, a3.after("eg", g, d))
                    dve.wait_ge(v3.sem, v3.after("nb", g, d))
                    dve.tensor_tensor(nb[d][:, 4:8], nb[d][:, 0:4], eg[d][:, 0:4], ALU.mult).then_inc(v3.step("nbe", g, d), 1)
                for d in range(2):
                    dve.wait_ge(v3.sem, v3.after("n0", g, d))
                    dve.tensor_tensor(heads(n_[d][:]), heads(n_[d][:]), bc(nb[d][:, 0:4].unsqueeze(2), P, H, P),
                                      ALU.mult).then_inc(v3.step("n1", g, d), 1)
                for d in range(2):
                    dve.wait_ge(a3.sem, a3.after("qdec", g, d))
                    dve.tensor_tensor(qk_[d][:], bank[4 * d + 3][:, :], qk_[d][:], ALU.mult).then_inc(v3.step("qk", g, d), 1)
                for d in range(2):
                    dve.wait_ge(g3.sem, g3.after("init", g, d))
                    dve.tensor_copy(dt_[d][:], d_[d][:]).then_inc(v3.step("p0", g, d), 1)
                for d in range(2):
                    dve.wait_ge(v3.sem, v3.after("p0", g, d))
                    dve.wait_ge(v3.sem, v3.after("n1", g, d))
                    dve.copy_predicated(heads(d_[d][:]), bc(lev[:, d, 0, :].unsqueeze(1), P, H, P), heads(n_[d][:]))
                    dve.wait_ge(p3.sem, p3.after("nt", g, d))
                    dve.copy_predicated(heads(dt_[d][:]), bc(lev[:, 1 - d, 0, :].unsqueeze(1), P, H, P),
                                        heads(bank[4 * d][:, :])).then_inc(v3.step("p1", g, d), 1)
                for l in inv:
                    for d in range(2):
                        dve.wait_ge(p3.sem, p3.after(("x", l), g, d))
                        dve.copy_predicated(heads(dt_[d][:]), bc(lev[:, 1 - d, l, :].unsqueeze(1), P, H, P),
                                            heads(bank[4 * d + 2][:, :])).then_inc(v3.step(("x", l), g, d), 1)
                for d in range(2):
                    dve.wait_ge(p3.sem, p3.after("ks", g, d))
                    dve.wait_ge(g3.sem, g3.after("vb", g, d))
                    dve.tensor_tensor(heads(w_[d][:]), heads(bank[4 * d][:, :]), bc(nb[d][:, 4:8].unsqueeze(2), P, H, HD),
                                      ALU.mult).then_inc(v3.step("w0", g, d), 1)
                for d in range(2):
                    dve.wait_ge(v3.sem, v3.after("w0", g, d))
                    dve.tensor_tensor(w_[d][:], w_[d][:], vb_[d][:], ALU.add).then_inc(v3.step("w1", g, d), 1)
                for d in range(2):
                    dve.wait_ge(p3.sem, p3.after("o", g, d))
                    dve.tensor_copy((o_b if d else o_f)[:, :, tok(tile_of(g, d))],
                                    heads(bank[4 * d + 2][:, :])).then_inc(v3.step("o", g, d), 1)
                if g == 1:
                    dve.wait_ge(got_s, 32)
                for d in range(2):
                    dve.wait_ge(a3.sem, a3.after("eg", g, d))
                    dve.tensor_tensor(heads(s_[d][:]), heads(s_[d][:]), bc(eg[d][:, 4:8].unsqueeze(2), P, H, HD),
                                      ALU.mult).then_inc(v3.step("s0", g, d), 1)
                for d in range(2):
                    dve.wait_ge(v3.sem, v3.after("s0", g, d))
                    dve.tensor_tensor(s_[d][:], s_[d][:], bank[4 * d + 3][:, :], ALU.add).then_inc(v3.step("s1", g, d), 1)
    if stop <= 3:
        return dict(locals())

    stage3_keep = stage2_keep + 64 + T * H * 4 + 32
    cursor[0] = base0
    qc = sb("qc", [P, H, T])
    kc = sb("kc", [P, H, T])
    og = sb("og", [P, H, T])
    cursor[0] = stage1_keep
    kc_tm = sb("kc_tm", [P, NT, H * HD])
    vc_tm = sb("vc_tm", [P, NT, H * HD])
    cursor[0] = stage3_keep
    sqa = sb("sqa", [P, H, T])
    rsa = sb("rsa", [P, H, T])
    tz = sb("tz", [P, H, T])
    UN = [("q", j) for j in range(4)] + [("k", j) for j in range(4)] + [("v", t) for t in range(NT)] + [("o", j) for j in range(4)]
    lp4, la4, lv4 = [], [], []
    for n, u in enumerate(UN):
        lp4 += [u] + ([("sum", u[1])] if u[0] == "k" else []) + ([("kt", u[1])] if u[0] == "v" else [])
        la4 += [u + (0,)] + ([u + (1,)] if u[0] == "o" else []) + ([("rms", u[1], 0), ("rms", u[1], 1)] if u[0] == "k" else [])
        la4 += [("tz",)] if n == 0 else []
        lv4 += [u] if u[0] in "qk" else [("kt", u[1])] if u[0] == "v" else []
        lv4 += [("fin", i) for i in range(4)] if n == 8 else []
    p4, a4, v4 = Steps(nc, "proj2_tensor", lp4), Steps(nc, "proj2_scalar", la4), Steps(nc, "proj2_vector", lv4)
    g4_ = Steps(nc, "proj2_gpsimd", [("o",), ("sq",)])
    with nc.Block("proj2", no_gpsimd_drain=True) as block:
        @block.sync
        def _(sp):
            for n, last in ((18, ("q", 3)), (19, ("k", 3)), (20, ("v", 4)), (21, ("o", 3))):
                load_block(sp, n + RING, p4.sem, p4.after(*last))

        @block.tensor
        def _(pe):
            for n, (kind, j) in enumerate(UN):
                blk = 18 + "qkvo".index(kind)
                if j == 0:
                    block_ready(pe, blk)
                if n >= 2:
                    prev = UN[n - 2]
                    pe.wait_ge(a4.sem, a4.after(*prev, 1 if prev[0] == "o" else 0))
                    if prev[0] in "qk":
                        pe.wait_ge(v4.sem, v4.after(*prev))
                lat, ctx = bank[2 * (n % 2)], bank[2 * (n % 2) + 1]
                for k in range(KD):
                    if kind == "v":
                        mm = pe.matmul(lat[:, :], hT[:, k, tok(j)], ring[:, blk % RING, 512 * k:512 * k + 512],
                                       start=(k == 0), stop=(k == KD - 1))
                    else:
                        w = ring[:, blk % RING, 512 * k + P * j:512 * k + P * j + P]
                        pe.matmul(lat[:, :], w, hT[:, k, P:T], start=(k == 0), stop=(k == KD - 1))
                        mm = pe.matmul(ctx[:, 0:P], w, hT[:, k, 0:P], start=(k == 0), stop=(k == KD - 1))
                mm.then_inc(p4.step(kind, j), 1)
                if kind == "k":
                    pe.wait_ge(g4_.sem, g4_.after("sq"))
                    if j:
                        pe.wait_ge(a4.sem, a4.after("rms", j - 1, 1))
                    pe.matmul(bank[4][:, :], ones, sqa[:, j, P:T], start=True, stop=True)
                    pe.matmul(bank[5][:, 0:P], ones, sqa[:, j, 0:P], start=True, stop=True).then_inc(p4.step("sum", j), 1)
                if kind == "v":
                    if j == 0:
                        for i in range(4):
                            pe.wait_ge(a4.sem, a4.after("k", i, 0))
                            pe.wait_ge(v4.sem, v4.after("k", i))
                    if j >= 2:
                        pe.wait_ge(v4.sem, v4.after("kt", j - 2))
                    for h in range(H):
                        mm = pe.transpose(bank[6 + j % 2][:, P * h:P * h + P], kc[:, h, tok(j)], ident)
                    mm.then_inc(p4.step("kt", j), 1)

        @block.scalar
        def _(act):
            for n, (kind, j) in enumerate(UN):
                act.wait_ge(p4.sem, p4.after(kind, j))
                lat, ctx = bank[2 * (n % 2)], bank[2 * (n % 2) + 1]
                if kind == "v":
                    act.activation(vc_tm[:, j, :], lat[:, :], ACT.Copy).then_inc(a4.step("v", j, 0), 1)
                elif kind == "o":
                    act.activation(og[:, j, P:T], lat[:, :], ACT.Tanh, scale=0.5).then_inc(a4.step("o", j, 0), 1)
                    act.activation(og[:, j, 0:P], ctx[:, 0:P], ACT.Tanh, scale=0.5).then_inc(a4.step("o", j, 1), 1)
                else:
                    act.activation((qc if kind == "q" else kc)[:, j, P:T], lat[:, :], ACT.Copy,
                                   scale=1.0 if kind == "q" else HD ** -0.5).then_inc(a4.step(kind, j, 0), 1)
                if kind == "k":
                    act.wait_ge(p4.sem, p4.after("sum", j))
                    act.activation(rsa[:, j, P:T], bank[4][:, :], ACT.Sqrt, scale=1.0 / HD, bias=col(E_RMS)).then_inc(a4.step("rms", j, 0), 1)
                    act.activation(rsa[:, j, 0:P], bank[5][:, 0:P], ACT.Sqrt, scale=1.0 / HD, bias=col(E_RMS)).then_inc(a4.step("rms", j, 1), 1)
                if n == 0:
                    act.activation(tz[:], yA[:], ACT.Tanh, scale=0.5).then_inc(a4.step("tz"), 1)

        @block.gpsimd
        def _(pool):
            pool.tensor_tensor(o_b[:], o_b[:], o_f[:], ALU.add).then_inc(g4_.step("o"), 1)
            pool.wait_ge(g4_.sem, g4_.after("o"))
            pool.tensor_tensor(sqa[:], o_b[:], o_b[:], ALU.mult).then_inc(g4_.step("sq"), 1)

        @block.vector
        def _(dve):
            for n, (kind, j) in enumerate(UN):
                ctx = bank[2 * (n % 2) + 1]
                if kind in "qk":
                    dve.wait_ge(p4.sem, p4.after(kind, j))
                    dve.tensor_scalar((qc if kind == "q" else kc)[:, j, 0:P], ctx[:, 0:P],
                                      1.0 if kind == "q" else HD ** -0.5, None, ALU.mult).then_inc(v4.step(kind, j), 1)
                elif kind == "v":
                    dve.wait_ge(p4.sem, p4.after("kt", j))
                    dve.tensor_copy(kc_tm[:, j, :], bank[6 + j % 2][:, :]).then_inc(v4.step("kt", j), 1)
                if n == 8:
                    dve.wait_ge(a4.sem, a4.after("rms", 3, 1))
                    dve.reciprocal(rsa[:], rsa[:]).then_inc(v4.step("fin", 0), 1)
                    dve.wait_ge(v4.sem, v4.after("fin", 0))
                    dve.scalar_tensor_tensor(o_b[:], o_b[:], vec[:, V_DN:V_DN + 1], rsa[:], ALU.mult,
                                             ALU.mult).then_inc(v4.step("fin", 1), 1)
                    dve.scalar_tensor_tensor(tz[:], tz[:], 1.0, yA[:], ALU.add, ALU.mult).then_inc(v4.step("fin", 2), 1)
                    dve.wait_ge(v4.sem, v4.after("fin", 2))
                    dve.scalar_tensor_tensor(yA[:], tz[:], 0.5, o_b[:], ALU.mult, ALU.mult).then_inc(v4.step("fin", 3), 1)
    if stop <= 4:
        return dict(locals())

    cursor[0] = stage2_keep
    h_f = sb("h_f", [P, NT, H * HD])
    h_b = sb("h_b", [P, NT, H * HD])
    hh = [h_f, h_b]
    r1_, r2_, am_, pt_, kw_, t1_, c_ = (two(x) for x in ("ml_r1", "ml_r2", "ml_am", "ml_pt", "ml_kw", "ml_t1", "ml_c"))
    fc = two("ml_fc", 8)
    sm = two("ml_sm", 48)
    nst, mst = two("ml_n", 4), two("ml_m", 4)
    X_A, X_AMAX, X_MLOC, X_M, X_MEND, X_E, X_DEN, X_NDEN = 0, 4, 8, 12, 16, 20, 36, 40
    E_WINT, E_EMT, E_WTOK, E_SINT = 20, 24, 28, 32
    nlf = sb("nlf", [P, NT, 8])
    got_c = nc.alloc_semaphore("got_mlstm_state")
    lv5 = both("r2", "fc", "a", "amax", "am", "mloc", "M", "Mend", "e1", "e2", "e3", "e4", "mnew", "sub", "pm", "dsum",
               "c0", "n0", "n1", "c1", "t1", "t2", "den", "nden", "den2", "den3", "rden", "h")
    la5, lp5 = both("e", "pm", "pt"), both("gcol", "arow", "qk", "pt", "qc", "pv", "cu")
    lg5 = both("r1", "kw")
    v5 = Steps(nc, "mlstm_vector", [("z", 0), ("z", 1), ("z", 2), ("z", 3), ("z", 4), ("z", 5), ("nlf", 0)] + lv5[:2 * 28]
               + [("init", 0), ("init", 1), ("init", 2), ("init", 3)] + lv5[2 * 28:])
    a5, p5, g5 = Steps(nc, "mlstm_scalar", la5), Steps(nc, "mlstm_tensor", lp5), Steps(nc, "mlstm_gpsimd", lg5)
    with nc.Block("mlstm", no_gpsimd_drain=True) as block:
        @block.sync
        def _(sp):
            for d in range(2):
                sp.wait_ge(v5.sem, v5.after("c1", 0, d))
                store(sp, O["mc"][d], c_[d][:])
                store(sp, O["mn"][d], nst[d][:])
                store(sp, O["mm"][4 * d:4 * d + 4].rearrange("(a b) -> a b", a=1), mst[d][0:1, :])
            sp.wait_ge(stored, stores[0])
            for d in range(2):
                sp.dma_start(c_[d][:], A["s_mc"][d]).then_inc(got_c, 16)
            sp.wait_ge(got_c, 32)

        @block.tensor
        def _(pe):
            def hd(t, h):
                return t[:, P * h:P * h + P]

            for g in range(NT):
                for d in range(2):
                    t = tile_of(g, d)
                    lf4 = smg[:, t, 24 + 4 * d:28 + 4 * d]
                    if g:
                        pe.wait_ge(v5.sem, v5.after("den", g - 1, d))
                        pe.wait_ge(a5.sem, a5.after("pt", g - 1, d))
                    pe.matmul(bank[4 * d][:, 0:4], tri[d], lf4, start=True, stop=True)
                    pe.matmul(bank[4 * d][:, 4:8], ones, lf4, start=True, stop=True).then_inc(p5.step("gcol", g, d), 1)
                for d in range(2):
                    pe.wait_ge(v5.sem, v5.after("r2", g, d))
                    pe.wait_ge(g5.sem, g5.after("r1", g, d))
                    if g:
                        pe.wait_ge(v5.sem, v5.after("c1", g - 1, d))
                    pe.matmul(bank[4 * d + 1][:, :], ones, r1_[d][:], start=True, stop=False)
                    pe.matmul(bank[4 * d + 1][:, :], ones, r2_[d][:], start=False, stop=True).then_inc(p5.step("arow", g, d), 1)
                for d in range(2):
                    ts = tok(tile_of(g, d))
                    if g:
                        pe.wait_ge(v5.sem, v5.after("t2", g - 1, d))
                    for h in range(H):
                        mm = pe.matmul(hd(bank[4 * d + 2], h), qc[:, h, ts], kc[:, h, ts], start=True, stop=True)
                    mm.then_inc(p5.step("qk", g, d), 1)
                for d in range(2):
                    pe.wait_ge(v5.sem, v5.after("pm", g, d))
                    if g:
                        pe.wait_ge(v5.sem, v5.after("t2", g - 1, d))
                    for h in range(H):
                        mm = pe.transpose(hd(bank[4 * d + 3], h), hd(am_[d], h), ident)
                    mm.then_inc(p5.step("pt", g, d), 1)
                for d in range(2):
                    ts = tok(tile_of(g, d))
                    if g == 0:
                        pe.wait_ge(v5.sem, v5.after("z", 5))
                    elif g == 1:
                        pe.wait_ge(got_c, 32)
                        pe.wait_ge(v5.sem, v5.after("init", 3))
                    pe.wait_ge(v5.sem, v5.after("fc", g, d))
                    for h in range(H):
                        pe.matmul(hd(bank[4 * d + 2], h), qc[:, h, ts], hd(c_[d], h), start=True, stop=True)
                    for h in range(H):
                        mm = pe.matmul(bank[4 * d][:, 16 + h:17 + h], qc[:, h, ts], nst[d][:, h:h + 1], start=True, stop=True)
                    mm.then_inc(p5.step("qc", g, d), 1)
                for d in range(2):
                    t = tile_of(g, d)
                    pe.wait_ge(a5.sem, a5.after("pt", g, d))
                    for h in range(H):
                        mm = pe.matmul(hd(bank[4 * d + 3], h), hd(pt_[d], h), vc_tm[:, t, P * h:P * h + P], start=True, stop=True)
                    mm.then_inc(p5.step("pv", g, d), 1)
                for d in range(2):
                    t = tile_of(g, d)
                    pe.wait_ge(g5.sem, g5.after("kw", g, d))
                    pe.wait_ge(v5.sem, v5.after("am", g, d))
                    for h in range(H):
                        pe.matmul(hd(bank[4 * d + 1], h), hd(kw_[d], h), vc_tm[:, t, P * h:P * h + P], start=True, stop=True)
                    for h in range(H):
                        mm = pe.matmul(bank[4 * d][:, 24 + h:25 + h], hd(kw_[d], h), ones[:, 0:1], start=True, stop=True)
                    mm.then_inc(p5.step("cu", g, d), 1)

        @block.gpsimd
        def _(pool):
            for g in range(NT):
                for d in range(2):
                    i4 = smg[:, tile_of(g, d), 16 + 4 * d:20 + 4 * d]
                    if g:
                        pool.wait_ge(p5.sem, p5.after("arow", g - 1, d))
                    pool.tensor_tensor(heads(r1_[d][:]), bc(ident.unsqueeze(1), P, H, P), bc(i4.unsqueeze(2), P, H, P),
                                       ALU.mult).then_inc(g5.step("r1", g, d), 1)
                for d in range(2):
                    pool.wait_ge(a5.sem, a5.after("e", g, d))
                    if g:
                        pool.wait_ge(p5.sem, p5.after("cu", g - 1, d))
                    pool.tensor_tensor(heads(kw_[d][:]), heads(kc_tm[:, tile_of(g, d), :]),
                                       bc(sm[d][:, E_WTOK:E_WTOK + 4].unsqueeze(2), P, H, HD), ALU.mult).then_inc(g5.step("kw", g, d), 1)

        @block.scalar
        def _(act):
            for g in range(NT):
                for d in range(2):
                    act.wait_ge(v5.sem, v5.after("e4", g, d))
                    act.activation(sm[d][:, X_E:X_E + 16], sm[d][:, X_E:X_E + 16], ACT.Exp).then_inc(a5.step("e", g, d), 1)
                for d in range(2):
                    act.wait_ge(v5.sem, v5.after("sub", g, d))
                    act.activation(am_[d][:], am_[d][:], ACT.Exp).then_inc(a5.step("pm", g, d), 1)
                for d in range(2):
                    act.wait_ge(p5.sem, p5.after("pt", g, d))
                    if g:
                        act.wait_ge(p5.sem, p5.after("pv", g - 1, d))
                    act.activation(pt_[d][:], bank[4 * d + 3][:, :], ACT.Copy).then_inc(a5.step("pt", g, d), 1)

        @block.vector
        def _(dve):
            for d in range(2):
                dve.memset(c_[d][:], 0.0).then_inc(v5.step("z", 3 * d), 1)
                dve.memset(nst[d][:], 0.0).then_inc(v5.step("z", 3 * d + 1), 1)
                dve.memset(mst[d][:], 0.0).then_inc(v5.step("z", 3 * d + 2), 1)
            dve.tensor_scalar(nlf[:], smg[:, :, 24:32], -1.0, None, ALU.mult).then_inc(v5.step("nlf", 0), 1)
            dve.wait_ge(v5.sem, v5.after("nlf", 0))
            for g in range(NT):
                for d in range(2):
                    if g:
                        dve.wait_ge(p5.sem, p5.after("arow", g - 1, d))
                    dve.tensor_tensor(heads(r2_[d][:]), bc(tri[d].unsqueeze(1), P, H, P),
                                      bc(nlf[:, tile_of(g, d), 4 * d:4 * d + 4].unsqueeze(2), P, H, P),
                                      ALU.mult).then_inc(v5.step("r2", g, d), 1)
                for d in range(2):
                    dve.wait_ge(p5.sem, p5.after("gcol", g, d))
                    dve.tensor_copy(fc[d][:], bank[4 * d][:, 0:8]).then_inc(v5.step("fc", g, d), 1)
                for d in range(2):
                    dve.wait_ge(v5.sem, v5.after("fc", g, d))
                    dve.tensor_tensor(sm[d][:, X_A:X_A + 4], smg[:, tile_of(g, d), 16 + 4 * d:20 + 4 * d], fc[d][:, 0:4],
                                      ALU.subtract).then_inc(v5.step("a", g, d), 1)
                for d in range(2):
                    dve.wait_ge(p5.sem, p5.after("arow", g, d))
                    dve.tensor_reduce(sm[d][:, X_AMAX:X_AMAX + 4], heads(bank[4 * d + 1][:, :]), AX, ALU.max).then_inc(v5.step("amax", g, d), 1)
                for d in range(2):
                    if g:
                        dve.wait_ge(p5.sem, p5.after("pt", g - 1, d))
                    dve.tensor_tensor(heads(am_[d][:]), heads(bank[4 * d + 1][:, :]), bc(neg[d].unsqueeze(1), P, H, P),
                                      ALU.add).then_inc(v5.step("am", g, d), 1)
                for d in range(2):
                    dve.wait_ge(v5.sem, v5.after("am", g, d))
                    dve.tensor_reduce(sm[d][:, X_MLOC:X_MLOC + 4], heads(am_[d][:]), AX, ALU.max).then_inc(v5.step("mloc", g, d), 1)
                s4 = lambda d, x: sm[d][:, x:x + 4]
                for d in range(2):
                    dve.wait_ge(v5.sem, v5.after("mloc", g, d))
                    dve.tensor_tensor(s4(d, X_M), s4(d, X_MLOC), mst[d][:], ALU.max).then_inc(v5.step("M", g, d), 1)
                for d in range(2):
                    dve.tensor_tensor(s4(d, X_MEND), s4(d, X_AMAX), mst[d][:], ALU.max).then_inc(v5.step("Mend", g, d), 1)
                for d in range(2):
                    dve.wait_ge(v5.sem, v5.after("Mend", g, d))
                    dve.tensor_tensor(s4(d, E_WINT), mst[d][:], s4(d, X_M), ALU.subtract).then_inc(v5.step("e1", g, d), 1)
                for d in range(2):
                    dve.scalar_tensor_tensor(s4(d, E_EMT), fc[d][:, 0:4], -1.0, s4(d, X_M), ALU.mult,
                                             ALU.subtract).then_inc(v5.step("e2", g, d), 1)
                for d in range(2):
                    dve.tensor_tensor(s4(d, E_WTOK), s4(d, X_A), s4(d, X_MEND), ALU.subtract).then_inc(v5.step("e3", g, d), 1)
                for d in range(2):
                    dve.tensor_tensor(s4(d, E_SINT), mst[d][:], s4(d, X_MEND), ALU.subtract).then_inc(v5.step("e4", g, d), 1)
                for d in range(2):
                    dve.wait_ge(v5.sem, v5.after("e4", g, d))
                    dve.tensor_tensor(mst[d][:], fc[d][:, 4:8], s4(d, X_MEND), ALU.add).then_inc(v5.step("mnew", g, d), 1)
                for d in range(2):
                    dve.tensor_tensor(heads(am_[d][:]), heads(am_[d][:]), bc(s4(d, X_M).unsqueeze(2), P, H, P),
                                      ALU.subtract).then_inc(v5.step("sub", g, d), 1)
                for d in range(2):
                    dve.wait_ge(a5.sem, a5.after("pm", g, d))
                    dve.wait_ge(p5.sem, p5.after("qk", g, d))
                    dve.tensor_tensor(am_[d][:], am_[d][:], bank[4 * d + 2][:, :], ALU.mult).then_inc(v5.step("pm", g, d), 1)
                for d in range(2):
                    dve.wait_ge(v5.sem, v5.after("pm", g, d))
                    dve.tensor_reduce(s4(d, X_DEN), heads(am_[d][:]), AX, ALU.add).then_inc(v5.step("dsum", g, d), 1)
                for d in range(2):
                    dve.wait_ge(p5.sem, p5.after("qc", g, d))
                    dve.wait_ge(a5.sem, a5.after("e", g, d))
                    dve.tensor_tensor(heads(c_[d][:]), heads(c_[d][:]), bc(s4(d, E_SINT).unsqueeze(2), P, H, HD),
                                      ALU.mult).then_inc(v5.step("c0", g, d), 1)
                for d in range(2):
                    dve.tensor_tensor(nst[d][:], nst[d][:], s4(d, E_SINT), ALU.mult).then_inc(v5.step("n0", g, d), 1)
                for d in range(2):
                    dve.wait_ge(p5.sem, p5.after("cu", g, d))
                    dve.wait_ge(v5.sem, v5.after("n0", g, d))
                    dve.tensor_tensor(nst[d][:], nst[d][:], bank[4 * d][:, 24:28], ALU.add).then_inc(v5.step("n1", g, d), 1)
                for d in range(2):
                    dve.tensor_tensor(c_[d][:], c_[d][:], bank[4 * d + 1][:, :], ALU.add).then_inc(v5.step("c1", g, d), 1)
                for d in range(2):
                    dve.tensor_tensor(heads(t1_[d][:]), heads(bank[4 * d + 2][:, :]), bc(s4(d, E_WINT).unsqueeze(2), P, H, HD),
                                      ALU.mult).then_inc(v5.step("t1", g, d), 1)
                for d in range(2):
                    dve.wait_ge(p5.sem, p5.after("pv", g, d))
                    dve.wait_ge(v5.sem, v5.after("t1", g, d))
                    dve.tensor_tensor(t1_[d][:], t1_[d][:], bank[4 * d + 3][:, :], ALU.add).then_inc(v5.step("t2", g, d), 1)
                for d in range(2):
                    dve.tensor_tensor(s4(d, X_NDEN), bank[4 * d][:, 16:20], s4(d, E_WINT), ALU.mult).then_inc(v5.step("den", g, d), 1)
                for d in range(2):
                    dve.wait_ge(v5.sem, v5.after("den", g, d))
                    dve.tensor_tensor(s4(d, X_DEN), s4(d, X_DEN), s4(d, X_NDEN), ALU.add).then_inc(v5.step("nden", g, d), 1)
                for d in range(2):
                    dve.wait_ge(v5.sem, v5.after("nden", g, d))
                    dve.scalar_tensor_tensor(s4(d, X_DEN), s4(d, X_DEN), -1.0, s4(d, X_DEN), ALU.mult, ALU.max).then_inc(v5.step("den2", g, d), 1)
                for d in range(2):
                    dve.wait_ge(v5.sem, v5.after("den2", g, d))
                    dve.tensor_tensor(s4(d, X_DEN), s4(d, X_DEN), s4(d, E_EMT), ALU.max).then_inc(v5.step("den3", g, d), 1)
                for d in range(2):
                    dve.wait_ge(v5.sem, v5.after("den3", g, d))
                    dve.reciprocal(s4(d, X_DEN), s4(d, X_DEN)).then_inc(v5.step("rden", g, d), 1)
                for d in range(2):
                    dve.wait_ge(v5.sem, v5.after("rden", g, d))
                    dve.wait_ge(v5.sem, v5.after("t2", g, d))
                    dve.tensor_tensor(heads(hh[d][:, tile_of(g, d), :]), heads(t1_[d][:]), bc(s4(d, X_DEN).unsqueeze(2), P, H, HD),
                                      ALU.mult).then_inc(v5.step("h", g, d), 1)
                if g == 0:
                    dve.wait_ge(got_c, 32)
                    for d in range(2):
                        dve.tensor_copy(nst[d][:], vec[:, V_SN + 4 * d:V_SN + 4 * d + 4]).then_inc(v5.step("init", 2 * d), 1)
                        dve.tensor_copy(mst[d][:], row[:, R_M + 4 * d:R_M + 4 * d + 4]).then_inc(v5.step("init", 2 * d + 1), 1)
    if stop <= 5:
        return dict(locals())

    sqc = sb("sqc", [P, NT, H * HD])
    mu = sb("mu", [P, NT * H])
    va = sb("va", [P, NT * H])
    v6 = Steps(nc, "mlstm_norm_vector", [("add",), ("mean",), ("mean1",), ("sub",), ("var",), ("rec",), ("og",), ("norm",)]
               + [("y", t) for t in range(NT)])
    p6 = Steps(nc, "mlstm_norm_tensor", [("t", t) for t in range(NT)])
    a6, g6 = Steps(nc, "mlstm_norm_scalar", [("sqrt",)]), Steps(nc, "mlstm_norm_gpsimd", [("sq",)])
    per_head = lambda t: t[:].rearrange("p t (h v) -> p (t h) v", h=H)
    with nc.Block("mlstm_norm", no_gpsimd_drain=True) as block:
        @block.vector
        def _(dve):
            x = per_head(h_f)
            dve.tensor_tensor(h_f[:], h_f[:], h_b[:], ALU.add).then_inc(v6.step("add"), 1)
            dve.wait_ge(v6.sem, v6.after("add"))
            dve.tensor_reduce(mu[:], x, AX, ALU.add).then_inc(v6.step("mean"), 1)
            dve.wait_ge(v6.sem, v6.after("mean"))
            dve.tensor_scalar(mu[:], mu[:], 1.0 / HD, None, ALU.mult).then_inc(v6.step("mean1"), 1)
            dve.wait_ge(v6.sem, v6.after("mean1"))
            dve.tensor_tensor(x, x, bc(mu[:].unsqueeze(2), P, NT * H, HD), ALU.subtract).then_inc(v6.step("sub"), 1)
            dve.wait_ge(g6.sem, g6.after("sq"))
            dve.tensor_reduce(va[:], per_head(sqc), AX, ALU.add).then_inc(v6.step("var"), 1)
            dve.wait_ge(a6.sem, a6.after("sqrt"))
            dve.reciprocal(va[:], va[:]).then_inc(v6.step("rec"), 1)
            dve.tensor_scalar(og[:], og[:], 1.0, 0.5, ALU.add, ALU.mult).then_inc(v6.step("og"), 1)
            dve.wait_ge(v6.sem, v6.after("rec"))
            dve.tensor_tensor(x, x, bc(va[:].unsqueeze(2), P, NT * H, HD), ALU.mult).then_inc(v6.step("norm"), 1)
            dve.wait_ge(v6.sem, v6.after("og"))
            for t in range(NT):
                dve.wait_ge(p6.sem, p6.after("t", t))
                for h in range(H):
                    ins = dve.scalar_tensor_tensor(yC[:, h, tok(t)], bank[t][:, P * h:P * h + P], vec[:, V_MN + h:V_MN + h + 1],
                                                   og[:, h, tok(t)], ALU.mult, ALU.mult)
                ins.then_inc(v6.step("y", t), 1)

        @block.gpsimd
        def _(pool):
            pool.wait_ge(v6.sem, v6.after("sub"))
            pool.tensor_tensor(sqc[:], h_f[:], h_f[:], ALU.mult).then_inc(g6.step("sq"), 1)

        @block.scalar
        def _(act):
            act.wait_ge(v6.sem, v6.after("var"))
            act.activation(va[:], va[:], ACT.Sqrt, scale=1.0 / HD, bias=col(E_LN)).then_inc(a6.step("sqrt"), 1)

        @block.tensor
        def _(pe):
            pe.wait_ge(v6.sem, v6.after("norm"))
            for t in range(NT):
                for h in range(H):
                    mm = pe.transpose(bank[t][:, P * h:P * h + P], h_f[:, t, P * h:P * h + P], ident)
                mm.then_inc(p6.step("t", t), 1)
    if stop <= 6:
        return dict(locals())

    MW = 3 * (KD + 4) * P
    cursor[0] = base0 - RING * 4096 * 4
    mT = sb("mT", [P, KD, T])
    rows_off = cursor[0]
    rows = sb("rows", [P, 4, 2, D])
    w_out = sb("w_out", [P, KD, D])
    stage7_keep = cursor[0]
    mring = sb("mring", [P, 2, MW])
    sg = sb("sg", [P, 2, T])
    pr = sb("pr", [P, 2, T])
    acc = sb("acc", [P, T])
    dg = sb("dg", [P, 2, 4 * P])
    ROWS = [(r, c, f) for r in range(4) for c in range(2) for f in range(2)]
    a7r, p7r = Steps(nc, "rows_scalar", [("r", i) for i in range(16)]), Steps(nc, "rows_tensor", [("r", i) for i in range(16)])
    g7r = Steps(nc, "rows_gpsimd", [("r", i) for i in range(16)])
    U = range(6)
    p7 = LoopSteps(nc, "merge_tensor", [(x, u) for u in U for x in ("gate", "proj")])
    a7 = LoopSteps(nc, "merge_scalar", [("sg", u) for u in U])
    v7 = LoopSteps(nc, "merge_vector", [(x, u) for u in U for x in (("pr",) if u % 3 == 0 else ("pr", "add"))])
    got_m = [nc.alloc_semaphore(f"got_merge{i}") for i in range(2)]
    got_wo = nc.alloc_semaphore("got_w_out")
    branch = [yA, yB, yC]
    with nc.Block("merge", no_gpsimd_drain=True) as block:
        @block.sync
        def _(sp):
            for x in range(2):
                sp.dma_start(mring[:, x, :], A["merge"][x]).then_inc(got_m[x], 16)
            sp.dma_start(w_out[:], A["w_out"]).then_inc(got_wo, 16)
            with sp.Fori(1, KD // 2) as i:
                for x in range(2):
                    sp.wait_ge(p7.sem, p7.after("proj", 3 * x + 2, turn=i - 1))
                    sp.dma_start(mring[:, x, :], A["merge"][bass.ds(2 * i + x, 1)].rearrange("a p n -> (a p) n")).then_inc(got_m[x], 16)

        @block.gpsimd
        def _(pool):
            for i, (r, c, f) in enumerate(ROWS):
                if i >= 2:
                    pool.wait_ge(p7r.sem, p7r.after("r", i - 2))
                m = 16 + 8 * ((r - 1) % 4) + 4 * f
                pool.tensor_tensor(heads(dg[:, i % 2, :]), bc(ident.unsqueeze(1), P, 4, P),
                                   bc(modc[:, m:m + 4, c].unsqueeze(2), P, 4, P), ALU.mult).then_inc(g7r.step("r", i), 1)

        @block.scalar
        def _(act):
            a7.credit(act)
            for i, (r, c, f) in enumerate(ROWS):
                act.wait_ge(p7r.sem, p7r.after("r", i))
                act.activation(rows[:, r, c, 512 * f:512 * f + 512], bank[i % 2][:, :], ACT.Copy,
                               scale=0.5 if r == 1 else 1.0).then_inc(a7r.step("r", i), 1)
            with act.Fori(0, KD // 2) as i:
                a7.turn()
                for u in U:
                    s_ = u % 2
                    act.wait_ge(p7.sem, p7.after("gate", u, turn=i))
                    act.wait_ge(v7.sem, v7.after("pr", (u - 2) % 6, turn=i if u >= 2 else i - 1))
                    act.activation(sg[:, s_, P:T], bank[4 * s_][:, :], ACT.Tanh, scale=0.5)
                    act.activation(sg[:, s_, 0:P], bank[4 * s_ + 1][:, 0:P], ACT.Tanh, scale=0.5).then_inc(a7.step("sg", u), 1)

        @block.tensor
        def _(pe):
            p7.credit(pe)
            for i in range(16):
                pe.wait_ge(g7r.sem, g7r.after("r", i))
                if i >= 2:
                    pe.wait_ge(a7r.sem, a7r.after("r", i - 2))
                pe.matmul(bank[i % 2][:, :], ones, dg[:, i % 2, :], start=True, stop=True).then_inc(p7r.step("r", i), 1)
            pe.wait_ge(a7r.sem, a7r.after("r", 15))
            with pe.Fori(0, KD // 2) as i:
                p7.turn()
                for u in U:
                    s_, x, br = u % 2, u // 3, u % 3
                    last = i if u >= 2 else i - 1
                    if br == 0:
                        pe.wait_ge(got_m[x], 16 * (i + 1))
                    w = mring[:, x, (KD + 4) * P * br:(KD + 4) * P * (br + 1)].rearrange("p (k m) -> p k m", m=P)
                    pe.wait_ge(a7.sem, a7.after("sg", (u - 2) % 6, turn=last))
                    for k in range(KD):
                        pe.matmul(bank[4 * s_][:, :], w[:, k, :], hT[:, k, P:T], start=(k == 0), stop=(k == KD - 1))
                        mm = pe.matmul(bank[4 * s_ + 1][:, 0:P], w[:, k, :], hT[:, k, 0:P], start=(k == 0), stop=(k == KD - 1))
                    mm.then_inc(p7.step("gate", u), 1)
                    pe.wait_ge(v7.sem, v7.after("pr", (u - 2) % 6, turn=last))
                    y = branch[br]
                    for k in range(4):
                        pe.matmul(bank[4 * s_ + 2][:, :], w[:, KD + k, :], y[:, k, P:T], start=(k == 0), stop=(k == 3))
                        mm = pe.matmul(bank[4 * s_ + 3][:, 0:P], w[:, KD + k, :], y[:, k, 0:P], start=(k == 0), stop=(k == 3))
                    mm.then_inc(p7.step("proj", u), 1)

        @block.vector
        def _(dve):
            v7.credit(dve)
            with dve.Fori(0, KD // 2) as i:
                v7.turn()
                for u in U:
                    s_, x, br = u % 2, u // 3, u % 3
                    dve.wait_ge(a7.sem, a7.after("sg", u, turn=i))
                    dve.wait_ge(p7.sem, p7.after("proj", u, turn=i))
                    if br == 0:
                        dve.wait_ge(v7.sem, v7.after("add", (u - 1) % 6, turn=i if u else i - 1))
                    dst = acc[:, :] if br == 0 else pr[:, s_, :]
                    dve.scalar_tensor_tensor(dst[:, P:T], sg[:, s_, P:T], 1.0, bank[4 * s_ + 2][:, :], ALU.add, ALU.mult)
                    dve.scalar_tensor_tensor(dst[:, 0:P], sg[:, s_, 0:P], 1.0, bank[4 * s_ + 3][:, 0:P], ALU.add,
                                             ALU.mult).then_inc(v7.step("pr", u), 1)
                    if br:
                        dve.wait_ge(v7.sem, v7.after("pr", u, turn=i))
                        out = acc[:] if br == 1 else mT[:, bass.ds(2 * i + x, 1), :].rearrange("p a t -> p (a t)")
                        dve.tensor_tensor(out, acc[:], pr[:, s_, :], ALU.add).then_inc(v7.step("add", u), 1)
    if stop <= 7:
        return dict(locals())

    x1 = nc.alloc_sbuf_tensor_at("x1", [P, NT, D], F32, offset=yA_off)
    cursor[0] = stage7_keep
    pos2 = sb("pos2", [P, NT - 1, D])
    lnr = sb("lnr", [P, 2, D])
    h2 = sb("h2", [P, 2, D])
    st8 = sb("st8", [P, 2, 2, 6])
    mv8 = sb("mv8", [P, 2, NT, 2])
    rs8 = sb("rs8", [P, 2, NT])
    w_r = sb("w_r", [P, KD, NG + NE])
    h2d = nc.dram_tensor("h2_rows", (T, D), F32, kind="Internal").ap()
    yd = nc.dram_tensor("expert_rows", (2 * T, D), F32, kind="Internal").ap()
    got8 = nc.alloc_semaphore("got_ln_rows")
    got_x2 = nc.alloc_semaphore("got_x_again")
    sent8 = [nc.alloc_semaphore(f"h2_sent{i}") for i in range(2)]
    lv8 = [(k, t) for t in range(NT) for k in ("g0", "g1", "res", "s0", "s1", "mv", "rec", "xn", "t0", "t1", "mv2", "rec2", "xn2")]
    v8 = Steps(nc, "out_vector", lv8)
    a8 = Steps(nc, "out_scalar", [(k, t) for t in range(NT) for k in ("sqrt", "sqrt2", "h0", "h1")])
    g8 = Steps(nc, "out_gpsimd", [("pos", t) for t in range(1, NT)] + [(k, t) for t in range(NT) for k in ("lg", "lb", "sc", "sh")])
    p8 = Steps(nc, "out_tensor", [("mix", 0)] + [x for t in range(NT) for x in ([("mix", t + 1)] if t < NT - 1 else []) + [("tr", t), ("lg", t)]])
    with nc.Block("out", no_gpsimd_drain=True) as block:
        @block.sync
        def _(sp):
            sp.dma_start(x1[:, 0, :], A["xp"]).then_inc(got_x2, 16)
            sp.dma_start(x1[:, 1:NT, :], A["xs"].rearrange("(t p) d -> p t d", p=P)).then_inc(got_x2, 16)
            sp.dma_start(pos2[:], A["pos"].rearrange("(t p) d -> p t d", p=P)).then_inc(got_x2, 16)
            sp.dma_start(lnr[:], A["ln"][0:2 * D].partition_broadcast(P).rearrange("p (a d) -> p a d", a=2)).then_inc(got8, 16)
            sp.dma_start(w_r[:], A["w_r"]).then_inc(got8, 16)
            for t in range(NT):
                sp.wait_ge(g8.sem, g8.after("sh", t))
                sp.dma_start(h2d[t * P:t * P + P, :], h2[:, t % 2, :]).then_inc(sent8[t % 2], 16)
            sp.wait_ge(sent8[0], 48)
            sp.wait_ge(sent8[1], 32)

        @block.tensor
        def _(pe):
            def mix(t):
                for f in range(2):
                    if t >= 2:
                        pe.wait_ge(v8.sem, v8.after(f"g{f}", t - 2))
                    for k in range(KD):
                        mm = pe.matmul(bank[2 * (t % 2) + f][:, :], mT[:, k, tok(t)], w_out[:, k, 512 * f:512 * f + 512],
                                       start=(k == 0), stop=(k == KD - 1))
                mm.then_inc(p8.step("mix", t), 1)

            pe.wait_ge(got_wo, 16)
            mix(0)
            for t in range(NT):
                if t < NT - 1:
                    mix(t + 1)
                pe.wait_ge(g8.sem, g8.after("sh", t))
                if t:
                    pe.wait_ge(a8.sem, a8.after("h1", t - 1))
                for k in range(KD):
                    mm = pe.transpose(bank[4 + k // 4][:, P * (k % 4):P * (k % 4) + P], h2[:, t % 2, P * k:P * k + P], ident)
                mm.then_inc(p8.step("tr", t), 1)
                pe.wait_ge(a8.sem, a8.after("h1", t))
                if t == 0:
                    pe.wait_ge(got8, 32)
                for k in range(KD):
                    mm = pe.matmul(bank[6][:, 64 * t:64 * t + NG + NE], hT[:, k, tok(t)], w_r[:, k, :], start=(k == 0), stop=(k == KD - 1))
                mm.then_inc(p8.step("lg", t), 1)

        @block.scalar
        def _(act):
            for t in range(NT):
                act.wait_ge(v8.sem, v8.after("mv", t))
                act.activation(rs8[:, 0, t:t + 1], mv8[:, 0, t, 1:2], ACT.Sqrt, bias=col(E_LN)).then_inc(a8.step("sqrt", t), 1)
                act.wait_ge(v8.sem, v8.after("mv2", t))
                act.activation(rs8[:, 1, t:t + 1], mv8[:, 1, t, 1:2], ACT.Sqrt, bias=col(E_LN)).then_inc(a8.step("sqrt2", t), 1)
                act.wait_ge(p8.sem, p8.after("tr", t))
                for f in range(2):
                    act.activation(hT[:, 4 * f:4 * f + 4, tok(t)], bank[4 + f][:, :].rearrange("p (k m) -> p k m", m=P),
                                   ACT.Copy).then_inc(a8.step(f"h{f}", t), 1)

        @block.gpsimd
        def _(pool):
            pool.wait_ge(got_x2, 48)
            for t in range(1, NT):
                pool.tensor_tensor(x1[:, t, :], x1[:, t, :], pos2[:, t - 1, :], ALU.add).then_inc(g8.step("pos", t), 1)
            pool.wait_ge(got8, 32)
            for t in range(NT):
                c = 1 if t else 0
                pool.wait_ge(v8.sem, v8.after("xn", t))
                pool.tensor_tensor(x1[:, t, :], x1[:, t, :], lnr[:, 0, :], ALU.mult).then_inc(g8.step("lg", t), 1)
                pool.wait_ge(g8.sem, g8.after("lg", t))
                pool.tensor_tensor(x1[:, t, :], x1[:, t, :], lnr[:, 1, :], ALU.add).then_inc(g8.step("lb", t), 1)
                pool.wait_ge(v8.sem, v8.after("xn2", t))
                pool.tensor_tensor(h2[:, t % 2, :], h2[:, t % 2, :], rows[:, 3, c, :], ALU.mult).then_inc(g8.step("sc", t), 1)
                pool.wait_ge(g8.sem, g8.after("sc", t))
                pool.tensor_tensor(h2[:, t % 2, :], h2[:, t % 2, :], rows[:, 2, c, :], ALU.add).then_inc(g8.step("sh", t), 1)

        @block.vector
        def _(dve):
            dve.wait_ge(got_x2, 48)
            for t in range(NT):
                c = 1 if t else 0
                m_ = h2[:, t % 2, :]
                if t >= 2:
                    dve.wait_ge(p8.sem, p8.after("tr", t - 2))
                    dve.wait_ge(sent8[t % 2], 16 * (t // 2))
                dve.wait_ge(p8.sem, p8.after("mix", t))
                for f in range(2):
                    fs = slice(512 * f, 512 * f + 512)
                    dve.tensor_tensor(m_[:, fs], bank[2 * (t % 2) + f][:, :], rows[:, 1, c, fs], ALU.mult).then_inc(v8.step(f"g{f}", t), 1)
                dve.wait_ge(v8.sem, v8.after("g1", t))
                if t:
                    dve.wait_ge(g8.sem, g8.after("pos", t))
                dve.scalar_tensor_tensor(x1[:, t, :], x1[:, t, :], ALPHA, m_, ALU.mult, ALU.add).then_inc(v8.step("res", t), 1)
                dve.wait_ge(v8.sem, v8.after("res", t))
                for i in range(2):
                    dve.bn_stats(st8[:, 0, i, :], x1[:, t, 512 * i:512 * i + 512]).then_inc(v8.step(f"s{i}", t), 1)
                dve.wait_ge(v8.sem, v8.after("s1", t))
                dve.bn_aggr(mv8[:, 0, t, :], st8[:, 0, :, :]).then_inc(v8.step("mv", t), 1)
                dve.wait_ge(a8.sem, a8.after("sqrt", t))
                dve.reciprocal(rs8[:, 0, t:t + 1], rs8[:, 0, t:t + 1]).then_inc(v8.step("rec", t), 1)
                dve.wait_ge(v8.sem, v8.after("rec", t))
                dve.tensor_scalar(x1[:, t, :], x1[:, t, :], mv8[:, 0, t, 0:1], rs8[:, 0, t:t + 1], ALU.subtract,
                                  ALU.mult).then_inc(v8.step("xn", t), 1)
                dve.wait_ge(g8.sem, g8.after("lb", t))
                for i in range(2):
                    dve.bn_stats(st8[:, 1, i, :], x1[:, t, 512 * i:512 * i + 512]).then_inc(v8.step(f"t{i}", t), 1)
                dve.wait_ge(v8.sem, v8.after("t1", t))
                dve.bn_aggr(mv8[:, 1, t, :], st8[:, 1, :, :]).then_inc(v8.step("mv2", t), 1)
                dve.wait_ge(a8.sem, a8.after("sqrt2", t))
                dve.reciprocal(rs8[:, 1, t:t + 1], rs8[:, 1, t:t + 1]).then_inc(v8.step("rec2", t), 1)
                dve.wait_ge(v8.sem, v8.after("rec2", t))
                dve.tensor_scalar(m_, x1[:, t, :], mv8[:, 1, t, 0:1], rs8[:, 1, t:t + 1], ALU.subtract,
                                  ALU.mult).then_inc(v8.step("xn2", t), 1)
    if stop <= 8:
        return dict(locals())

    NP = NT
    EW = KD * 2 * DE + 2 * D
    cursor[0] = rows_off + 2 * D * 4
    ew = sb("ew", [P, 4, EW])
    route_base = cursor[0]
    lgt = sb("lgt", [P, NT, NG + NE])
    lw = sb("lw", [P, NT, NG, EPG])
    ohg = sb("ohg", [P, NT, NG])
    ohk = sb("ohk", [P, 2, NT, EPG])
    w8 = sb("w8", [P, 5, NT, EPG])
    w1s = sb("w1s", [P, 12, NT])
    mk = sb("mk", [P, 2, NT, NE])
    mall = sb("mall", [P, NT, NE])
    rk = sb("rk", [P, 2, NT])
    rhs = sb("rhs", [P, 2, NT, 3, NE])
    oneh = sb("oneh", [P, 2, P])
    tmp = sb("tmp", [P, NP, 2, NE])
    cursor[0] = base0 - RING * 4096 * 4
    idx = sb("idx", [P, 2, NP * NE], I32)
    gate = sb("gate", [P, NP * NE])
    cnt = sb("cnt", [P, 4])
    cnti = sb("cnti", [P, 1], I32)
    moe_keep = cursor[0]
    got_e = [nc.alloc_semaphore(f"got_expert{x}") for x in range(4)]
    G_MAX, G_MIN, G_SUM, G_P, T_M1, T_M2, T_MN, T_E, T_S, W_1, W_2, _ = range(12)
    lv9 = ["lgt", "gmax", "geq", "gv", "gmin", "goh", "gsub", "gsum", "gp", "lsel0", "lsel1", "m1", "eq1", "v1", "mn1", "oh1", "le2",
           "m2", "eq2", "v2", "mn2", "oh2", "dm", "s", "r", "w1", "w2", "w2b", "mk1", "mk2", "mall"]
    lv9 += [("rank", k) for k in range(2)] + [("rank1", k) for k in range(2)] + [("rhs", k, i) for k in range(2) for i in range(3)]
    lv9 += ["cnt0", "cnt1"] + [("oneh", n) for n in range(10 * NP)]
    lv9 += [("tab", j, i) for j in range(NP) for i in range(2)] + ["tmp", "idx"]
    v9 = Steps(nc, "route_vector", [x if isinstance(x, tuple) else (x,) for x in lv9])
    a9, p9 = Steps(nc, "route_scalar", [("gexp",), ("dexp",)]), Steps(nc, "route_tensor", [("rank",)] + [("tab", n) for n in range(10 * NP)])
    EXPERT = lambda n: A["experts"][bass.ds(n, 1)].rearrange("a p n -> (a p) n")
    with nc.Block("route", no_gpsimd_drain=True) as block:
        @block.sync
        def _(sp):
            for x in range(4):
                sp.dma_start(ew[:, x, :], A["experts"][x]).then_inc(got_e[x], 16)

        @block.scalar
        def _(act):
            act.wait_ge(v9.sem, v9.after("gsub"))
            act.activation(w8[:, 0, :, 0:NG], w8[:, 0, :, 0:NG], ACT.Exp).then_inc(a9.step("gexp"), 1)
            act.wait_ge(v9.sem, v9.after("dm"))
            act.activation(w1s[:, T_E, :], w1s[:, T_E, :], ACT.Exp).then_inc(a9.step("dexp"), 1)

        @block.tensor
        def _(pe):
            pe.wait_ge(v9.sem, v9.after("mall"))
            su = cst[:, C_SU:C_SU + P]
            for t in range(NT):
                for t2 in range(t + 1):
                    pe.matmul(bank[0][:, NE * t:NE * t + NE], su if t2 == t else ones, mall[:, t2, :], start=(t2 == 0), stop=(t2 == t))
            for t in range(NT):
                mm = pe.matmul(bank[0][:, NE * NT:NE * NT + NE], ones, mall[:, t, :], start=(t == 0), stop=(t == NT - 1))
            mm.then_inc(p9.step("rank"), 1)
            n = 0
            for j in range(NP):
                for t in range(NT):
                    for k in range(2):
                        pe.wait_ge(v9.sem, v9.after("oneh", n))
                        pe.matmul(bank[1 + j][:, 0:3 * NE], oneh[:, n % 2, :], rhs[:, k, t, :, :].rearrange("p a e -> p (a e)"),
                                  start=(t == 0 and k == 0), stop=(t == NT - 1 and k == 1)).then_inc(p9.step("tab", n), 1)
                        n += 1

        @block.vector
        def _(dve):
            s1 = lambda x: w1s[:, x, :]
            b_ = lambda ap, n: bc(ap.unsqueeze(2), P, NT, n)
            iota = lambda n: bc(cst[:, C_IOTA:C_IOTA + n].unsqueeze(1), P, NT, n)
            dve.tensor_tensor(lgt[:], bank[6][:, 0:64 * NT].rearrange("p (t x) -> p t x", x=64)[:, :, 0:NG + NE],
                                  bc(row[:, R_BRG:R_BRG + NG + NE].unsqueeze(1), P, NT, NG + NE), ALU.add).then_inc(v9.step("lgt"), 1)
            dve.wait_ge(v9.sem, v9.after("lgt"))
            lg, le = lgt[:, :, 0:NG], lgt[:, :, NG:].rearrange("p t (g e) -> p t g e", g=NG)

            def first_max(x, n, best, low, work, out, names):
                dve.tensor_reduce(s1(best), x, AX, ALU.max).then_inc(v9.step(names[0]), 1)
                dve.wait_ge(v9.sem, v9.after(names[0]))
                dve.tensor_tensor(work, x, b_(s1(best), n), ALU.is_equal).then_inc(v9.step(names[1]), 1)
                dve.wait_ge(v9.sem, v9.after(names[1]))
                dve.scalar_tensor_tensor(work, work, -64.0, iota(n), ALU.mult, ALU.add).then_inc(v9.step(names[2]), 1)
                dve.wait_ge(v9.sem, v9.after(names[2]))
                dve.tensor_reduce(s1(low), work, AX, ALU.min).then_inc(v9.step(names[3]), 1)
                dve.wait_ge(v9.sem, v9.after(names[3]))
                dve.tensor_tensor(out, work, b_(s1(low), n), ALU.is_equal).then_inc(v9.step(names[4]), 1)
                dve.wait_ge(v9.sem, v9.after(names[4]))

            first_max(lg, NG, G_MAX, G_MIN, w8[:, 1, :, 0:NG], ohg[:], ("gmax", "geq", "gv", "gmin", "goh"))
            dve.tensor_tensor(w8[:, 0, :, 0:NG], lg, b_(s1(G_MAX), NG), ALU.subtract).then_inc(v9.step("gsub"), 1)
            dve.wait_ge(v9.sem, v9.after("gsub"))
            dve.wait_ge(a9.sem, a9.after("gexp"))
            dve.tensor_reduce(s1(G_SUM), w8[:, 0, :, 0:NG], AX, ALU.add).then_inc(v9.step("gsum"), 1)
            dve.wait_ge(v9.sem, v9.after("gsum"))
            dve.reciprocal(s1(G_P), s1(G_SUM)).then_inc(v9.step("gp"), 1)
            dve.wait_ge(v9.sem, v9.after("gp"))
            dve.tensor_tensor(lw[:], le, bc(ohg[:].unsqueeze(3), P, NT, NG, EPG), ALU.mult).then_inc(v9.step("lsel0"), 1)
            dve.wait_ge(v9.sem, v9.after("lsel0"))
            dve.tensor_reduce(w8[:, 2, :, :], lw[:].rearrange("p t g e -> p t e g"), AX, ALU.add).then_inc(v9.step("lsel1"), 1)
            dve.wait_ge(v9.sem, v9.after("lsel1"))
            first_max(w8[:, 2, :, :], EPG, T_M1, T_MN, w8[:, 3, :, :], ohk[:, 0, :, :], ("m1", "eq1", "v1", "mn1", "oh1"))
            dve.scalar_tensor_tensor(w8[:, 4, :, :], ohk[:, 0, :, :], NEG, w8[:, 2, :, :], ALU.mult, ALU.add).then_inc(v9.step("le2"), 1)
            dve.wait_ge(v9.sem, v9.after("le2"))
            first_max(w8[:, 4, :, :], EPG, T_M2, T_MN, w8[:, 3, :, :], ohk[:, 1, :, :], ("m2", "eq2", "v2", "mn2", "oh2"))
            dve.tensor_tensor(s1(T_E), s1(T_M2), s1(T_M1), ALU.subtract).then_inc(v9.step("dm"), 1)
            dve.wait_ge(v9.sem, v9.after("dm"))
            dve.wait_ge(a9.sem, a9.after("dexp"))
            dve.tensor_scalar(s1(T_S), s1(T_E), 1.0, None, ALU.add).then_inc(v9.step("s"), 1)
            dve.wait_ge(v9.sem, v9.after("s"))
            dve.reciprocal(s1(T_S), s1(T_S)).then_inc(v9.step("r"), 1)
            dve.wait_ge(v9.sem, v9.after("r"))
            dve.tensor_tensor(s1(W_1), s1(T_S), s1(G_P), ALU.mult).then_inc(v9.step("w1"), 1)
            dve.wait_ge(v9.sem, v9.after("w1"))
            dve.tensor_tensor(s1(W_2), s1(W_1), s1(T_E), ALU.mult).then_inc(v9.step("w2"), 1)
            dve.wait_ge(v9.sem, v9.after("w2"))
            dve.tensor_copy(s1(T_S), s1(W_2)).then_inc(v9.step("w2b"), 1)
            dve.wait_ge(v9.sem, v9.after("w2b"))
            for k in range(2):
                dve.tensor_tensor(mk[:, k, :, :].rearrange("p t (g e) -> p t g e", g=NG), bc(ohg[:].unsqueeze(3), P, NT, NG, EPG),
                                      bc(ohk[:, k, :, :].unsqueeze(2), P, NT, NG, EPG), ALU.mult).then_inc(v9.step(f"mk{k + 1}"), 1)
                dve.wait_ge(v9.sem, v9.after(f"mk{k + 1}"))
            dve.tensor_tensor(mall[:], mk[:, 0, :, :], mk[:, 1, :, :], ALU.add).then_inc(v9.step("mall"), 1)
            dve.wait_ge(v9.sem, v9.after("mall"))
            dve.wait_ge(p9.sem, p9.after("rank"))
            rank = bank[0][:, 0:NE * NT].rearrange("p (t e) -> p t e", e=NE)
            for k in range(2):
                dve.tensor_tensor(tmp[:, :, k, :], mk[:, k, :, :], rank, ALU.mult).then_inc(v9.step("rank", k), 1)
                dve.wait_ge(v9.sem, v9.after("rank", k))
            for k in range(2):
                dve.tensor_reduce(rk[:, k, :], tmp[:, :, k, :], AX, ALU.add).then_inc(v9.step("rank1", k), 1)
                dve.wait_ge(v9.sem, v9.after("rank1", k))
            for k in range(2):
                for i in range(2):
                    dve.tensor_tensor(rhs[:, k, :, i, :], mk[:, k, :, :], b_(cst[:, (C_TOKP if k and i else C_TOK1):(C_TOKP if k and i else C_TOK1) + NT], NE),
                                      ALU.mult).then_inc(v9.step("rhs", k, i), 1)
                dve.scalar_tensor_tensor(rhs[:, k, :, 2, :], mk[:, k, :, :], 0.5, b_(s1(W_1 + k), NE), ALU.mult,
                                         ALU.mult).then_inc(v9.step("rhs", k, 2), 1)
            dve.tensor_reduce(cnt[:, 0:1], bank[0][:, NE * NT:NE * NT + NE], AX, ALU.max).then_inc(v9.step("cnt0"), 1)
            dve.wait_ge(v9.sem, v9.after("cnt0"))
            dve.tensor_scalar(cnti[:], cnt[:, 0:1], 1.0, None, ALU.mult).then_inc(v9.step("cnt1"), 1)
            dve.wait_ge(v9.sem, v9.after("cnt1"))
            n = 0
            for j in range(NP):
                for t in range(NT):
                    for k in range(2):
                        if n >= 2:
                            dve.wait_ge(p9.sem, p9.after("tab", n - 2))
                        dve.tensor_scalar(oneh[:, n % 2, :], cst[:, C_IOTA + P * j:C_IOTA + P * j + P], rk[:, k, t:t + 1], None,
                                          ALU.is_equal).then_inc(v9.step("oneh", n), 1)
                        n += 1
            for j in range(NP):
                dve.wait_ge(p9.sem, p9.after("tab", 10 * j + 9))
                tab = bank[1 + j][:, 0:2 * NE].rearrange("p (a e) -> p a e", a=2)
                dve.tensor_scalar(gate[:, NE * j:NE * j + NE], bank[1 + j][:, 2 * NE:3 * NE], 1.0, None, ALU.mult).then_inc(v9.step("tab", j, 0), 1)
                dve.tensor_scalar(tmp[:, j, :, :], tab, -1.0, None, ALU.add).then_inc(v9.step("tab", j, 1), 1)
            dve.wait_ge(v9.sem, v9.after("tab", NP - 1, 1))
            dve.tensor_scalar(rhs[:, 0, :, 0:2, :], tmp[:], 0.0, 65536.0, ALU.is_lt, ALU.mult).then_inc(v9.step("tmp"), 1)
            dve.wait_ge(v9.sem, v9.after("tmp"))
            dve.tensor_tensor(idx[:].rearrange("p a (j e) -> p j a e", e=NE), tmp[:], rhs[:, 0, :, 0:2, :], ALU.add).then_inc(v9.step("idx"), 1)
            dve.wait_ge(v9.sem, v9.after("idx"))
    if stop <= 9:
        return dict(locals())

    xg = nc.alloc_sbuf_tensor_at("xg", [P, 2, D], F32, offset=hT_off)
    xgT = nc.alloc_sbuf_tensor_at("xgT", [P, 2, KD, P], F32, offset=hT_off + 2 * D * 4)
    cursor[0] = route_base
    uh = sb("uh", [P, 2, DE])
    hid = sb("hid", [P, 2, DE])
    hidT = sb("hidT", [P, 2, 2 * P])
    cursor[0] = moe_keep
    yo = sb("yo", [P, 2, D])
    ig = sb("ig", [P, 4, 1], I32)
    isc = sb("isc", [P, 4, 1], I32)
    gsc = sb("gsc", [P, 4, 1])
    gathered = [nc.alloc_semaphore(f"gathered{i}") for i in range(2)]
    scattered = [nc.alloc_semaphore(f"scattered{i}") for i in range(2)]
    zeroed = nc.alloc_semaphore("gather_zeroed")

    class Marks:
        def __init__(self, name, labels):
            self.sem = {x: nc.alloc_semaphore(f"{name}_{x}") for x in labels}

    pt_m = Marks("te", ("xT", "hT", "f1", "f2"))
    ac_m = Marks("se", ("x", "tanh", "h", "y"))
    ve_m = Marks("ve", ("x", "u", "hid", "y"))
    po_m = Marks("pe", ("small", "gather", "scatter"))

    def sync_pass(sp, n0, first_pass):
        if not first_pass:
            for x in range(4):
                sp.wait_ge(pt_m.sem["f2"], n0 + x - 4 + 1)
                sp.dma_start(ew[:, x, :], A["experts"][x]).then_inc(got_e[x], 16)
        with sp.Fori(0, NE // 4 - 1) as i:
            for x in range(4):
                sp.wait_ge(pt_m.sem["f2"], n0 + 4 * i + x + 1)
                sp.dma_start(ew[:, x, :], EXPERT(4 * i + (x + 4))).then_inc(got_e[x], 16)

    last_row = []

    def pool_pass(pool, n0, first_pass):
        def prepare(n, x):
            if not (first_pass and isinstance(n, int) and n < 2):
                pool.wait_ge(pt_m.sem["xT"], n - 2 + 1)
            if not (first_pass and isinstance(n, int) and n < 4):
                pool.wait_ge(scattered[x % 2], half16(n, x) - 32)
                pool.wait_ge(ve_m.sem["hid"], n - 4 + 1)
            pool.tensor_copy(ig[:, x, :], idx[:, 0, bass.ds(n, 1)])
            pool.tensor_copy(gsc[:, x, :], gate[:, bass.ds(n, 1)])
            pool.tensor_copy(isc[:, x, :], idx[:, 1, bass.ds(n, 1)]).then_inc(po_m.sem["small"], 1)
            pool.wait_ge(po_m.sem["small"], n + 1)
            pool.sem_inc(po_m.sem["gather"], 1)
            pool.indirect_dma_start(xg[:, x % 2, :], None, h2d, bass.IndirectOffsetOnAxis(ig[:, x, :], 0),
                                    bounds_check=last_row[0], oob_is_err=False).then_inc(gathered[x % 2], 16)

        def scatter(n, x):
            pool.wait_ge(ac_m.sem["y"], n + 1)
            pool.wait_ge(ve_m.sem["y"], n + 1)
            pool.sem_inc(po_m.sem["scatter"], 1)
            pool.indirect_dma_start(yd, bass.IndirectOffsetOnAxis(isc[:, x, :], 0), yo[:, x % 2, :], None,
                                    bounds_check=last_row[1], oob_is_err=False).then_inc(scattered[x % 2], 16)

        for x in range(4):
            prepare(n0 + x, x)
        scatter(n0, 0)
        with pool.Fori(0, NE // 4 - 1) as i:
            for x in range(4):
                prepare(n0 + 4 * i + (x + 4), x)
                scatter(n0 + 4 * i + (x + 1), (x + 1) % 4)
        for n in range(NE - 3, NE):
            scatter(n0 + n, n % 4)
        pool.wait_ge(scattered[0], half16(n0 + NE - 2, 2))
        pool.wait_ge(scattered[1], half16(n0 + NE - 1, 3))

    def pe_pass(pe, n0, first_pass):
        def xT(n, x):
            pe.wait_ge(gathered[x % 2], half16(n, x))
            if not (first_pass and isinstance(n, int) and n < 1):
                pe.wait_ge(ac_m.sem["x"], n - 1 + 1)
                pe.wait_ge(ve_m.sem["x"], n - 1 + 1)
            for k in range(KD):
                mm = pe.transpose(bank[k // 4][:, P * (k % 4):P * (k % 4) + P], xg[:, x % 2, P * k:P * k + P], ident)
            mm.then_inc(pt_m.sem["xT"], 1)

        def hT_(n, x):
            pe.wait_ge(ve_m.sem["hid"], n + 1)
            for k in range(2):
                mm = pe.transpose(bank[4][:, P * k:P * k + P], hid[:, x % 2, P * k:P * k + P], ident)
            mm.then_inc(pt_m.sem["hT"], 1)

        def ffn1(n, x):
            pe.wait_ge(got_e[x], quarter16(n, x))
            pe.wait_ge(ac_m.sem["x"], n + 1)
            pe.wait_ge(ve_m.sem["x"], n + 1)
            if not (first_pass and isinstance(n, int) and n < 2):
                pe.wait_ge(ve_m.sem["hid"], n - 2 + 1)
            for k in range(KD):
                mm = pe.matmul(bank[2 + x % 2][:, :], xgT[:, x % 2, k, :], ew[:, x, 2 * DE * k:2 * DE * (k + 1)], start=(k == 0), stop=(k == KD - 1))
            mm.then_inc(pt_m.sem["f1"], 1)

        def ffn2(n, x):
            pe.wait_ge(ac_m.sem["h"], n + 1)
            if not (first_pass and isinstance(n, int) and n < 1):
                pe.wait_ge(ac_m.sem["y"], n - 1 + 1)
                pe.wait_ge(ve_m.sem["y"], n - 1 + 1)
            for f in range(2):
                for k in range(2):
                    at = KD * 2 * DE + D * k + 512 * f
                    mm = pe.matmul(bank[5 + f][:, :], hidT[:, x % 2, P * k:P * k + P], ew[:, x, at:at + 512], start=(k == 0), stop=(k == 1))
            mm.then_inc(pt_m.sem["f2"], 1)

        def step(n, x, more=True):
            hT_(n - 1, (x - 1) % 4)
            ffn1(n, x)
            if more:
                xT(n + 1, (x + 1) % 4)
            ffn2(n - 1, (x - 1) % 4)

        xT(n0, 0)
        ffn1(n0, 0)
        xT(n0 + 1, 1)
        step(n0 + 1, 1)
        with pe.Fori(0, NE // 4 - 1) as i:
            for x in range(4):
                step(n0 + 4 * i + (2 + x), (2 + x) % 4)
        step(n0 + NE - 2, 2)
        step(n0 + NE - 1, 3, more=False)
        hT_(n0 + NE - 1, 3)
        ffn2(n0 + NE - 1, 3)

    def act_pass(act, n0, first_pass):
        def x_(n, x):
            act.wait_ge(pt_m.sem["xT"], n + 1)
            if not (first_pass and isinstance(n, int) and n < 2):
                act.wait_ge(pt_m.sem["f1"], n - 2 + 1)
            act.activation(xgT[:, x % 2, 0:4, :], bank[0][:, :].rearrange("p (k m) -> p k m", m=P), ACT.Copy).then_inc(ac_m.sem["x"], 1)

        def h_(n, x):
            act.wait_ge(pt_m.sem["hT"], n + 1)
            if not (first_pass and isinstance(n, int) and n < 2):
                act.wait_ge(pt_m.sem["f2"], n - 2 + 1)
            act.activation(hidT[:, x % 2, :], bank[4][:, 0:2 * P], ACT.Copy).then_inc(ac_m.sem["h"], 1)

        def tanh(n, x):
            act.wait_ge(pt_m.sem["f1"], n + 1)
            if not (first_pass and isinstance(n, int) and n < 2):
                act.wait_ge(ve_m.sem["hid"], n - 2 + 1)
            act.activation(uh[:, x % 2, :], bank[2 + x % 2][:, 0:DE], ACT.Tanh, scale=0.5).then_inc(ac_m.sem["tanh"], 1)

        def y_(n, x):
            act.wait_ge(pt_m.sem["f2"], n + 1)
            if not (first_pass and isinstance(n, int) and n < 2):
                act.wait_ge(scattered[x % 2], half16(n, x) - 16)
            act.activation(yo[:, x % 2, 0:512], bank[5][:, :], ACT.Copy).then_inc(ac_m.sem["y"], 1)

        def step(n, x, more=True):
            h_(n - 1, (x - 1) % 4)
            tanh(n, x)
            if more:
                x_(n + 1, (x + 1) % 4)
            y_(n - 1, (x - 1) % 4)

        x_(n0, 0)
        tanh(n0, 0)
        x_(n0 + 1, 1)
        step(n0 + 1, 1)
        step(n0 + 2, 2)
        with act.Fori(0, NE // 4 - 2) as i:
            for x in range(4):
                step(n0 + 4 * i + (3 + x), (3 + x) % 4)
        for n in range(NE - 5, NE):
            step(n0 + n, n % 4, more=(n < NE - 1))
        h_(n0 + NE - 1, 3)
        y_(n0 + NE - 1, 3)

    def dve_pass(dve, n0, first_pass):
        def x_(n, x):
            dve.wait_ge(pt_m.sem["xT"], n + 1)
            if not (first_pass and isinstance(n, int) and n < 2):
                dve.wait_ge(pt_m.sem["f1"], n - 2 + 1)
            dve.tensor_copy(xgT[:, x % 2, 4:8, :], bank[1][:, :].rearrange("p (k m) -> p k m", m=P)).then_inc(ve_m.sem["x"], 1)

        def hid_(n, x):
            dve.wait_ge(ac_m.sem["tanh"], n + 1)
            if not (first_pass and isinstance(n, int) and n < 2):
                dve.wait_ge(pt_m.sem["hT"], n - 2 + 1)
            b = bank[2 + x % 2]
            dve.scalar_tensor_tensor(uh[:, x % 2, :], uh[:, x % 2, :], 1.0, b[:, 0:DE], ALU.add, ALU.mult).then_inc(ve_m.sem["u"], 1)
            dve.wait_ge(ve_m.sem["u"], n + 1)
            dve.wait_ge(po_m.sem["small"], n + 1)
            dve.scalar_tensor_tensor(hid[:, x % 2, :], uh[:, x % 2, :], gsc[:, x, :], b[:, DE:2 * DE], ALU.mult,
                                     ALU.mult).then_inc(ve_m.sem["hid"], 1)

        def y_(n, x):
            dve.wait_ge(pt_m.sem["f2"], n + 1)
            if not (first_pass and isinstance(n, int) and n < 2):
                dve.wait_ge(scattered[x % 2], half16(n, x) - 16)
            dve.tensor_copy(yo[:, x % 2, 512:D], bank[6][:, :]).then_inc(ve_m.sem["y"], 1)

        def step(n, x, more=True):
            hid_(n, x)
            if more:
                x_(n + 1, (x + 1) % 4)
            y_(n - 1, (x - 1) % 4)

        x_(n0, 0)
        hid_(n0, 0)
        x_(n0 + 1, 1)
        step(n0 + 1, 1)
        step(n0 + 2, 2)
        with dve.Fori(0, NE // 4 - 2) as i:
            for x in range(4):
                step(n0 + 4 * i + (3 + x), (3 + x) % 4)
        for n in range(NE - 5, NE):
            step(n0 + n, n % 4, more=(n < NE - 1))
        y_(n0 + NE - 1, 3)

    def half16(n, x):
        return (n - x % 2) * 8 + 16

    def quarter16(n, x):
        return (n - x) * 4 + 16

    def all_passes(e, one_pass):
        one_pass(e, 0, True)
        most = e.value_load(cnti[0:1, 0:1], min_val=0, max_val=T)
        for j in range(1, NP):
            with e.If(most > P * j):
                one_pass(e, NE * j, False)
                e.nop()

    with nc.Block("experts", no_gpsimd_drain=True) as block:
        @block.sync
        def _(sp):
            all_passes(sp, sync_pass)

        @block.gpsimd
        def _(pool):
            last_row.extend([pool.to_reg(T - 1), pool.to_reg(2 * T - 1)])
            pool.memset(xg[:], 0.0).then_inc(zeroed, 1)
            pool.wait_ge(zeroed, 1)
            all_passes(pool, pool_pass)

        @block.tensor
        def _(pe):
            all_passes(pe, pe_pass)

        @block.scalar
        def _(act):
            all_passes(act, act_pass)

        @block.vector
        def _(dve):
            all_passes(dve, dve_pass)
    if stop <= 10:
        return dict(locals())

    cursor[0] = route_base - 4 * EW * 4
    yt = sb("yt", [P, 2, 2, D])
    lnr2 = sb("lnr2", [P, 2, D])
    st11 = sb("st11", [P, 2, 6])
    mv11 = sb("mv11", [P, NT, 2])
    rs11 = sb("rs11", [P, NT])
    got_y = [nc.alloc_semaphore(f"got_y{i}") for i in range(2)]
    got_l2 = nc.alloc_semaphore("got_ln2_rows")
    out_sent = nc.alloc_semaphore("out_sent")
    v11 = Steps(nc, "final_vector", [(k, t) for t in range(NT) for k in ("gate", "res", "s0", "s1", "mv", "rec", "xn")])
    a11 = Steps(nc, "final_scalar", [("sqrt", t) for t in range(NT)])
    g11 = Steps(nc, "final_gpsimd", [("sum", 0)] + [x for t in range(NT) for x in ([("sum", t + 1)] if t < NT - 1 else []) + [("lg", t), ("lb", t)]])
    with nc.Block("final", no_gpsimd_drain=True) as block:
        @block.sync
        def _(sp):
            sp.dma_start(lnr2[:], A["ln"][2 * D:4 * D].partition_broadcast(P).rearrange("p (a d) -> p a d", a=2)).then_inc(got_l2, 16)
            for t in range(NT):
                if t >= 2:
                    sp.wait_ge(v11.sem, v11.after("gate", t - 2))
                sp.dma_start(yt[:, t % 2, :, :], yd.rearrange("(k r) d -> r k d", k=2)[t * P:t * P + P]).then_inc(got_y[t % 2], 16)
                if t:
                    sp.wait_ge(g11.sem, g11.after("lb", t - 1))
                    sp.dma_start(O["y"][(t - 1) * P:t * P, :], x1[:, t - 1, :]).then_inc(out_sent, 16)
            sp.wait_ge(g11.sem, g11.after("lb", NT - 1))
            sp.dma_start(O["y"][(NT - 1) * P:NT * P, :], x1[:, NT - 1, :]).then_inc(out_sent, 16)
            sp.wait_ge(out_sent, 16 * NT)

        @block.gpsimd
        def _(pool):
            def add(t):
                pool.wait_ge(got_y[t % 2], 16 * (t // 2 + 1))
                pool.tensor_tensor(yt[:, t % 2, 0, :], yt[:, t % 2, 0, :], yt[:, t % 2, 1, :], ALU.add).then_inc(g11.step("sum", t), 1)

            pool.wait_ge(got_l2, 16)
            add(0)
            for t in range(NT):
                if t < NT - 1:
                    add(t + 1)
                pool.wait_ge(v11.sem, v11.after("xn", t))
                pool.tensor_tensor(x1[:, t, :], x1[:, t, :], lnr2[:, 0, :], ALU.mult).then_inc(g11.step("lg", t), 1)
                pool.wait_ge(g11.sem, g11.after("lg", t))
                pool.tensor_tensor(x1[:, t, :], x1[:, t, :], lnr2[:, 1, :], ALU.add).then_inc(g11.step("lb", t), 1)

        @block.scalar
        def _(act):
            for t in range(NT):
                act.wait_ge(v11.sem, v11.after("mv", t))
                act.activation(rs11[:, t:t + 1], mv11[:, t, 1:2], ACT.Sqrt, bias=col(E_LN)).then_inc(a11.step("sqrt", t), 1)

        @block.vector
        def _(dve):
            for t in range(NT):
                dve.wait_ge(g11.sem, g11.after("sum", t))
                dve.tensor_tensor(yt[:, t % 2, 0, :], yt[:, t % 2, 0, :], rows[:, 0, 1 if t else 0, :], ALU.mult).then_inc(v11.step("gate", t), 1)
                dve.wait_ge(v11.sem, v11.after("gate", t))
                dve.scalar_tensor_tensor(x1[:, t, :], x1[:, t, :], ALPHA, yt[:, t % 2, 0, :], ALU.mult, ALU.add).then_inc(v11.step("res", t), 1)
                dve.wait_ge(v11.sem, v11.after("res", t))
                for i in range(2):
                    dve.bn_stats(st11[:, i, :], x1[:, t, 512 * i:512 * i + 512]).then_inc(v11.step(f"s{i}", t), 1)
                dve.wait_ge(v11.sem, v11.after("s1", t))
                dve.bn_aggr(mv11[:, t, :], st11[:]).then_inc(v11.step("mv", t), 1)
                dve.wait_ge(a11.sem, a11.after("sqrt", t))
                dve.reciprocal(rs11[:, t:t + 1], rs11[:, t:t + 1]).then_inc(v11.step("rec", t), 1)
                dve.wait_ge(v11.sem, v11.after("rec", t))
                dve.tensor_scalar(x1[:, t, :], x1[:, t, :], mv11[:, t, 0:1], rs11[:, t:t + 1], ALU.subtract, ALU.mult).then_inc(v11.step("xn", t), 1)
    return dict(locals())


def host_layout(i):
    import numpy as np

    f = {k: np.asarray(v) for k, v in i.items()}
    out = {}
    rows = lambda *names: [f[n].reshape(-1, P) for n in names]
    out["vecs"] = np.ascontiguousarray(np.concatenate(rows(
        "b_mod", "conv_a", "conv_b_w", "conv_b_b", "lru_ba", "lru_bx", "lru_lambda", "delta_norm", "mlstm_norm",
        "state_lru", "state_mlstm_n")).T)
    out["rows"] = np.concatenate([f[n].reshape(-1) for n in (
        "delta_a_log", "delta_dt_bias", "mlstm_bi", "mlstm_bf", "state_mlstm_m", "b_rg", "b_re")])
    out["cond"] = np.ascontiguousarray(np.stack([f["c_ctx"].reshape(KD, P).T, f["c"].reshape(KD, P).T], axis=2))
    out["xp"], out["xs"] = f["x_prompt"][0], f["x_sample"][0]
    w_in, w_mod = f["w_in"][0], f["w_mod"][0]
    at = {0: 1536, 1: 2576, 2: 0, 3: 512, 4: 1024, 5: 2048, 6: 3088, 7: 3600, 8: 4112, 9: 4624}
    blocks = np.empty((len(BLOCKS), P, 4096), w_in.dtype)
    for n, (kind, m) in enumerate(BLOCKS):
        w = w_mod[:, 512 * m:512 * m + 512] if kind == "mod" else w_in[:, at[m]:at[m] + 512]
        blocks[n].reshape(P, KD, 512)[:] = w.reshape(KD, P, 512).transpose(1, 0, 2)
    out["blocks"] = blocks
    small = np.concatenate([w_in[:, 2560:2576], w_in[:, 5136:5152]], axis=1)
    out["w_small"] = np.ascontiguousarray(small.reshape(KD, P, 32).transpose(1, 0, 2))
    out["w_lru"] = np.ascontiguousarray(np.stack([f["lru_wa"][0], f["lru_wx"][0]]).transpose(3, 0, 1, 2, 4))
    out["s_delta"] = np.ascontiguousarray(f["state_delta"][0, 0].transpose(0, 2, 1, 3).reshape(2, P, H * HD))
    out["s_mc"] = np.ascontiguousarray(f["state_mlstm_C"][0, 0].transpose(0, 2, 1, 3).reshape(2, P, H * HD))
    merge = np.empty((KD, P, 3, KD + 4, P), w_in.dtype)
    for b, name in enumerate(("w_pa", "w_pb", "w_pc")):
        gate = w_in[:, 5152 + D * b:5152 + D * (b + 1)].reshape(KD, P, KD, P)
        merge[:, :, b, 0:KD] = gate.transpose(2, 1, 0, 3)
        merge[:, :, b, KD:] = f[name][0].reshape(4, P, KD, P).transpose(2, 1, 0, 3)
    out["merge"] = merge.reshape(KD, P, -1)
    out["w_out"] = np.ascontiguousarray(f["w_out"][0].reshape(KD, P, D).transpose(1, 0, 2))
    out["w_r"] = np.ascontiguousarray(np.concatenate([f["w_rg"][0], f["w_re"][0]], axis=1).reshape(KD, P, NG + NE).transpose(1, 0, 2))
    out["ln"] = np.concatenate([f[n].reshape(-1) for n in ("ln1_g", "ln1_b", "ln2_g", "ln2_b")])
    experts = np.empty((NE, P, KD * 2 * DE + 2 * D), w_in.dtype)
    first = experts[:, :, :KD * 2 * DE].reshape(NE, P, KD, 2, DE)
    for b, name in enumerate(("w_e1", "w_e3")):
        first[:, :, :, b] = f[name][0].reshape(NE, KD, P, DE).transpose(0, 2, 1, 3)
    experts[:, :, KD * 2 * DE:].reshape(NE, P, 2, D)[:] = f["w_e2"][0].reshape(NE, 2, P, D).transpose(0, 2, 1, 3)
    out["experts"] = experts
    out.update(shape_constants())
    return out


def shape_constants():
    import numpy as np

    p = np.arange(P)
    c = np.zeros((P, N_CONST), np.float32)
    c[:, C_ID:C_ID + P] = np.eye(P)
    c[:, C_TRI:C_TRI + P] = p[:, None] <= p[None]
    c[:, C_TRI + P:C_TRI + 2 * P] = p[:, None] >= p[None]
    c[:, C_ONE:C_ONE + P] = 1.0
    c[:, C_NEG:C_NEG + P] = np.where(p[None] <= p[:, None], 0.0, NEG)
    c[:, C_NEG + P:C_NEG + 2 * P] = np.where(p[None] >= p[:, None], 0.0, NEG)
    c[:, C_SU:C_SU + P] = p[:, None] < p[None]
    c[:, C_IOTA:C_IOTA + NT * P] = np.arange(NT * P)
    c[:, C_COL:C_COL + len(COLS)] = COLS
    c[:, C_TOK1:C_TOK1 + NT] = p[:, None] + P * np.arange(NT) + 1
    c[:, C_TOKP:C_TOKP + NT] = p[:, None] + P * np.arange(NT) + 1 + T
    lev = np.zeros((P, 2, LEVELS, P), np.int32)
    for n in range(LEVELS):
        s = 1 << n
        pair = (p[:, None] // (2 * s) == p[None] // (2 * s)) & (p[:, None] // s != p[None] // s)
        lev[:, 0, n] = pair & (p[:, None] > p[None])
        lev[:, 1, n] = pair & (p[:, None] < p[None])
    rows, grid = T_LAT // 64, 64
    freqs = np.exp(-math.log(10000.0) * np.arange(D // 4, dtype=np.float32) / (D // 4)).astype(np.float32)
    r, q = np.meshgrid(np.arange(rows, dtype=np.float32), np.arange(grid, dtype=np.float32), indexing="ij")
    ar, ac = r.reshape(-1, 1) * freqs, q.reshape(-1, 1) * freqs
    pos = np.concatenate([np.sin(ar), np.cos(ar), np.sin(ac), np.cos(ac)], axis=-1).astype(np.float32)
    return {"consts": c, "levels": lev, "pos": pos}


OUTPUTS = {"lru": (P, 8), "delta": (2, P, H * HD), "mc": (2, P, H * HD), "mn": (2, P, H), "mm": (8,), "y": (T, D)}


def build(nc, shapes, stop=99, dbg=None):
    A = {n: nc.dram_tensor(f"in_{n}", s, mybir.dt.from_np(d), kind="ExternalInput").ap() for n, (s, d) in shapes.items()}
    O = {n: nc.dram_tensor(f"out_{n}", s, F32, kind="ExternalOutput").ap() for n, s in OUTPUTS.items()}
    return program(nc, A, O, dbg, stop)


def unlay(o):
    import numpy as np

    per_head = lambda a: np.ascontiguousarray(a.reshape(2, P, H, HD).transpose(0, 2, 1, 3))[None, None]
    return (o["y"][:T_CTX][None], o["y"][T_CTX:][None], per_head(o["delta"]),
            np.ascontiguousarray(o["lru"].reshape(P, 2, 4).transpose(1, 2, 0)).reshape(1, 1, 2, 512), per_head(o["mc"]),
            np.ascontiguousarray(o["mn"].transpose(0, 2, 1))[None, None], o["mm"].reshape(1, 1, 2, H))


def kernel(**inputs):
    import concourse.bacc as bacc
    from concourse.bass_utils import run_bass_kernel_spmd

    arrays = host_layout(inputs)
    nc = bacc.Bacc("TRN2", target_bir_lowering=False, num_devices=1)
    build(nc, {n: (a.shape, a.dtype) for n, a in arrays.items()})
    r = run_bass_kernel_spmd(nc, [{f"in_{n}": a for n, a in arrays.items()}], core_ids=[0])
    return unlay({n: r.results[0][f"out_{n}"] for n in OUTPUTS})
```

```python
import math

import concourse.bass as bass
from concourse import mybir

F32 = mybir.dt.float32
I32 = mybir.dt.int32
ALU = mybir.AluOpType
ACT = mybir.ActivationFunctionType
AX = mybir.AxisListType.X

P = 128
D = 1024
KD = D // P
T_CTX, T_LAT = 128, 512
T = T_CTX + T_LAT
NT = T // P
H = 4
HD = 128
LN_EPS, RMS_EPS = 1e-5, 1e-6
ALPHA = 2.0 ** 0.25
NG, EPG = 4, 8
NE = NG * EPG
DE = 256
CW = T + 2
LAT = T_CTX + 2
RAW = CW + 3
NEG = -1.0e30
LEVELS = 7

C_ID, C_TRI, C_ONE, C_NEG, C_SU, C_IOTA, C_COL = 0, 128, 384, 512, 768, 896, 1536
C_TOK1, C_TOKP = C_COL + 8, C_COL + 16
N_CONST = C_COL + 32
COLS = [LN_EPS, RMS_EPS, 128 * RMS_EPS, 0.0, 1.0, 0.5]
E_LN, E_RMS, E_RMS128, E_ZERO, E_ONE, E_HALF = [C_COL + i for i in range(6)]
V_BMOD, V_CONVA, V_CONVB, V_CONVBB, V_BA, V_BX, V_LAM, V_DN, V_MN, V_SLRU, V_SN = 0, 48, 96, 112, 116, 124, 132, 140, 141, 145, 153
N_VEC = 161
R_ALOG, R_DT, R_BI, R_BF, R_M, R_BRG, R_BRE = 0, 8, 16, 24, 32, 40, 44
N_ROW = 76
RING = 2


def tok(tt):
    return slice(tt * P, tt * P + P)


def ctok(tt):
    lo = 0 if tt == 0 else LAT + (tt - 1) * P
    return slice(lo, lo + P)


BLOCKS = [("mod", n) for n in range(4)]
BLOCKS += [x for n in range(6) for x in (("mod", 4 + n), ("in", n))] + [("mod", 10), ("mod", 11)]
BLOCKS += [("in", n) for n in range(6, 10)]


class Steps:

    def __init__(self, nc, name, labels):
        self.sem = nc.alloc_semaphore(name)
        self.at = {x: n + 1 for n, x in enumerate(labels)}
        self.n, self.count = 0, len(labels)
        assert len(self.at) == len(labels), name

    def step(self, *label):
        self.n += 1
        assert self.at[label] == self.n, (label, self.at[label], self.n)
        return self.sem

    def after(self, *label):
        return self.at[label]


class LoopSteps(Steps):

    def credit(self, e):
        e.sem_inc(self.sem, self.count)

    def turn(self):
        self.n = 0

    def after(self, *label, turn):
        return (turn + 1) * self.count + self.at[label]


def program(nc, A, O, stop=99):
    cursor = [0]

    def sb(name, shape, dt=F32):
        n = 4
        for s in shape[1:]:
            n *= s
        off = cursor[0]
        cursor[0] = off + (n + 31) // 32 * 32
        assert cursor[0] <= 229344, (name, cursor[0])
        return nc.alloc_sbuf_tensor_at(name, list(shape), dt, offset=off)

    cursor[0] = (nc.sbuf_base + 63) // 64 * 64
    bank = [nc.alloc_psum_tensor(f"bank{i}", [P, 512], F32) for i in range(8)]

    def bc(ap, *shape):
        return ap.to_broadcast(list(shape))

    def heads(ap, n=HD):
        return ap.rearrange("p (h i) -> p h i", h=H)

    cst = sb("cst", [P, N_CONST])
    lev = sb("lev", [P, 2, LEVELS, P], I32)
    vec = sb("vec", [P, N_VEC])
    row = sb("row", [P, N_ROW])
    cond = sb("cond", [P, KD, 2])
    modc = sb("modc", [P, 48, 2])
    smg = sb("smg", [P, NT, 32])
    hT_off = cursor[0]
    hT = sb("hT", [P, KD, T])
    yA_off = cursor[0]
    yA = sb("yA", [P, H, T])
    yB = sb("yB", [P, H, T])
    yC = sb("yC", [P, H, T])
    ident = cst[:, C_ID:C_ID + P]
    tri = [cst[:, C_TRI + P * d:C_TRI + P * d + P] for d in range(2)]
    ones = cst[:, C_ONE:C_ONE + P]
    neg = [cst[:, C_NEG + P * d:C_NEG + P * d + P] for d in range(2)]
    col = lambda c: cst[:, c:c + 1]
    ring = sb("ring", [P, RING, 4096])

    landed = [nc.alloc_semaphore(f"block_landed{i}") for i in range(RING)]
    used = nc.alloc_semaphore("mod_block_used")
    stored = nc.alloc_semaphore("stored")
    stores = [0]
    N_BLOCK = len(BLOCKS)

    def load_block(sp, n, sem=None, value=0):
        if n < N_BLOCK:
            if n >= RING:
                sp.wait_ge(sem, value)
            sp.dma_start(ring[:, n % RING, :], A["blocks"][n]).then_inc(landed[n % RING], 16)

    def block_ready(pe, n):
        pe.wait_ge(landed[n % RING], 16 * (n // RING + 1))

    def store(sp, out, in_):
        stores[0] += 16
        sp.dma_start(out, in_).then_inc(stored, 16)

    def mod_rows(pe, n, out):
        for k in range(KD):
            mm = pe.matmul(out, cond[:, k, :], ring[:, n % RING, 512 * k:512 * k + 512], start=(k == 0), stop=(k == KD - 1))
        return mm

    def mod_columns(pe, out, rows2):
        for j in range(4):
            mm = pe.transpose(out[:, 2 * j:2 * j + 2], rows2[:, P * j:P * j + P], ident[0:2, 0:2])
        return mm

    base0 = cursor[0]

    x_sb = sb("x_sb", [P, NT, D])
    pos_sb = sb("pos_sb", [P, NT - 1, D])
    cond_t = sb("cond_t", [P, KD, 2])
    mrow0 = sb("mrow0", [2, 4, 512])
    stats = sb("stats", [P, NT, 2, 6])
    mv = sb("mv", [P, NT, 2])
    rstd = sb("rstd", [P, NT])
    got_cst = nc.alloc_semaphore("got_constants")
    got_lev = nc.alloc_semaphore("got_levels")
    got_x = [nc.alloc_semaphore(f"got_x{i}") for i in range(NT)]
    got_pos = nc.alloc_semaphore("got_pos")
    vs = Steps(nc, "ln1_vector", [("cond", 0)] + [(k, t) for t in range(NT) for k in ("stat0", "stat1", "mv")]
               + [(k, t) for t in range(NT) for k in ("rec", "xn")] + [("modc", 0), ("scale1", 0)]
               + [("h", k) for k in range(KD)])
    as_ = Steps(nc, "ln1_scalar", [("tanh", 0)] + [("sqrt", t) for t in range(NT)] + [("row", m) for m in range(4)] + [("hc", k) for k in range(KD)])
    ps = Steps(nc, "ln1_tensor", [("columns", m) for m in range(4)] + [("xt", k) for k in range(KD)])
    gs = Steps(nc, "ln1_gpsimd", [("pos", t) for t in range(1, NT)])

    with nc.Block("ln1", no_gpsimd_drain=True) as block:
        @block.sync
        def _(sp):
            sp.dma_start(cond[:], A["cond"]).then_inc(got_cst, 16)
            sp.dma_start(vec[:], A["vecs"]).then_inc(got_cst, 16)
            sp.dma_start(cst[:], A["consts"]).then_inc(got_cst, 16)
            sp.dma_start(row[:], A["rows"].partition_broadcast(P)).then_inc(got_cst, 16)
            load_block(sp, 0)
            load_block(sp, 1)
            sp.dma_start(x_sb[:, 0, :], A["xp"]).then_inc(got_x[0], 16)
            for t in range(1, NT):
                sp.dma_start(x_sb[:, t, :], A["xs"][(t - 1) * P:t * P, :]).then_inc(got_x[t], 16)
            sp.dma_start(pos_sb[:], A["pos"].rearrange("(t p) d -> p t d", p=P)).then_inc(got_pos, 16)
            for n in range(4):
                load_block(sp, n + RING, used, n + 1)
            sp.dma_start(lev[:], A["levels"]).then_inc(got_lev, 16)

        @block.gpsimd
        def _(pool):
            pool.wait_ge(got_pos, 16)
            for t in range(1, NT):
                pool.wait_ge(got_x[t], 16)
                pool.tensor_tensor(x_sb[:, t, :], x_sb[:, t, :], pos_sb[:, t - 1, :], ALU.add).then_inc(gs.step("pos", t), 1)

        @block.scalar
        def _(act):
            act.wait_ge(got_cst, 64)
            act.activation(cond_t[:], cond[:], ACT.Tanh, scale=0.5).then_inc(as_.step("tanh", 0), 1)
            for t in range(NT):
                act.wait_ge(vs.sem, vs.after("mv", t))
                act.activation(rstd[:, t:t + 1], mv[:, t, 1:2], ACT.Sqrt, bias=col(E_LN)).then_inc(as_.step("sqrt", t), 1)
            for m in range(4):
                act.wait_ge(used, m + 1)
                act.activation(mrow0[:, m, :], bank[m][0:2, :], ACT.Copy).then_inc(as_.step("row", m), 1)
            for k in range(KD):
                act.wait_ge(ps.sem, ps.after("xt", k))
                act.wait_ge(vs.sem, vs.after("scale1", 0))
                act.activation(hT[:, k, 0:P], bank[4 + k % 2][:, 0:P], ACT.Identity, scale=modc[:, 8 + k, 0:1],
                               bias=modc[:, k, 0:1]).then_inc(as_.step("hc", k), 1)

        @block.vector
        def _(dve):
            dve.wait_ge(got_cst, 64)
            dve.wait_ge(as_.sem, as_.after("tanh", 0))
            dve.scalar_tensor_tensor(cond[:], cond_t[:], 1.0, cond[:], ALU.add, ALU.mult).then_inc(vs.step("cond", 0), 1)
            for t in range(NT):
                dve.wait_ge(got_x[t], 16)
                if t:
                    dve.wait_ge(gs.sem, gs.after("pos", t))
                for i in range(2):
                    dve.bn_stats(stats[:, t, i, :], x_sb[:, t, 512 * i:512 * i + 512]).then_inc(vs.step(f"stat{i}", t), 1)
                dve.wait_ge(vs.sem, vs.after("stat1", t))
                dve.bn_aggr(mv[:, t, :], stats[:, t, :, :]).then_inc(vs.step("mv", t), 1)
            for t in range(NT):
                dve.wait_ge(as_.sem, as_.after("sqrt", t))
                dve.reciprocal(rstd[:, t:t + 1], rstd[:, t:t + 1]).then_inc(vs.step("rec", t), 1)
                dve.wait_ge(vs.sem, vs.after("rec", t))
                dve.tensor_scalar(x_sb[:, t, :], x_sb[:, t, :], mv[:, t, 0:1], rstd[:, t:t + 1], ALU.subtract,
                                  ALU.mult).then_inc(vs.step("xn", t), 1)
            dve.wait_ge(ps.sem, ps.after("columns", 3))
            dve.scalar_tensor_tensor(modc[:, 0:16, :], bank[7][:, 0:32].rearrange("p (m c) -> p m c", c=2), 0.5,
                                     bc(vec[:, V_BMOD:V_BMOD + 16].unsqueeze(2), P, 16, 2),
                                     ALU.mult, ALU.add).then_inc(vs.step("modc", 0), 1)
            dve.wait_ge(vs.sem, vs.after("modc", 0))
            dve.tensor_scalar(modc[:, 8:16, :], modc[:, 8:16, :], 1.0, None, ALU.add).then_inc(vs.step("scale1", 0), 1)
            dve.wait_ge(vs.sem, vs.after("scale1", 0))
            for k in range(KD):
                dve.wait_ge(ps.sem, ps.after("xt", k))
                dve.tensor_scalar(hT[:, k, P:T], bank[k % 2][:, :], modc[:, 8 + k, 1:2], modc[:, k, 1:2], ALU.mult,
                                  ALU.add).then_inc(vs.step("h", k), 1)

        @block.tensor
        def _(pe):
            pe.wait_ge(vs.sem, vs.after("cond", 0))
            for m in range(4):
                block_ready(pe, m)
                mod_rows(pe, m, bank[m][0:2, :]).then_inc(used, 1)
                if m:
                    pe.wait_ge(as_.sem, as_.after("row", m - 1))
                    mod_columns(pe, bank[7][:, 8 * m - 8:8 * m], mrow0[:, m - 1, :]).then_inc(ps.step("columns", m - 1), 1)
            pe.wait_ge(as_.sem, as_.after("row", 3))
            mod_columns(pe, bank[7][:, 24:32], mrow0[:, 3, :]).then_inc(ps.step("columns", 3), 1)
            pe.wait_ge(vs.sem, vs.after("xn", NT - 1))
            for k in range(KD):
                if k >= 2:
                    pe.wait_ge(vs.sem, vs.after("h", k - 2))
                    pe.wait_ge(as_.sem, as_.after("hc", k - 2))
                for t in range(1, NT):
                    pe.transpose(bank[k % 2][:, (t - 1) * P:t * P], x_sb[:, t, k * P:k * P + P], ident)
                mm = pe.transpose(bank[4 + k % 2][:, 0:P], x_sb[:, 0, k * P:k * P + P], ident)
                mm.then_inc(ps.step("xt", k), 1)


    cursor[0] = base0
    qkv = sb("qkv", [P, 12, CW])
    stage1_keep = cursor[0]
    xc = sb("xc", [P, 4, CW])
    rawc = sb("rawc", [P, 2, RAW])
    yc_half = sb("yc_half", [P, 2, CW])
    tch = sb("tch", [P, 2, CW])
    w_small = sb("w_small", [P, KD, 32])
    tr = sb("tr", [P, T])
    tg = sb("tg", [P, T])
    A4 = sb("A4", [P, 4, T])
    Q4 = sb("Q4", [P, 4, T])
    G4 = sb("G4", [P, 4, T])
    HF = yC
    spx = sb("spx", [P, 88])
    spn = sb("spn", [P, 88])
    ea = sb("ea", [P, 8])
    bah = sb("bah", [P, 16])
    cah = sb("cah", [P, 48])
    hn = sb("hn", [P, 2, 8])
    nlru = sb("nlru", [P, 8])
    mrow = sb("mrow", [2, 512])
    C1 = 24
    CONV = [c for c in range(C1) if c // 4 in (0, 2, 3, 4)]
    kth = {c: i for i, c in enumerate(CONV)}
    w_lru = sb("w_lru", [P, 2, 2, 4, P])
    got_lru = nc.alloc_semaphore("got_w_lru")
    got_ws = nc.alloc_semaphore("got_w_small")

    def dve_chunk(c):
        out = [("ctx", c)]
        if c in kth:
            out += [("conv", c, j) for j in range(4)]
        return out

    def dve_unit(u):
        return [(k, u) for k in ("gx0", "gx1", "q")]

    def dve_dir(d):
        out = [("b", d)] + [("scan", d, b, i) for b in range(4) for i in range(2)] + [("state", d)]
        return out + ([("sum", 0)] if d else [])

    lab_v = [("pad", 0), ("prep", 0), ("prep", 1), ("prep", 2), ("sm", 0), ("sm", 1), ("sm", 2), ("sm", 3), ("sm", 4), ("sm", 5)]
    lab_v += [("sm", i) for i in range(6, 12)]
    for c in range(C1):
        if c in (12, 16):
            lab_v += dve_dir(0 if c == 12 else 1)
        if c % 4 == 0:
            lab_v += [("row", 4 + c // 4)]
        lab_v += dve_chunk(c)
        if c % 4 == 0:
            lab_v += [("column", 4 + c // 4)]
        if 8 <= c < 16:
            lab_v += dve_unit(c - 8)
        if c in kth and c >= 8:
            lab_v += [("silu", c)]
    lab_v += [(x, m) for m in (10, 11) for x in ("row", "column")] + [("y", 0), ("y", 1), ("scale2", 0)]
    lab_a = [("ea", 0), ("sm", 0), ("sm", 1), ("sm", 2)]
    for c in range(C1):
        if c in (12, 16):
            lab_a += [("sqrt", c // 16)]
        if 8 <= c < 16:
            lab_a += [(k, c - 8) for k in ("tr0", "tr1", "tg0", "tg1")]
        lab_a += [("evac", c)]
        if 8 <= c < 16:
            lab_a += [(k, c - 8) for k in ("a", "th")]
        lab_a += [("tanh", c)] if c in kth and c >= 8 else []
    lab_a += [("gelu", 0)]
    lab_p = [("small", 0)]
    for c in range(C1):
        lab_p += [("chunk", c)] + ([("columns", 4 + c // 4)] if c % 4 == 0 else [])
        if 7 <= c < 15:
            lab_p += [("lru", c - 7)]
    lab_p += [("columns", 10), ("columns", 11)]
    v1 = Steps(nc, "proj1_vector", lab_v)
    a1 = Steps(nc, "proj1_scalar", lab_a)
    p1 = Steps(nc, "proj1_tensor", lab_p)
    g1 = Steps(nc, "proj1_gpsimd", [("g", i) for i in range(3)])
    first_in = {n: i for i, (kind, n) in enumerate(BLOCKS) if kind == "in"}

    with nc.Block("proj1", no_gpsimd_drain=True) as block:
        @block.sync
        def _(sp):
            sp.dma_start(w_small[:], A["w_small"]).then_inc(got_ws, 16)
            for n in range(4, 18):
                kind, m = BLOCKS[n]
                last = (used, m + 1) if kind == "mod" else (p1.sem, p1.after("chunk", 4 * m + 3))
                load_block(sp, n + RING, *last)
            sp.wait_ge(got_lev, 16)
            sp.wait_ge(v1.sem, v1.after("state", 1))
            store(sp, O["lru"], nlru[:])
            sp.wait_ge(stored, stores[0])

        @block.tensor
        def _(pe):
            pe.wait_ge(got_ws, 16)
            for t in range(NT):
                for k in range(KD):
                    mm = pe.matmul(bank[6][:, 32 * t:32 * t + 32], hT[:, k, tok(t)], w_small[:, k, :],
                                   start=(k == 0), stop=(k == KD - 1))
            mm.then_inc(p1.step("small", 0), 1)
            for n in range(4, 18):
                kind, m = BLOCKS[n]
                if kind == "mod":
                    block_ready(pe, n)
                    if m > 4:
                        pe.wait_ge(v1.sem, v1.after("column", m - 1))
                    mod_rows(pe, n, bank[7][0:2, :]).then_inc(used, 1)
                    if m >= 10:
                        pe.wait_ge(v1.sem, v1.after("row", m))
                        mod_columns(pe, bank[7][:, 0:8], mrow[:]).then_inc(p1.step("columns", m), 1)
                    continue
                block_ready(pe, n)
                for j in range(4):
                    c = 4 * m + j
                    if c >= 2:
                        pe.wait_ge(a1.sem, a1.after("evac", c - 2))
                        pe.wait_ge(v1.sem, v1.after("ctx", c - 2))
                    lat, ctx = bank[2 * (c % 2)], bank[2 * (c % 2) + 1]
                    for k in range(KD):
                        w = ring[:, n % RING, 512 * k + P * j:512 * k + P * j + P]
                        pe.matmul(lat[:, :], w, hT[:, k, P:T], start=(k == 0), stop=(k == KD - 1))
                        mm = pe.matmul(ctx[:, 0:P], w, hT[:, k, 0:P], start=(k == 0), stop=(k == KD - 1))
                    mm.then_inc(p1.step("chunk", c), 1)
                    if j == 0:
                        pe.wait_ge(v1.sem, v1.after("row", 4 + m))
                        mod_columns(pe, bank[7][:, 0:8], mrow[:]).then_inc(p1.step("columns", 4 + m), 1)
                    if 7 <= c < 15:
                        u = c - 7
                        d, b = u // 4, u % 4
                        if u == 0:
                            pe.wait_ge(v1.sem, v1.after("conv", 3, 3))
                            pe.wait_ge(v1.sem, v1.after("sm", 0))
                            pe.wait_ge(got_lru, 16)
                        else:
                            pe.wait_ge(a1.sem, a1.after("tg1", u - 1))
                        for g in range(2):
                            w = w_lru[:, g, d, b, :]
                            pe.matmul(bank[4 + g][:, :], w, xc[:, b, LAT:CW], start=True, stop=True)
                            mm = pe.matmul(bank[6][:, P * g:P * g + P], w, xc[:, b, 0:P], start=True, stop=True)
                        mm.then_inc(p1.step("lru", u), 1)

        @block.scalar
        def _(act):
            act.dma_start(w_lru[:], A["w_lru"]).then_inc(got_lru, 16)
            act.activation(ea[:], row[:, R_ALOG:R_ALOG + 8], ACT.Exp).then_inc(a1.step("ea", 0), 1)
            act.wait_ge(v1.sem, v1.after("sm", 5))
            act.activation(spn[:], spn[:], ACT.Exp).then_inc(a1.step("sm", 0), 1)
            act.activation(smg[:, :, 0:8], smg[:, :, 0:8], ACT.Tanh, scale=0.5).then_inc(a1.step("sm", 1), 1)
            act.wait_ge(a1.sem, a1.after("sm", 0))
            act.activation(spn[:], spn[:], ACT.Ln, bias=col(E_ONE)).then_inc(a1.step("sm", 2), 1)
            for c in range(C1):
                if c in (12, 16):
                    act.wait_ge(a1.sem, a1.after("th", c - 9))
                    act.activation(Q4[:], Q4[:], ACT.Sqrt, scale=0.25).then_inc(a1.step("sqrt", c // 16), 1)
                if 8 <= c < 16:
                    u = c - 8
                    act.wait_ge(p1.sem, p1.after("lru", u))
                    if u == 0:
                        act.wait_ge(v1.sem, v1.after("sm", 11))
                    else:
                        act.wait_ge(v1.sem, v1.after("gx1", u - 1))
                        act.wait_ge(a1.sem, a1.after("th", u - 1))
                    for t_, g, n_ in ((tr, 0, "tr"), (tg, 1, "tg")):
                        act.activation(t_[:, P:T], bank[4 + g][:, :], ACT.Tanh, scale=0.5,
                                       bias=bah[:, 8 * g + u:8 * g + u + 1]).then_inc(a1.step(n_ + "0", u), 1)
                        act.activation(t_[:, 0:P], bank[6][:, P * g:P * g + P], ACT.Tanh, scale=0.5,
                                       bias=bah[:, 8 * g + u:8 * g + u + 1]).then_inc(a1.step(n_ + "1", u), 1)
                act.wait_ge(p1.sem, p1.after("chunk", c))
                lat = bank[2 * (c % 2)]
                if c in kth:
                    i = kth[c]
                    if i >= 2:
                        act.wait_ge(v1.sem, v1.after("conv", CONV[i - 2], 3))
                    else:
                        act.wait_ge(v1.sem, v1.after("pad", 0))
                    dst = rawc[:, i % 2, 1 + LAT:1 + CW]
                else:
                    dst = (yB if c < 8 else yA)[:, c % 4, P:T]
                act.activation(dst, lat[:, :], ACT.Copy).then_inc(a1.step("evac", c), 1)
                if 8 <= c < 16:
                    if u >= 4:
                        act.wait_ge(v1.sem, v1.after("scan", 0, u - 4, 1))
                    act.wait_ge(a1.sem, a1.after("tr1", u))
                    act.activation(A4[:, u % 4, :], tr[:], ACT.Exp, scale=hn[:, 1, u:u + 1],
                                   bias=hn[:, 1, u:u + 1]).then_inc(a1.step("a", u), 1)
                    act.activation(Q4[:, u % 4, :], tr[:], ACT.Tanh, scale=hn[:, 0, u:u + 1],
                                   bias=hn[:, 0, u:u + 1]).then_inc(a1.step("th", u), 1)
                if c in kth and c >= 8:
                    act.wait_ge(v1.sem, v1.after("conv", c, 3))
                    if kth[c] >= 6:
                        act.wait_ge(v1.sem, v1.after("silu", CONV[kth[c] - 2]))
                    act.activation(tch[:, kth[c] % 2, :], yc_half[:, kth[c] % 2, :], ACT.Tanh).then_inc(a1.step("tanh", c), 1)
            act.wait_ge(g1.sem, g1.after("g", 2))
            act.activation(G4[:], G4[:], ACT.Tanh, scale=math.sqrt(2.0 / math.pi)).then_inc(a1.step("gelu", 0), 1)

        @block.gpsimd
        def _(pool):
            pool.wait_ge(a1.sem, a1.after("evac", 7))
            pool.wait_ge(v1.sem, v1.after("ctx", 7))
            pool.wait_ge(v1.sem, v1.after("scan", 1, 3, 1))
            pool.tensor_tensor(G4[:], yB[:], yB[:], ALU.mult).then_inc(g1.step("g", 0), 1)
            pool.wait_ge(g1.sem, g1.after("g", 0))
            pool.tensor_scalar(G4[:], G4[:], 0.044715, 1.0, ALU.mult, ALU.add).then_inc(g1.step("g", 1), 1)
            pool.wait_ge(g1.sem, g1.after("g", 1))
            pool.tensor_tensor(G4[:], G4[:], yB[:], ALU.mult).then_inc(g1.step("g", 2), 1)

        @block.vector
        def _(dve):
            dve.memset(rawc[:], 0.0).then_inc(v1.step("pad", 0), 1)
            dve.tensor_scalar(cah[:], vec[:, V_CONVA:V_CONVA + 48], 0.5, None, ALU.mult).then_inc(v1.step("prep", 0), 1)
            dve.tensor_scalar(bah[:], vec[:, V_BA:V_BA + 16], 0.5, None, ALU.mult).then_inc(v1.step("prep", 1), 1)
            dve.tensor_scalar(spx[:, 80:88], vec[:, V_LAM:V_LAM + 8], -1.0, None, ALU.mult).then_inc(v1.step("prep", 2), 1)
            dve.wait_ge(p1.sem, p1.after("small", 0))
            dve.tensor_copy(smg[:], bank[6][:, 0:160].rearrange("p (t s) -> p t s", s=32)).then_inc(v1.step("sm", 0), 1)
            dve.wait_ge(v1.sem, v1.after("sm", 0))
            dve.tensor_tensor(spx[:, 0:40].rearrange("p (t s) -> p t s", s=8), smg[:, :, 8:16],
                              bc(row[:, R_DT:R_DT + 8].unsqueeze(1), P, NT, 8), ALU.add).then_inc(v1.step("sm", 1), 1)
            dve.tensor_tensor(spx[:, 40:80].rearrange("p (t s) -> p t s", s=8), smg[:, :, 24:32],
                              bc(row[:, R_BF:R_BF + 8].unsqueeze(1), P, NT, 8), ALU.add).then_inc(v1.step("sm", 2), 1)
            dve.tensor_tensor(smg[:, :, 16:24], smg[:, :, 16:24],
                              bc(row[:, R_BI:R_BI + 8].unsqueeze(1), P, NT, 8), ALU.add).then_inc(v1.step("sm", 3), 1)
            dve.wait_ge(v1.sem, v1.after("sm", 2))
            dve.tensor_scalar(spx[:, 40:80], spx[:, 40:80], -1.0, None, ALU.mult).then_inc(v1.step("sm", 4), 1)
            dve.wait_ge(v1.sem, v1.after("sm", 4))
            dve.scalar_tensor_tensor(spn[:], spx[:], -1.0, spx[:], ALU.mult, ALU.min).then_inc(v1.step("sm", 5), 1)
            dve.wait_ge(a1.sem, a1.after("sm", 2))
            dve.scalar_tensor_tensor(spx[:], spx[:], 0.0, spn[:], ALU.max, ALU.add).then_inc(v1.step("sm", 6), 1)
            dve.wait_ge(v1.sem, v1.after("sm", 6))
            dve.scalar_tensor_tensor(smg[:, :, 8:16], spx[:, 0:40].rearrange("p (t s) -> p t s", s=8), -1.0,
                                     bc(ea[:].unsqueeze(1), P, NT, 8), ALU.mult, ALU.mult).then_inc(v1.step("sm", 7), 1)
            dve.tensor_scalar(smg[:, :, 24:32], spx[:, 40:80].rearrange("p (t s) -> p t s", s=8), -1.0, None,
                              ALU.mult).then_inc(v1.step("sm", 8), 1)
            dve.tensor_scalar(hn[:, 0, :], spx[:, 80:88], 2.0, None, ALU.mult).then_inc(v1.step("sm", 9), 1)
            dve.tensor_scalar(hn[:, 1, :], spx[:, 80:88], -4.0, None, ALU.mult).then_inc(v1.step("sm", 10), 1)
            dve.tensor_scalar(smg[:, :, 0:8], smg[:, :, 0:8], 0.5, 0.5, ALU.mult, ALU.add).then_inc(v1.step("sm", 11), 1)

            def chunk(c):
                dve.wait_ge(p1.sem, p1.after("chunk", c))
                ctx = bank[2 * (c % 2) + 1]
                if c not in kth:
                    dve.tensor_copy((yB if c < 8 else yA)[:, c % 4, 0:P], ctx[:, 0:P]).then_inc(v1.step("ctx", c), 1)
                    return
                i = kth[c]
                s_ = i % 2
                dve.tensor_copy(rawc[:, s_, 1:1 + P], ctx[:, 0:P]).then_inc(v1.step("ctx", c), 1)
                dve.wait_ge(v1.sem, v1.after("ctx", c))
                dve.wait_ge(a1.sem, a1.after("evac", c))
                if c < 4:
                    dst = xc[:, c, :]
                    w = [vec[:, V_CONVB + 4 * j + c:V_CONVB + 4 * j + c + 1] for j in range(4)]
                    dve.tensor_scalar(dst, rawc[:, s_, 0:CW], w[0], vec[:, V_CONVBB + c:V_CONVBB + c + 1], ALU.mult,
                                      ALU.add).then_inc(v1.step("conv", c, 0), 1)
                else:
                    dst = yc_half[:, s_, :]
                    w = [cah[:, 12 * j + c - 8:12 * j + c - 7] for j in range(4)]
                    if i >= 6:
                        dve.wait_ge(a1.sem, a1.after("tanh", CONV[i - 2]))
                    dve.tensor_scalar(dst, rawc[:, s_, 0:CW], w[0], None, ALU.mult).then_inc(v1.step("conv", c, 0), 1)
                for j in range(1, 4):
                    dve.wait_ge(v1.sem, v1.after("conv", c, j - 1))
                    dve.scalar_tensor_tensor(dst, rawc[:, s_, j:j + CW], w[j], dst, ALU.mult,
                                             ALU.add).then_inc(v1.step("conv", c, j), 1)

            def silu(c):
                s_ = kth[c] % 2
                dve.wait_ge(a1.sem, a1.after("tanh", c))
                dve.scalar_tensor_tensor(qkv[:, c - 8, :], tch[:, s_, :], 1.0, yc_half[:, s_, :], ALU.add,
                                         ALU.mult).then_inc(v1.step("silu", c), 1)

            def unit(u):
                b = u % 4
                dve.wait_ge(a1.sem, a1.after("tg1", u))
                dve.scalar_tensor_tensor(G4[:, b, 0:P], tg[:, 0:P], 1.0, xc[:, b, 0:P], ALU.add,
                                         ALU.mult).then_inc(v1.step("gx0", u), 1)
                dve.scalar_tensor_tensor(G4[:, b, P:T], tg[:, P:T], 1.0, xc[:, b, LAT:CW], ALU.add,
                                         ALU.mult).then_inc(v1.step("gx1", u), 1)
                dve.wait_ge(v1.sem, v1.after("gx1", u))
                dve.wait_ge(a1.sem, a1.after("a", u))
                dve.scalar_tensor_tensor(G4[:, b, :], A4[:, b, :], 1.0, G4[:, b, :], ALU.add, ALU.mult).then_inc(v1.step("q", u), 1)

            def direction(d):
                dve.wait_ge(a1.sem, a1.after("sqrt", d))
                dve.wait_ge(v1.sem, v1.after("q", 4 * d + 3))
                dve.tensor_tensor(G4[:], G4[:], Q4[:], ALU.mult).then_inc(v1.step("b", d), 1)
                dve.wait_ge(v1.sem, v1.after("b", d))
                dve.wait_ge(a1.sem, a1.after("a", 4 * d + 3))
                out = Q4 if d else HF
                for b in range(4):
                    h0 = vec[:, V_SLRU + 4 * d + b:V_SLRU + 4 * d + b + 1]
                    for i, (lo, hi, init) in enumerate(((0, P, 0.0), (P, T, h0))):
                        sl = slice(lo, hi) if d == 0 else slice(hi - 1, lo - 1 if lo else None, -1)
                        dve.tensor_tensor_scan(out[:, b, sl], A4[:, b, sl], G4[:, b, sl], init, ALU.mult,
                                               ALU.add).then_inc(v1.step("scan", d, b, i), 1)
                dve.wait_ge(v1.sem, v1.after("scan", d, 3, 1))
                dve.tensor_copy(nlru[:, 4 * d:4 * d + 4], out[:, :, 0 if d else P - 1]).then_inc(v1.step("state", d), 1)
                if d:
                    dve.tensor_tensor(HF[:], HF[:], Q4[:], ALU.add).then_inc(v1.step("sum", 0), 1)

            def mod_row(m):
                dve.wait_ge(used, m + 1)
                if m > 4:
                    dve.wait_ge(p1.sem, p1.after("columns", m - 1))
                dve.tensor_copy(mrow[:], bank[7][0:2, :]).then_inc(v1.step("row", m), 1)

            def mod_column(m):
                dve.wait_ge(p1.sem, p1.after("columns", m))
                dve.scalar_tensor_tensor(modc[:, 4 * m:4 * m + 4, :], bank[7][:, 0:8].rearrange("p (m c) -> p m c", c=2), 0.5,
                                         bc(vec[:, V_BMOD + 4 * m:V_BMOD + 4 * m + 4].unsqueeze(2), P, 4, 2),
                                         ALU.mult, ALU.add).then_inc(v1.step("column", m), 1)

            for c in range(C1):
                if c in (12, 16):
                    direction(0 if c == 12 else 1)
                if c % 4 == 0:
                    mod_row(4 + c // 4)
                chunk(c)
                if c % 4 == 0:
                    mod_column(4 + c // 4)
                if 8 <= c < 16:
                    unit(c - 8)
                if c in kth and c >= 8:
                    silu(c)
            for m in (10, 11):
                mod_row(m)
                mod_column(m)
            dve.wait_ge(a1.sem, a1.after("gelu", 0))
            dve.scalar_tensor_tensor(G4[:], G4[:], 1.0, yB[:], ALU.add, ALU.mult).then_inc(v1.step("y", 0), 1)
            dve.wait_ge(v1.sem, v1.after("y", 0))
            dve.scalar_tensor_tensor(yB[:], G4[:], 0.5, HF[:], ALU.mult, ALU.mult).then_inc(v1.step("y", 1), 1)
            dve.wait_ge(v1.sem, v1.after("column", 9))
            dve.tensor_scalar(modc[:, 32:40, :], modc[:, 32:40, :], 1.0, None, ALU.add).then_inc(v1.step("scale2", 0), 1)
    if stop <= 1:
        return dict(locals())

    cursor[0] = stage1_keep
    k_tm = sb("k_tm", [P, NT, H * HD])
    v_tm = sb("v_tm", [P, NT, H * HD])
    stage2_keep = cursor[0]
    sq = sb("sq", [P, 2, CW])
    rs = sb("rs", [P, 8, CW])
    HC = CW // 2
    v2 = Steps(nc, "delta_prep_vector", [("norm", i) for i in range(8)] + [("k", t) for t in range(NT)])
    a2 = Steps(nc, "delta_prep_scalar", [("v", t) for t in range(2)] + [("ln", i, j) for i in range(8) for j in range(2)] + [("rsqrt", i) for i in range(8)]
               + [("v", t) for t in range(2, NT)])
    p2 = Steps(nc, "delta_prep_tensor", [("v", 0), ("v", 1)] + [("sum", i) for i in range(8)] + [("v", t) for t in range(2, NT)]
               + [("k", t) for t in range(NT)])
    g2 = Steps(nc, "delta_prep_gpsimd", [("sq", i) for i in range(8)])
    with nc.Block("delta_prep", no_gpsimd_drain=True) as block:
        @block.gpsimd
        def _(pool):
            for i in range(8):
                if i >= 2:
                    pool.wait_ge(p2.sem, p2.after("sum", i - 2))
                pool.tensor_tensor(sq[:, i % 2, :], qkv[:, i, :], qkv[:, i, :], ALU.mult).then_inc(g2.step("sq", i), 1)

        @block.tensor
        def _(pe):
            def v_tile(t):
                if t >= 2:
                    pe.wait_ge(a2.sem, a2.after("v", t - 2))
                for h in range(H):
                    mm = pe.transpose(bank[4 + t % 2][:, P * h:P * h + P], qkv[:, 8 + h, ctok(t)], ident)
                mm.then_inc(p2.step("v", t), 1)

            v_tile(0)
            v_tile(1)
            for i in range(8):
                pe.wait_ge(g2.sem, g2.after("sq", i))
                if i >= 2:
                    pe.wait_ge(a2.sem, a2.after("ln", i - 2, 1))
                for j in range(2):
                    mm = pe.matmul(bank[2 * (i % 2) + j][:, 0:HC], ones, sq[:, i % 2, HC * j:HC * j + HC], start=True, stop=True)
                mm.then_inc(p2.step("sum", i), 1)
            for t in range(2, NT):
                v_tile(t)
            pe.wait_ge(v2.sem, v2.after("norm", 7))
            for t in range(NT):
                if t >= 2:
                    pe.wait_ge(v2.sem, v2.after("k", t - 2))
                for h in range(H):
                    mm = pe.transpose(bank[6 + t % 2][:, P * h:P * h + P], qkv[:, 4 + h, ctok(t)], ident)
                mm.then_inc(p2.step("k", t), 1)

        @block.scalar
        def _(act):
            def v_tile(t):
                act.wait_ge(p2.sem, p2.after("v", t))
                act.activation(v_tm[:, t, :], bank[4 + t % 2][:, :], ACT.Copy).then_inc(a2.step("v", t), 1)

            v_tile(0)
            v_tile(1)
            for i in range(8):
                act.wait_ge(p2.sem, p2.after("sum", i))
                for j in range(2):
                    act.activation(rs[:, i, HC * j:HC * j + HC], bank[2 * (i % 2) + j][:, 0:HC], ACT.Ln, scale=128.0 if i < 4 else 1.0,
                                   bias=col(E_RMS128 if i < 4 else E_RMS)).then_inc(a2.step("ln", i, j), 1)
            for i in range(8):
                act.wait_ge(a2.sem, a2.after("ln", i, 1))
                act.activation(rs[:, i, :], rs[:, i, :], ACT.Exp, scale=-0.5).then_inc(a2.step("rsqrt", i), 1)
            for t in range(2, NT):
                v_tile(t)

        @block.vector
        def _(dve):
            for i in range(8):
                dve.wait_ge(a2.sem, a2.after("rsqrt", i))
                dve.tensor_tensor(qkv[:, i, :], qkv[:, i, :], rs[:, i, :], ALU.mult).then_inc(v2.step("norm", i), 1)
            for t in range(NT):
                dve.wait_ge(p2.sem, p2.after("k", t))
                dve.tensor_copy(k_tm[:, t, :], bank[6 + t % 2][:, :]).then_inc(v2.step("k", t), 1)

    cursor[0] = stage2_keep + 64
    o_f = yC
    o_b = sb("o_b", [P, H, T])

    def two(name, w=H * HD):
        return [sb(f"{name}{d}", [P, w]) for d in range(2)]

    n_, w_, f_, qk_, qd_, kd_, vb_, d_, dt_, s_ = (two(x) for x in ("dl_n", "dl_w", "dl_f", "dl_qk", "dl_qd", "dl_kd",
                                                                    "dl_vb", "dl_d", "dl_dt", "dl_s"))
    gc = two("dl_gc", 12)
    eg = two("dl_eg", 12)
    nb = two("dl_nb", 8)
    got_s = nc.alloc_semaphore("got_delta_state")

    def tile_of(g, d):
        return g if d == 0 or g == 0 else NT - g

    def both(*names):
        return [(x, g, d) for g in range(NT) for x in names for d in range(2)]

    inv = range(1, LEVELS)
    lv3 = both("gtri", "gc", "kd", "nb", "t1", "n0", "nbe", "n1", "qk", "p0", "p1", *[("x", l) for l in inv],
               "w0", "w1", "o", "s0", "s1")
    la3 = both("eg", "egb", "dec", "qdec", *[(x, l) for l in inv for x in ("f", "d") if (x, l) != ("d", LEVELS - 1)], "u")
    lp3 = both("gcol", "gb", "kk", "nt", *[(x, l) for l in inv for x in ("f", "x", "d") if (x, l) != ("d", LEVELS - 1)],
               "ks", "u", "o")
    lg3 = both("init", "m1", "m2", "kd", "vb", "qd")
    v3, a3 = Steps(nc, "delta_vector", [("z", 0), ("z", 1)] + lv3), Steps(nc, "delta_scalar", la3)
    p3, g3 = Steps(nc, "delta_tensor", lp3), Steps(nc, "delta_gpsimd", lg3)
    with nc.Block("delta", no_gpsimd_drain=True) as block:
        @block.sync
        def _(sp):
            for d in range(2):
                sp.wait_ge(v3.sem, v3.after("s1", 0, d))
                store(sp, O["delta"][d], s_[d][:])
            sp.wait_ge(stored, stores[0])
            for d in range(2):
                sp.dma_start(s_[d][:], A["s_delta"][d]).then_inc(got_s, 16)
            sp.wait_ge(got_s, 32)

        @block.tensor
        def _(pe):
            def kt(g, d, h):
                return qkv[:, 4 + h, ctok(tile_of(g, d))]

            def hd(t, h):
                return t[:, P * h:P * h + P]

            for g in range(NT):
                for d in range(2):
                    if g:
                        pe.wait_ge(v3.sem, v3.after("w0", g - 1, d))
                    t = tile_of(g, d)
                    g4 = smg[:, t, 8 + 4 * d:12 + 4 * d]
                    pe.matmul(bank[4 * d][:, 0:4], tri[d], g4, start=True, stop=True)
                    pe.matmul(bank[4 * d][:, 4:8], ones, g4, start=True, stop=True).then_inc(p3.step("gcol", g, d), 1)
                for d in range(2):
                    pe.wait_ge(v3.sem, v3.after("gtri", g, d))
                    if g:
                        pe.wait_ge(a3.sem, a3.after("u", g - 1, d))
                    pe.matmul(bank[4 * d + 1][:, :], ones, n_[d][:], start=True, stop=True).then_inc(p3.step("gb", g, d), 1)
                for d in range(2):
                    if g:
                        pe.wait_ge(v3.sem, v3.after("o", g - 1, d))
                        pe.wait_ge(v3.sem, v3.after("s1", g - 1, d))
                    for h in range(H):
                        pe.matmul(hd(bank[4 * d + 2], h), kt(g, d, h), kt(g, d, h), start=True, stop=True)
                    for h in range(H):
                        mm = pe.matmul(hd(bank[4 * d + 3], h), kt(g, d, h), qkv[:, h, ctok(tile_of(g, d))], start=True, stop=True)
                    mm.then_inc(p3.step("kk", g, d), 1)
                for d in range(2):
                    pe.wait_ge(v3.sem, v3.after("n1", g, d))
                    pe.wait_ge(v3.sem, v3.after("gc", g, d))
                    for h in range(H):
                        mm = pe.transpose(hd(bank[4 * d], h), hd(n_[d], h), ident)
                    mm.then_inc(p3.step("nt", g, d), 1)
                for l in inv:
                    for d in range(2):
                        if l == 1:
                            pe.wait_ge(v3.sem, v3.after("p1", g, d))
                            pe.wait_ge(a3.sem, a3.after("egb", g, d))
                        else:
                            pe.wait_ge(v3.sem, v3.after(("x", l - 1), g, d))
                        for h in range(H):
                            mm = pe.matmul(hd(bank[4 * d + 1], h), hd(n_[d], h), hd(dt_[d], h), start=True, stop=True)
                        mm.then_inc(p3.step(("f", l), g, d), 1)
                    for d in range(2):
                        pe.wait_ge(a3.sem, a3.after(("f", l), g, d))
                        if l > 1:
                            pe.wait_ge(a3.sem, a3.after(("d", l - 1), g, d))
                        for h in range(H):
                            mm = pe.matmul(hd(bank[4 * d + 2], h), hd(d_[d], h), hd(f_[d], h), start=True, stop=True)
                        mm.then_inc(p3.step(("x", l), g, d), 1)
                    if l < LEVELS - 1:
                        for d in range(2):
                            pe.wait_ge(v3.sem, v3.after(("x", l), g, d))
                            if l == 1:
                                pe.wait_ge(v3.sem, v3.after("qk", g, d))
                            for h in range(H):
                                mm = pe.transpose(hd(bank[4 * d + 3], h), hd(dt_[d], h), ident)
                            mm.then_inc(p3.step(("d", l), g, d), 1)
                for d in range(2):
                    if g == 0:
                        pe.wait_ge(v3.sem, v3.after("z", d))
                    elif g == 1:
                        pe.wait_ge(got_s, 32)
                    for h in range(H):
                        mm = pe.matmul(hd(bank[4 * d], h), kt(g, d, h), hd(s_[d], h), start=True, stop=True)
                    mm.then_inc(p3.step("ks", g, d), 1)
                for d in range(2):
                    pe.wait_ge(v3.sem, v3.after("w1", g, d))
                    for h in range(H):
                        mm = pe.matmul(hd(bank[4 * d + 1], h), hd(dt_[d], h), hd(w_[d], h), start=True, stop=True)
                    mm.then_inc(p3.step("u", g, d), 1)
                for d in range(2):
                    pe.wait_ge(a3.sem, a3.after("u", g, d))
                    pe.wait_ge(g3.sem, g3.after("qd", g, d))
                    for h in range(H):
                        pe.matmul(hd(bank[4 * d + 2], h), hd(s_[d], h), hd(qd_[d], h), start=True, stop=False)
                        pe.matmul(hd(bank[4 * d + 2], h), hd(d_[d], h), hd(qk_[d], h), start=False, stop=True)
                    for h in range(H):
                        mm = pe.matmul(hd(bank[4 * d + 3], h), hd(kd_[d], h), hd(d_[d], h), start=True, stop=True)
                    mm.then_inc(p3.step("o", g, d), 1)

        @block.scalar
        def _(act):
            for g in range(NT):
                for d in range(2):
                    act.wait_ge(v3.sem, v3.after("kd", g, d))
                    if g:
                        act.wait_ge(v3.sem, v3.after("s0", g - 1, d))
                    act.activation(eg[d][:], gc[d][:], ACT.Exp).then_inc(a3.step("eg", g, d), 1)
                for d in range(2):
                    act.wait_ge(p3.sem, p3.after("gb", g, d))
                    act.wait_ge(v3.sem, v3.after("t1", g, d))
                    if g:
                        act.wait_ge(p3.sem, p3.after("o", g - 1, d))
                    act.activation(qd_[d][:], bank[4 * d + 1][:, :], ACT.Exp).then_inc(a3.step("egb", g, d), 1)
                for d in range(2):
                    act.wait_ge(g3.sem, g3.after("m1", g, d))
                    act.activation(f_[d][:], f_[d][:], ACT.Exp).then_inc(a3.step("dec", g, d), 1)
                for d in range(2):
                    act.wait_ge(g3.sem, g3.after("m2", g, d))
                    act.activation(qk_[d][:], qk_[d][:], ACT.Exp).then_inc(a3.step("qdec", g, d), 1)
                for l in inv:
                    for d in range(2):
                        act.wait_ge(p3.sem, p3.after(("f", l), g, d))
                        act.activation(f_[d][:], bank[4 * d + 1][:, :], ACT.Copy).then_inc(a3.step(("f", l), g, d), 1)
                    if l < LEVELS - 1:
                        for d in range(2):
                            act.wait_ge(p3.sem, p3.after(("d", l), g, d))
                            act.activation(d_[d][:], bank[4 * d + 3][:, :], ACT.Copy).then_inc(a3.step(("d", l), g, d), 1)
                for d in range(2):
                    act.wait_ge(p3.sem, p3.after("u", g, d))
                    act.activation(d_[d][:], bank[4 * d + 1][:, :], ACT.Copy).then_inc(a3.step("u", g, d), 1)

        @block.gpsimd
        def _(pool):
            for g in range(NT):
                for d in range(2):
                    if g:
                        pool.wait_ge(p3.sem, p3.after("o", g - 1, d))
                    pool.tensor_copy(heads(d_[d][:]), bc(ident.unsqueeze(1), P, H, P)).then_inc(g3.step("init", g, d), 1)
                for d in range(2):
                    pool.wait_ge(v3.sem, v3.after("t1", g, d))
                    pool.tensor_tensor(heads(f_[d][:]), heads(w_[d][:]), bc(neg[d].unsqueeze(1), P, H, P),
                                       ALU.add).then_inc(g3.step("m1", g, d), 1)
                for d in range(2):
                    pool.tensor_tensor(heads(qk_[d][:]), bc(neg[1 - d].unsqueeze(1), P, H, P), heads(w_[d][:]),
                                       ALU.subtract).then_inc(g3.step("m2", g, d), 1)
                for d in range(2):
                    pool.wait_ge(a3.sem, a3.after("eg", g, d))
                    pool.tensor_tensor(heads(kd_[d][:]), heads(k_tm[:, tile_of(g, d), :]),
                                       bc(eg[d][:, 8:12].unsqueeze(2), P, H, HD), ALU.mult).then_inc(g3.step("kd", g, d), 1)
                for d in range(2):
                    t = tile_of(g, d)
                    pool.tensor_tensor(heads(vb_[d][:]), heads(v_tm[:, t, :]),
                                       bc(smg[:, t, 4 * d:4 * d + 4].unsqueeze(2), P, H, HD), ALU.mult).then_inc(g3.step("vb", g, d), 1)
                for d in range(2):
                    pool.wait_ge(a3.sem, a3.after("egb", g, d))
                    pool.tensor_tensor(heads(qd_[d][:]), heads(qd_[d][:]), qkv[:, 0:4, ctok(tile_of(g, d))],
                                       ALU.mult).then_inc(g3.step("qd", g, d), 1)

        @block.vector
        def _(dve):
            for d in range(2):
                dve.memset(s_[d][:], 0.0).then_inc(v3.step("z", d), 1)
            for g in range(NT):
                for d in range(2):
                    g4 = smg[:, tile_of(g, d), 8 + 4 * d:12 + 4 * d]
                    dve.tensor_tensor(heads(n_[d][:]), bc(tri[d].unsqueeze(1), P, H, P), bc(g4.unsqueeze(2), P, H, P),
                                      ALU.mult).then_inc(v3.step("gtri", g, d), 1)
                for d in range(2):
                    dve.wait_ge(p3.sem, p3.after("gcol", g, d))
                    dve.tensor_copy(gc[d][:, 0:8], bank[4 * d][:, 0:8]).then_inc(v3.step("gc", g, d), 1)
                for d in range(2):
                    dve.wait_ge(v3.sem, v3.after("gc", g, d))
                    dve.tensor_tensor(gc[d][:, 8:12], gc[d][:, 4:8], gc[d][:, 0:4], ALU.subtract).then_inc(v3.step("kd", g, d), 1)
                for d in range(2):
                    dve.tensor_scalar(nb[d][:, 0:4], smg[:, tile_of(g, d), 4 * d:4 * d + 4], -1.0, None,
                                      ALU.mult).then_inc(v3.step("nb", g, d), 1)
                for d in range(2):
                    dve.wait_ge(p3.sem, p3.after("gb", g, d))
                    dve.tensor_tensor(heads(w_[d][:]), bc(gc[d][:, 0:4].unsqueeze(2), P, H, P), heads(bank[4 * d + 1][:, :]),
                                      ALU.subtract).then_inc(v3.step("t1", g, d), 1)
                for d in range(2):
                    dve.wait_ge(p3.sem, p3.after("kk", g, d))
                    dve.wait_ge(a3.sem, a3.after("dec", g, d))
                    dve.tensor_tensor(n_[d][:], bank[4 * d + 2][:, :], f_[d][:], ALU.mult).then_inc(v3.step("n0", g, d), 1)
                for d in range(2):
                    dve.wait_ge(a3.sem, a3.after("eg", g, d))
                    dve.wait_ge(v3.sem, v3.after("nb", g, d))
                    dve.tensor_tensor(nb[d][:, 4:8], nb[d][:, 0:4], eg[d][:, 0:4], ALU.mult).then_inc(v3.step("nbe", g, d), 1)
                for d in range(2):
                    dve.wait_ge(v3.sem, v3.after("n0", g, d))
                    dve.tensor_tensor(heads(n_[d][:]), heads(n_[d][:]), bc(nb[d][:, 0:4].unsqueeze(2), P, H, P),
                                      ALU.mult).then_inc(v3.step("n1", g, d), 1)
                for d in range(2):
                    dve.wait_ge(a3.sem, a3.after("qdec", g, d))
                    dve.tensor_tensor(qk_[d][:], bank[4 * d + 3][:, :], qk_[d][:], ALU.mult).then_inc(v3.step("qk", g, d), 1)
                for d in range(2):
                    dve.wait_ge(g3.sem, g3.after("init", g, d))
                    dve.tensor_copy(dt_[d][:], d_[d][:]).then_inc(v3.step("p0", g, d), 1)
                for d in range(2):
                    dve.wait_ge(v3.sem, v3.after("p0", g, d))
                    dve.wait_ge(v3.sem, v3.after("n1", g, d))
                    dve.copy_predicated(heads(d_[d][:]), bc(lev[:, d, 0, :].unsqueeze(1), P, H, P), heads(n_[d][:]))
                    dve.wait_ge(p3.sem, p3.after("nt", g, d))
                    dve.copy_predicated(heads(dt_[d][:]), bc(lev[:, 1 - d, 0, :].unsqueeze(1), P, H, P),
                                        heads(bank[4 * d][:, :])).then_inc(v3.step("p1", g, d), 1)
                for l in inv:
                    for d in range(2):
                        dve.wait_ge(p3.sem, p3.after(("x", l), g, d))
                        dve.copy_predicated(heads(dt_[d][:]), bc(lev[:, 1 - d, l, :].unsqueeze(1), P, H, P),
                                            heads(bank[4 * d + 2][:, :])).then_inc(v3.step(("x", l), g, d), 1)
                for d in range(2):
                    dve.wait_ge(p3.sem, p3.after("ks", g, d))
                    dve.wait_ge(g3.sem, g3.after("vb", g, d))
                    dve.tensor_tensor(heads(w_[d][:]), heads(bank[4 * d][:, :]), bc(nb[d][:, 4:8].unsqueeze(2), P, H, HD),
                                      ALU.mult).then_inc(v3.step("w0", g, d), 1)
                for d in range(2):
                    dve.wait_ge(v3.sem, v3.after("w0", g, d))
                    dve.tensor_tensor(w_[d][:], w_[d][:], vb_[d][:], ALU.add).then_inc(v3.step("w1", g, d), 1)
                for d in range(2):
                    dve.wait_ge(p3.sem, p3.after("o", g, d))
                    dve.tensor_copy((o_b if d else o_f)[:, :, tok(tile_of(g, d))],
                                    heads(bank[4 * d + 2][:, :])).then_inc(v3.step("o", g, d), 1)
                if g == 1:
                    dve.wait_ge(got_s, 32)
                for d in range(2):
                    dve.wait_ge(a3.sem, a3.after("eg", g, d))
                    dve.tensor_tensor(heads(s_[d][:]), heads(s_[d][:]), bc(eg[d][:, 4:8].unsqueeze(2), P, H, HD),
                                      ALU.mult).then_inc(v3.step("s0", g, d), 1)
                for d in range(2):
                    dve.wait_ge(v3.sem, v3.after("s0", g, d))
                    dve.tensor_tensor(s_[d][:], s_[d][:], bank[4 * d + 3][:, :], ALU.add).then_inc(v3.step("s1", g, d), 1)
    if stop <= 3:
        return dict(locals())

    stage3_keep = stage2_keep + 64 + T * H * 4 + 32
    cursor[0] = base0
    qc = sb("qc", [P, H, T])
    kc = sb("kc", [P, H, T])
    og = sb("og", [P, H, T])
    cursor[0] = stage1_keep
    kc_tm = sb("kc_tm", [P, NT, H * HD])
    vc_tm = sb("vc_tm", [P, NT, H * HD])
    cursor[0] = stage3_keep
    sqa = sb("sqa", [P, H, T])
    rsa = sb("rsa", [P, H, T])
    tz = sb("tz", [P, H, T])
    UN = [("q", j) for j in range(4)] + [("k", j) for j in range(4)] + [("v", t) for t in range(NT)] + [("o", j) for j in range(4)]
    lp4, la4, lv4 = [], [], []
    for n, u in enumerate(UN):
        lp4 += [u] + ([("sum", u[1])] if u[0] == "k" else []) + ([("kt", u[1])] if u[0] == "v" else [])
        la4 += [u + (0,)] + ([u + (1,)] if u[0] == "o" else []) + ([("rms", u[1], 0), ("rms", u[1], 1)] if u[0] == "k" else [])
        la4 += [("tz",)] if n == 0 else []
        lv4 += [u] if u[0] in "qk" else [("kt", u[1])] if u[0] == "v" else []
        lv4 += [("fin", i) for i in range(4)] if n == 8 else []
    p4, a4, v4 = Steps(nc, "proj2_tensor", lp4), Steps(nc, "proj2_scalar", la4), Steps(nc, "proj2_vector", lv4)
    g4_ = Steps(nc, "proj2_gpsimd", [("o",), ("sq",)])
    with nc.Block("proj2", no_gpsimd_drain=True) as block:
        @block.sync
        def _(sp):
            for n, last in ((18, ("q", 3)), (19, ("k", 3)), (20, ("v", 4)), (21, ("o", 3))):
                load_block(sp, n + RING, p4.sem, p4.after(*last))

        @block.tensor
        def _(pe):
            for n, (kind, j) in enumerate(UN):
                blk = 18 + "qkvo".index(kind)
                if j == 0:
                    block_ready(pe, blk)
                if n >= 2:
                    prev = UN[n - 2]
                    pe.wait_ge(a4.sem, a4.after(*prev, 1 if prev[0] == "o" else 0))
                    if prev[0] in "qk":
                        pe.wait_ge(v4.sem, v4.after(*prev))
                lat, ctx = bank[2 * (n % 2)], bank[2 * (n % 2) + 1]
                for k in range(KD):
                    if kind == "v":
                        mm = pe.matmul(lat[:, :], hT[:, k, tok(j)], ring[:, blk % RING, 512 * k:512 * k + 512],
                                       start=(k == 0), stop=(k == KD - 1))
                    else:
                        w = ring[:, blk % RING, 512 * k + P * j:512 * k + P * j + P]
                        pe.matmul(lat[:, :], w, hT[:, k, P:T], start=(k == 0), stop=(k == KD - 1))
                        mm = pe.matmul(ctx[:, 0:P], w, hT[:, k, 0:P], start=(k == 0), stop=(k == KD - 1))
                mm.then_inc(p4.step(kind, j), 1)
                if kind == "k":
                    pe.wait_ge(g4_.sem, g4_.after("sq"))
                    if j:
                        pe.wait_ge(a4.sem, a4.after("rms", j - 1, 1))
                    pe.matmul(bank[4][:, :], ones, sqa[:, j, P:T], start=True, stop=True)
                    pe.matmul(bank[5][:, 0:P], ones, sqa[:, j, 0:P], start=True, stop=True).then_inc(p4.step("sum", j), 1)
                if kind == "v":
                    if j == 0:
                        for i in range(4):
                            pe.wait_ge(a4.sem, a4.after("k", i, 0))
                            pe.wait_ge(v4.sem, v4.after("k", i))
                    if j >= 2:
                        pe.wait_ge(v4.sem, v4.after("kt", j - 2))
                    for h in range(H):
                        mm = pe.transpose(bank[6 + j % 2][:, P * h:P * h + P], kc[:, h, tok(j)], ident)
                    mm.then_inc(p4.step("kt", j), 1)

        @block.scalar
        def _(act):
            for n, (kind, j) in enumerate(UN):
                act.wait_ge(p4.sem, p4.after(kind, j))
                lat, ctx = bank[2 * (n % 2)], bank[2 * (n % 2) + 1]
                if kind == "v":
                    act.activation(vc_tm[:, j, :], lat[:, :], ACT.Copy).then_inc(a4.step("v", j, 0), 1)
                elif kind == "o":
                    act.activation(og[:, j, P:T], lat[:, :], ACT.Tanh, scale=0.5).then_inc(a4.step("o", j, 0), 1)
                    act.activation(og[:, j, 0:P], ctx[:, 0:P], ACT.Tanh, scale=0.5).then_inc(a4.step("o", j, 1), 1)
                else:
                    act.activation((qc if kind == "q" else kc)[:, j, P:T], lat[:, :], ACT.Copy,
                                   scale=1.0 if kind == "q" else HD ** -0.5).then_inc(a4.step(kind, j, 0), 1)
                if kind == "k":
                    act.wait_ge(p4.sem, p4.after("sum", j))
                    act.activation(rsa[:, j, P:T], bank[4][:, :], ACT.Sqrt, scale=1.0 / HD, bias=col(E_RMS)).then_inc(a4.step("rms", j, 0), 1)
                    act.activation(rsa[:, j, 0:P], bank[5][:, 0:P], ACT.Sqrt, scale=1.0 / HD, bias=col(E_RMS)).then_inc(a4.step("rms", j, 1), 1)
                if n == 0:
                    act.activation(tz[:], yA[:], ACT.Tanh, scale=0.5).then_inc(a4.step("tz"), 1)

        @block.gpsimd
        def _(pool):
            pool.tensor_tensor(o_b[:], o_b[:], o_f[:], ALU.add).then_inc(g4_.step("o"), 1)
            pool.wait_ge(g4_.sem, g4_.after("o"))
            pool.tensor_tensor(sqa[:], o_b[:], o_b[:], ALU.mult).then_inc(g4_.step("sq"), 1)

        @block.vector
        def _(dve):
            for n, (kind, j) in enumerate(UN):
                ctx = bank[2 * (n % 2) + 1]
                if kind in "qk":
                    dve.wait_ge(p4.sem, p4.after(kind, j))
                    dve.tensor_scalar((qc if kind == "q" else kc)[:, j, 0:P], ctx[:, 0:P],
                                      1.0 if kind == "q" else HD ** -0.5, None, ALU.mult).then_inc(v4.step(kind, j), 1)
                elif kind == "v":
                    dve.wait_ge(p4.sem, p4.after("kt", j))
                    dve.tensor_copy(kc_tm[:, j, :], bank[6 + j % 2][:, :]).then_inc(v4.step("kt", j), 1)
                if n == 8:
                    dve.wait_ge(a4.sem, a4.after("rms", 3, 1))
                    dve.reciprocal(rsa[:], rsa[:]).then_inc(v4.step("fin", 0), 1)
                    dve.wait_ge(v4.sem, v4.after("fin", 0))
                    dve.scalar_tensor_tensor(o_b[:], o_b[:], vec[:, V_DN:V_DN + 1], rsa[:], ALU.mult,
                                             ALU.mult).then_inc(v4.step("fin", 1), 1)
                    dve.scalar_tensor_tensor(tz[:], tz[:], 1.0, yA[:], ALU.add, ALU.mult).then_inc(v4.step("fin", 2), 1)
                    dve.wait_ge(v4.sem, v4.after("fin", 2))
                    dve.scalar_tensor_tensor(yA[:], tz[:], 0.5, o_b[:], ALU.mult, ALU.mult).then_inc(v4.step("fin", 3), 1)
    if stop <= 4:
        return dict(locals())

    cursor[0] = stage2_keep
    h_f = sb("h_f", [P, NT, H * HD])
    h_b = sb("h_b", [P, NT, H * HD])
    hh = [h_f, h_b]
    r1_, r2_, am_, pt_, kw_, t1_, c_ = (two(x) for x in ("ml_r1", "ml_r2", "ml_am", "ml_pt", "ml_kw", "ml_t1", "ml_c"))
    fc = two("ml_fc", 8)
    sm = two("ml_sm", 48)
    nst, mst = two("ml_n", 4), two("ml_m", 4)
    X_A, X_AMAX, X_MLOC, X_M, X_MEND, X_E, X_DEN, X_NDEN = 0, 4, 8, 12, 16, 20, 36, 40
    E_WINT, E_EMT, E_WTOK, E_SINT = 20, 24, 28, 32
    nlf = sb("nlf", [P, NT, 8])
    got_c = nc.alloc_semaphore("got_mlstm_state")
    lv5 = both("r2", "fc", "a", "amax", "am", "mloc", "M", "Mend", "e1", "e2", "e3", "e4", "mnew", "sub", "pm", "dsum",
               "c0", "n0", "n1", "c1", "t1", "t2", "den", "nden", "den2", "den3", "rden", "h")
    la5, lp5 = both("e", "pm", "pt"), both("gcol", "arow", "qk", "pt", "qc", "pv", "cu")
    lg5 = both("r1", "kw")
    v5 = Steps(nc, "mlstm_vector", [("z", 0), ("z", 1), ("z", 2), ("z", 3), ("z", 4), ("z", 5), ("nlf", 0)] + lv5[:2 * 28]
               + [("init", 0), ("init", 1), ("init", 2), ("init", 3)] + lv5[2 * 28:])
    a5, p5, g5 = Steps(nc, "mlstm_scalar", la5), Steps(nc, "mlstm_tensor", lp5), Steps(nc, "mlstm_gpsimd", lg5)
    with nc.Block("mlstm", no_gpsimd_drain=True) as block:
        @block.sync
        def _(sp):
            for d in range(2):
                sp.wait_ge(v5.sem, v5.after("c1", 0, d))
                store(sp, O["mc"][d], c_[d][:])
                store(sp, O["mn"][d], nst[d][:])
                store(sp, O["mm"][4 * d:4 * d + 4].rearrange("(a b) -> a b", a=1), mst[d][0:1, :])
            sp.wait_ge(stored, stores[0])
            for d in range(2):
                sp.dma_start(c_[d][:], A["s_mc"][d]).then_inc(got_c, 16)
            sp.wait_ge(got_c, 32)

        @block.tensor
        def _(pe):
            def hd(t, h):
                return t[:, P * h:P * h + P]

            for g in range(NT):
                for d in range(2):
                    t = tile_of(g, d)
                    lf4 = smg[:, t, 24 + 4 * d:28 + 4 * d]
                    if g:
                        pe.wait_ge(v5.sem, v5.after("den", g - 1, d))
                        pe.wait_ge(a5.sem, a5.after("pt", g - 1, d))
                    pe.matmul(bank[4 * d][:, 0:4], tri[d], lf4, start=True, stop=True)
                    pe.matmul(bank[4 * d][:, 4:8], ones, lf4, start=True, stop=True).then_inc(p5.step("gcol", g, d), 1)
                for d in range(2):
                    pe.wait_ge(v5.sem, v5.after("r2", g, d))
                    pe.wait_ge(g5.sem, g5.after("r1", g, d))
                    if g:
                        pe.wait_ge(v5.sem, v5.after("c1", g - 1, d))
                    pe.matmul(bank[4 * d + 1][:, :], ones, r1_[d][:], start=True, stop=False)
                    pe.matmul(bank[4 * d + 1][:, :], ones, r2_[d][:], start=False, stop=True).then_inc(p5.step("arow", g, d), 1)
                for d in range(2):
                    ts = tok(tile_of(g, d))
                    if g:
                        pe.wait_ge(v5.sem, v5.after("t2", g - 1, d))
                    for h in range(H):
                        mm = pe.matmul(hd(bank[4 * d + 2], h), qc[:, h, ts], kc[:, h, ts], start=True, stop=True)
                    mm.then_inc(p5.step("qk", g, d), 1)
                for d in range(2):
                    pe.wait_ge(v5.sem, v5.after("pm", g, d))
                    if g:
                        pe.wait_ge(v5.sem, v5.after("t2", g - 1, d))
                    for h in range(H):
                        mm = pe.transpose(hd(bank[4 * d + 3], h), hd(am_[d], h), ident)
                    mm.then_inc(p5.step("pt", g, d), 1)
                for d in range(2):
                    ts = tok(tile_of(g, d))
                    if g == 0:
                        pe.wait_ge(v5.sem, v5.after("z", 5))
                    elif g == 1:
                        pe.wait_ge(got_c, 32)
                        pe.wait_ge(v5.sem, v5.after("init", 3))
                    pe.wait_ge(v5.sem, v5.after("fc", g, d))
                    for h in range(H):
                        pe.matmul(hd(bank[4 * d + 2], h), qc[:, h, ts], hd(c_[d], h), start=True, stop=True)
                    for h in range(H):
                        mm = pe.matmul(bank[4 * d][:, 16 + h:17 + h], qc[:, h, ts], nst[d][:, h:h + 1], start=True, stop=True)
                    mm.then_inc(p5.step("qc", g, d), 1)
                for d in range(2):
                    t = tile_of(g, d)
                    pe.wait_ge(a5.sem, a5.after("pt", g, d))
                    for h in range(H):
                        mm = pe.matmul(hd(bank[4 * d + 3], h), hd(pt_[d], h), vc_tm[:, t, P * h:P * h + P], start=True, stop=True)
                    mm.then_inc(p5.step("pv", g, d), 1)
                for d in range(2):
                    t = tile_of(g, d)
                    pe.wait_ge(g5.sem, g5.after("kw", g, d))
                    pe.wait_ge(v5.sem, v5.after("am", g, d))
                    for h in range(H):
                        pe.matmul(hd(bank[4 * d + 1], h), hd(kw_[d], h), vc_tm[:, t, P * h:P * h + P], start=True, stop=True)
                    for h in range(H):
                        mm = pe.matmul(bank[4 * d][:, 24 + h:25 + h], hd(kw_[d], h), ones[:, 0:1], start=True, stop=True)
                    mm.then_inc(p5.step("cu", g, d), 1)

        @block.gpsimd
        def _(pool):
            for g in range(NT):
                for d in range(2):
                    i4 = smg[:, tile_of(g, d), 16 + 4 * d:20 + 4 * d]
                    if g:
                        pool.wait_ge(p5.sem, p5.after("arow", g - 1, d))
                    pool.tensor_tensor(heads(r1_[d][:]), bc(ident.unsqueeze(1), P, H, P), bc(i4.unsqueeze(2), P, H, P),
                                       ALU.mult).then_inc(g5.step("r1", g, d), 1)
                for d in range(2):
                    pool.wait_ge(a5.sem, a5.after("e", g, d))
                    if g:
                        pool.wait_ge(p5.sem, p5.after("cu", g - 1, d))
                    pool.tensor_tensor(heads(kw_[d][:]), heads(kc_tm[:, tile_of(g, d), :]),
                                       bc(sm[d][:, E_WTOK:E_WTOK + 4].unsqueeze(2), P, H, HD), ALU.mult).then_inc(g5.step("kw", g, d), 1)

        @block.scalar
        def _(act):
            for g in range(NT):
                for d in range(2):
                    act.wait_ge(v5.sem, v5.after("e4", g, d))
                    act.activation(sm[d][:, X_E:X_E + 16], sm[d][:, X_E:X_E + 16], ACT.Exp).then_inc(a5.step("e", g, d), 1)
                for d in range(2):
                    act.wait_ge(v5.sem, v5.after("sub", g, d))
                    act.activation(am_[d][:], am_[d][:], ACT.Exp).then_inc(a5.step("pm", g, d), 1)
                for d in range(2):
                    act.wait_ge(p5.sem, p5.after("pt", g, d))
                    if g:
                        act.wait_ge(p5.sem, p5.after("pv", g - 1, d))
                    act.activation(pt_[d][:], bank[4 * d + 3][:, :], ACT.Copy).then_inc(a5.step("pt", g, d), 1)

        @block.vector
        def _(dve):
            for d in range(2):
                dve.memset(c_[d][:], 0.0).then_inc(v5.step("z", 3 * d), 1)
                dve.memset(nst[d][:], 0.0).then_inc(v5.step("z", 3 * d + 1), 1)
                dve.memset(mst[d][:], 0.0).then_inc(v5.step("z", 3 * d + 2), 1)
            dve.tensor_scalar(nlf[:], smg[:, :, 24:32], -1.0, None, ALU.mult).then_inc(v5.step("nlf", 0), 1)
            dve.wait_ge(v5.sem, v5.after("nlf", 0))
            for g in range(NT):
                for d in range(2):
                    if g:
                        dve.wait_ge(p5.sem, p5.after("arow", g - 1, d))
                    dve.tensor_tensor(heads(r2_[d][:]), bc(tri[d].unsqueeze(1), P, H, P),
                                      bc(nlf[:, tile_of(g, d), 4 * d:4 * d + 4].unsqueeze(2), P, H, P),
                                      ALU.mult).then_inc(v5.step("r2", g, d), 1)
                for d in range(2):
                    dve.wait_ge(p5.sem, p5.after("gcol", g, d))
                    dve.tensor_copy(fc[d][:], bank[4 * d][:, 0:8]).then_inc(v5.step("fc", g, d), 1)
                for d in range(2):
                    dve.wait_ge(v5.sem, v5.after("fc", g, d))
                    dve.tensor_tensor(sm[d][:, X_A:X_A + 4], smg[:, tile_of(g, d), 16 + 4 * d:20 + 4 * d], fc[d][:, 0:4],
                                      ALU.subtract).then_inc(v5.step("a", g, d), 1)
                for d in range(2):
                    dve.wait_ge(p5.sem, p5.after("arow", g, d))
                    dve.tensor_reduce(sm[d][:, X_AMAX:X_AMAX + 4], heads(bank[4 * d + 1][:, :]), AX, ALU.max).then_inc(v5.step("amax", g, d), 1)
                for d in range(2):
                    if g:
                        dve.wait_ge(p5.sem, p5.after("pt", g - 1, d))
                    dve.tensor_tensor(heads(am_[d][:]), heads(bank[4 * d + 1][:, :]), bc(neg[d].unsqueeze(1), P, H, P),
                                      ALU.add).then_inc(v5.step("am", g, d), 1)
                for d in range(2):
                    dve.wait_ge(v5.sem, v5.after("am", g, d))
                    dve.tensor_reduce(sm[d][:, X_MLOC:X_MLOC + 4], heads(am_[d][:]), AX, ALU.max).then_inc(v5.step("mloc", g, d), 1)
                s4 = lambda d, x: sm[d][:, x:x + 4]
                for d in range(2):
                    dve.wait_ge(v5.sem, v5.after("mloc", g, d))
                    dve.tensor_tensor(s4(d, X_M), s4(d, X_MLOC), mst[d][:], ALU.max).then_inc(v5.step("M", g, d), 1)
                for d in range(2):
                    dve.tensor_tensor(s4(d, X_MEND), s4(d, X_AMAX), mst[d][:], ALU.max).then_inc(v5.step("Mend", g, d), 1)
                for d in range(2):
                    dve.wait_ge(v5.sem, v5.after("Mend", g, d))
                    dve.tensor_tensor(s4(d, E_WINT), mst[d][:], s4(d, X_M), ALU.subtract).then_inc(v5.step("e1", g, d), 1)
                for d in range(2):
                    dve.scalar_tensor_tensor(s4(d, E_EMT), fc[d][:, 0:4], -1.0, s4(d, X_M), ALU.mult,
                                             ALU.subtract).then_inc(v5.step("e2", g, d), 1)
                for d in range(2):
                    dve.tensor_tensor(s4(d, E_WTOK), s4(d, X_A), s4(d, X_MEND), ALU.subtract).then_inc(v5.step("e3", g, d), 1)
                for d in range(2):
                    dve.tensor_tensor(s4(d, E_SINT), mst[d][:], s4(d, X_MEND), ALU.subtract).then_inc(v5.step("e4", g, d), 1)
                for d in range(2):
                    dve.wait_ge(v5.sem, v5.after("e4", g, d))
                    dve.tensor_tensor(mst[d][:], fc[d][:, 4:8], s4(d, X_MEND), ALU.add).then_inc(v5.step("mnew", g, d), 1)
                for d in range(2):
                    dve.tensor_tensor(heads(am_[d][:]), heads(am_[d][:]), bc(s4(d, X_M).unsqueeze(2), P, H, P),
                                      ALU.subtract).then_inc(v5.step("sub", g, d), 1)
                for d in range(2):
                    dve.wait_ge(a5.sem, a5.after("pm", g, d))
                    dve.wait_ge(p5.sem, p5.after("qk", g, d))
                    dve.tensor_tensor(am_[d][:], am_[d][:], bank[4 * d + 2][:, :], ALU.mult).then_inc(v5.step("pm", g, d), 1)
                for d in range(2):
                    dve.wait_ge(v5.sem, v5.after("pm", g, d))
                    dve.tensor_reduce(s4(d, X_DEN), heads(am_[d][:]), AX, ALU.add).then_inc(v5.step("dsum", g, d), 1)
                for d in range(2):
                    dve.wait_ge(p5.sem, p5.after("qc", g, d))
                    dve.wait_ge(a5.sem, a5.after("e", g, d))
                    dve.tensor_tensor(heads(c_[d][:]), heads(c_[d][:]), bc(s4(d, E_SINT).unsqueeze(2), P, H, HD),
                                      ALU.mult).then_inc(v5.step("c0", g, d), 1)
                for d in range(2):
                    dve.tensor_tensor(nst[d][:], nst[d][:], s4(d, E_SINT), ALU.mult).then_inc(v5.step("n0", g, d), 1)
                for d in range(2):
                    dve.wait_ge(p5.sem, p5.after("cu", g, d))
                    dve.wait_ge(v5.sem, v5.after("n0", g, d))
                    dve.tensor_tensor(nst[d][:], nst[d][:], bank[4 * d][:, 24:28], ALU.add).then_inc(v5.step("n1", g, d), 1)
                for d in range(2):
                    dve.tensor_tensor(c_[d][:], c_[d][:], bank[4 * d + 1][:, :], ALU.add).then_inc(v5.step("c1", g, d), 1)
                for d in range(2):
                    dve.tensor_tensor(heads(t1_[d][:]), heads(bank[4 * d + 2][:, :]), bc(s4(d, E_WINT).unsqueeze(2), P, H, HD),
                                      ALU.mult).then_inc(v5.step("t1", g, d), 1)
                for d in range(2):
                    dve.wait_ge(p5.sem, p5.after("pv", g, d))
                    dve.wait_ge(v5.sem, v5.after("t1", g, d))
                    dve.tensor_tensor(t1_[d][:], t1_[d][:], bank[4 * d + 3][:, :], ALU.add).then_inc(v5.step("t2", g, d), 1)
                for d in range(2):
                    dve.tensor_tensor(s4(d, X_NDEN), bank[4 * d][:, 16:20], s4(d, E_WINT), ALU.mult).then_inc(v5.step("den", g, d), 1)
                for d in range(2):
                    dve.wait_ge(v5.sem, v5.after("den", g, d))
                    dve.tensor_tensor(s4(d, X_DEN), s4(d, X_DEN), s4(d, X_NDEN), ALU.add).then_inc(v5.step("nden", g, d), 1)
                for d in range(2):
                    dve.wait_ge(v5.sem, v5.after("nden", g, d))
                    dve.scalar_tensor_tensor(s4(d, X_DEN), s4(d, X_DEN), -1.0, s4(d, X_DEN), ALU.mult, ALU.max).then_inc(v5.step("den2", g, d), 1)
                for d in range(2):
                    dve.wait_ge(v5.sem, v5.after("den2", g, d))
                    dve.tensor_tensor(s4(d, X_DEN), s4(d, X_DEN), s4(d, E_EMT), ALU.max).then_inc(v5.step("den3", g, d), 1)
                for d in range(2):
                    dve.wait_ge(v5.sem, v5.after("den3", g, d))
                    dve.reciprocal(s4(d, X_DEN), s4(d, X_DEN)).then_inc(v5.step("rden", g, d), 1)
                for d in range(2):
                    dve.wait_ge(v5.sem, v5.after("rden", g, d))
                    dve.wait_ge(v5.sem, v5.after("t2", g, d))
                    dve.tensor_tensor(heads(hh[d][:, tile_of(g, d), :]), heads(t1_[d][:]), bc(s4(d, X_DEN).unsqueeze(2), P, H, HD),
                                      ALU.mult).then_inc(v5.step("h", g, d), 1)
                if g == 0:
                    dve.wait_ge(got_c, 32)
                    for d in range(2):
                        dve.tensor_copy(nst[d][:], vec[:, V_SN + 4 * d:V_SN + 4 * d + 4]).then_inc(v5.step("init", 2 * d), 1)
                        dve.tensor_copy(mst[d][:], row[:, R_M + 4 * d:R_M + 4 * d + 4]).then_inc(v5.step("init", 2 * d + 1), 1)
    if stop <= 5:
        return dict(locals())

    st6 = sb("st6", [P, NT * H, 6])
    mv6 = sb("mv6", [P, NT, H, 2])
    rs6 = sb("rs6", [P, NT, H])
    v6 = Steps(nc, "mlstm_norm_vector", [x for i in range(NT + 2) for x in (
        ([("add", i)] + [("stat", i, h) for h in range(H)] + [("mv", i, h) for h in range(H)] if i < NT else [])
        + ([("rec", i - 1), ("norm", i - 1)] if 0 < i <= NT else []) + ([("y", i - 2)] if i > 1 else []))])
    p6 = Steps(nc, "mlstm_norm_tensor", [("t", t) for t in range(NT)])
    a6, g6 = Steps(nc, "mlstm_norm_scalar", [("sqrt", t) for t in range(NT)]), Steps(nc, "mlstm_norm_gpsimd", [("og",)])
    with nc.Block("mlstm_norm", no_gpsimd_drain=True) as block:
        @block.vector
        def _(dve):
            def moments(t):
                dve.tensor_tensor(h_f[:, t, :], h_f[:, t, :], h_b[:, t, :], ALU.add).then_inc(v6.step("add", t), 1)
                dve.wait_ge(v6.sem, v6.after("add", t))
                for h in range(H):
                    dve.bn_stats(st6[:, H * t + h, :], h_f[:, t, P * h:P * h + P]).then_inc(v6.step("stat", t, h), 1)
                for h in range(H):
                    dve.wait_ge(v6.sem, v6.after("stat", t, h))
                    dve.bn_aggr(mv6[:, t, h, :], st6[:, H * t + h, :]).then_inc(v6.step("mv", t, h), 1)

            def norm(t):
                dve.wait_ge(a6.sem, a6.after("sqrt", t))
                dve.reciprocal(rs6[:, t, :], rs6[:, t, :]).then_inc(v6.step("rec", t), 1)
                dve.wait_ge(v6.sem, v6.after("rec", t))
                for h in range(H):
                    x = h_f[:, t, P * h:P * h + P]
                    ins = dve.tensor_scalar(x, x, mv6[:, t, h, 0:1], rs6[:, t, h:h + 1], ALU.subtract, ALU.mult)
                ins.then_inc(v6.step("norm", t), 1)

            def gated(t):
                dve.wait_ge(g6.sem, g6.after("og"))
                dve.wait_ge(p6.sem, p6.after("t", t))
                for h in range(H):
                    ins = dve.scalar_tensor_tensor(yC[:, h, tok(t)], bank[t][:, P * h:P * h + P], vec[:, V_MN + h:V_MN + h + 1],
                                                   og[:, h, tok(t)], ALU.mult, ALU.mult)
                ins.then_inc(v6.step("y", t), 1)

            for i in range(NT + 2):
                if i < NT:
                    moments(i)
                if 0 < i <= NT:
                    norm(i - 1)
                if i > 1:
                    gated(i - 2)

        @block.gpsimd
        def _(pool):
            pool.tensor_scalar(og[:], og[:], 1.0, 0.5, ALU.add, ALU.mult).then_inc(g6.step("og"), 1)

        @block.scalar
        def _(act):
            for t in range(NT):
                act.wait_ge(v6.sem, v6.after("mv", t, H - 1))
                act.activation(rs6[:, t, :], mv6[:, t, :, 1], ACT.Sqrt, bias=col(E_LN)).then_inc(a6.step("sqrt", t), 1)

        @block.tensor
        def _(pe):
            for t in range(NT):
                pe.wait_ge(v6.sem, v6.after("norm", t))
                for h in range(H):
                    mm = pe.transpose(bank[t][:, P * h:P * h + P], h_f[:, t, P * h:P * h + P], ident)
                mm.then_inc(p6.step("t", t), 1)
    if stop <= 6:
        return dict(locals())

    MW = 3 * (KD + 4) * P
    cursor[0] = base0 - RING * 4096 * 4
    mT = sb("mT", [P, KD, T])
    rows_off = cursor[0]
    rows = sb("rows", [P, 4, 2, D])
    w_out = sb("w_out", [P, KD, D])
    stage7_keep = cursor[0]
    mring = sb("mring", [P, 2, MW])
    sg = sb("sg", [P, 2, T])
    pr = sb("pr", [P, 2, T])
    acc = sb("acc", [P, T])
    dg = sb("dg", [P, 2, 4 * P])
    ROWS = [(r, c, f) for r in range(4) for c in range(2) for f in range(2)]
    a7r, p7r = Steps(nc, "rows_scalar", [("r", i) for i in range(16)]), Steps(nc, "rows_tensor", [("r", i) for i in range(16)])
    g7r = Steps(nc, "rows_gpsimd", [("r", i) for i in range(16)])
    U = range(6)
    p7 = LoopSteps(nc, "merge_tensor", [(x, u) for u in U for x in ("gate", "proj")])
    a7 = LoopSteps(nc, "merge_scalar", [("sg", u) for u in U])
    v7 = LoopSteps(nc, "merge_vector", [(x, u) for u in U for x in (("pr",) if u % 3 == 0 else ("pr", "add"))])
    got_m = [nc.alloc_semaphore(f"got_merge{i}") for i in range(2)]
    got_wo = nc.alloc_semaphore("got_w_out")
    branch = [yA, yB, yC]
    with nc.Block("merge", no_gpsimd_drain=True) as block:
        @block.sync
        def _(sp):
            for x in range(2):
                sp.dma_start(mring[:, x, :], A["merge"][x]).then_inc(got_m[x], 16)
            sp.dma_start(w_out[:], A["w_out"]).then_inc(got_wo, 16)
            with sp.Fori(1, KD // 2) as i:
                for x in range(2):
                    sp.wait_ge(p7.sem, p7.after("proj", 3 * x + 2, turn=i - 1))
                    sp.dma_start(mring[:, x, :], A["merge"][bass.ds(2 * i + x, 1)].rearrange("a p n -> (a p) n")).then_inc(got_m[x], 16)

        @block.gpsimd
        def _(pool):
            for i, (r, c, f) in enumerate(ROWS):
                if i >= 2:
                    pool.wait_ge(p7r.sem, p7r.after("r", i - 2))
                m = 16 + 8 * ((r - 1) % 4) + 4 * f
                pool.tensor_tensor(heads(dg[:, i % 2, :]), bc(ident.unsqueeze(1), P, 4, P),
                                   bc(modc[:, m:m + 4, c].unsqueeze(2), P, 4, P), ALU.mult).then_inc(g7r.step("r", i), 1)

        @block.scalar
        def _(act):
            a7.credit(act)
            for i, (r, c, f) in enumerate(ROWS):
                act.wait_ge(p7r.sem, p7r.after("r", i))
                act.activation(rows[:, r, c, 512 * f:512 * f + 512], bank[i % 2][:, :], ACT.Copy,
                               scale=0.5 if r == 1 else 1.0).then_inc(a7r.step("r", i), 1)
            with act.Fori(0, KD // 2) as i:
                a7.turn()
                for u in U:
                    s_ = u % 2
                    act.wait_ge(p7.sem, p7.after("gate", u, turn=i))
                    act.wait_ge(v7.sem, v7.after("pr", (u - 2) % 6, turn=i if u >= 2 else i - 1))
                    act.activation(sg[:, s_, P:T], bank[4 * s_][:, :], ACT.Tanh, scale=0.5)
                    act.activation(sg[:, s_, 0:P], bank[4 * s_ + 1][:, 0:P], ACT.Tanh, scale=0.5).then_inc(a7.step("sg", u), 1)

        @block.tensor
        def _(pe):
            p7.credit(pe)
            for i in range(16):
                pe.wait_ge(g7r.sem, g7r.after("r", i))
                if i >= 2:
                    pe.wait_ge(a7r.sem, a7r.after("r", i - 2))
                pe.matmul(bank[i % 2][:, :], ones, dg[:, i % 2, :], start=True, stop=True).then_inc(p7r.step("r", i), 1)
            pe.wait_ge(a7r.sem, a7r.after("r", 15))
            with pe.Fori(0, KD // 2) as i:
                p7.turn()
                for u in U:
                    s_, x, br = u % 2, u // 3, u % 3
                    last = i if u >= 2 else i - 1
                    if br == 0:
                        pe.wait_ge(got_m[x], 16 * (i + 1))
                    w = mring[:, x, (KD + 4) * P * br:(KD + 4) * P * (br + 1)].rearrange("p (k m) -> p k m", m=P)
                    pe.wait_ge(a7.sem, a7.after("sg", (u - 2) % 6, turn=last))
                    for k in range(KD):
                        pe.matmul(bank[4 * s_][:, :], w[:, k, :], hT[:, k, P:T], start=(k == 0), stop=(k == KD - 1))
                        mm = pe.matmul(bank[4 * s_ + 1][:, 0:P], w[:, k, :], hT[:, k, 0:P], start=(k == 0), stop=(k == KD - 1))
                    mm.then_inc(p7.step("gate", u), 1)
                    pe.wait_ge(v7.sem, v7.after("pr", (u - 2) % 6, turn=last))
                    y = branch[br]
                    for k in range(4):
                        pe.matmul(bank[4 * s_ + 2][:, :], w[:, KD + k, :], y[:, k, P:T], start=(k == 0), stop=(k == 3))
                        mm = pe.matmul(bank[4 * s_ + 3][:, 0:P], w[:, KD + k, :], y[:, k, 0:P], start=(k == 0), stop=(k == 3))
                    mm.then_inc(p7.step("proj", u), 1)

        @block.vector
        def _(dve):
            v7.credit(dve)
            with dve.Fori(0, KD // 2) as i:
                v7.turn()
                for u in U:
                    s_, x, br = u % 2, u // 3, u % 3
                    dve.wait_ge(a7.sem, a7.after("sg", u, turn=i))
                    dve.wait_ge(p7.sem, p7.after("proj", u, turn=i))
                    if br == 0:
                        dve.wait_ge(v7.sem, v7.after("add", (u - 1) % 6, turn=i if u else i - 1))
                    dst = acc[:, :] if br == 0 else pr[:, s_, :]
                    dve.scalar_tensor_tensor(dst[:, P:T], sg[:, s_, P:T], 1.0, bank[4 * s_ + 2][:, :], ALU.add, ALU.mult)
                    dve.scalar_tensor_tensor(dst[:, 0:P], sg[:, s_, 0:P], 1.0, bank[4 * s_ + 3][:, 0:P], ALU.add,
                                             ALU.mult).then_inc(v7.step("pr", u), 1)
                    if br:
                        dve.wait_ge(v7.sem, v7.after("pr", u, turn=i))
                        out = acc[:] if br == 1 else mT[:, bass.ds(2 * i + x, 1), :].rearrange("p a t -> p (a t)")
                        dve.tensor_tensor(out, acc[:], pr[:, s_, :], ALU.add).then_inc(v7.step("add", u), 1)
    if stop <= 7:
        return dict(locals())

    x1 = nc.alloc_sbuf_tensor_at("x1", [P, NT, D], F32, offset=yA_off)
    cursor[0] = stage7_keep
    pos2 = sb("pos2", [P, NT - 1, D])
    lnr = sb("lnr", [P, 2, D])
    h2 = sb("h2", [P, 3, D])
    st8 = sb("st8", [P, 2, 2, 6])
    mv8 = sb("mv8", [P, 2, NT, 2])
    rs8 = sb("rs8", [P, 2, NT])
    w_r = sb("w_r", [P, KD, NG + NE])
    h2d = nc.dram_tensor("h2_rows", (T, D), F32, kind="Internal").ap()
    yd = nc.dram_tensor("expert_rows", (2 * T, D), F32, kind="Internal").ap()
    got8 = nc.alloc_semaphore("got_ln_rows")
    got_x2 = nc.alloc_semaphore("got_x_again")
    sent8 = [nc.alloc_semaphore(f"h2_sent{i}") for i in range(3)]
    turns8 = lambda n, *parts: [(x, i - lag) for i in range(n) for lag, names in parts for x in names if 0 <= i - lag < NT]
    lv8 = turns8(NT + 1, (0, ("g0", "g1", "res", "s0", "s1", "mv")), (1, ("t0", "t1", "mv2")), (0, ("rec", "xn")), (1, ("rec2", "xn2")))
    v8 = Steps(nc, "out_vector", lv8)
    a8 = Steps(nc, "out_scalar", turns8(NT + 2, (2, ("h0", "h1")), (0, ("sqrt",)), (1, ("sqrt2",))))
    g8 = Steps(nc, "out_gpsimd", [("pos", t) for t in range(1, NT)] + turns8(NT + 1, (0, ("lg", "lb")), (1, ("sc", "sh"))))
    p8 = Steps(nc, "out_tensor", turns8(NT + 3, (0, ("mix",)), (2, ("tr",)), (3, ("lg",))))
    with nc.Block("out", no_gpsimd_drain=True) as block:
        @block.sync
        def _(sp):
            sp.dma_start(x1[:, 0, :], A["xp"]).then_inc(got_x2, 16)
            sp.dma_start(x1[:, 1:NT, :], A["xs"].rearrange("(t p) d -> p t d", p=P)).then_inc(got_x2, 16)
            sp.dma_start(pos2[:], A["pos"].rearrange("(t p) d -> p t d", p=P)).then_inc(got_x2, 16)
            sp.dma_start(lnr[:], A["ln"][0:2 * D].partition_broadcast(P).rearrange("p (a d) -> p a d", a=2)).then_inc(got8, 16)
            sp.dma_start(w_r[:], A["w_r"]).then_inc(got8, 16)
            for t in range(NT):
                sp.wait_ge(g8.sem, g8.after("sh", t))
                sp.dma_start(h2d[t * P:t * P + P, :], h2[:, t % 3, :]).then_inc(sent8[t % 3], 16)
            for x in range(3):
                sp.wait_ge(sent8[x], 16 * len(range(x, NT, 3)))

        @block.tensor
        def _(pe):
            def mix(t):
                for f in range(2):
                    if t >= 2:
                        pe.wait_ge(v8.sem, v8.after(f"g{f}", t - 2))
                    for k in range(KD):
                        mm = pe.matmul(bank[2 * (t % 2) + f][:, :], mT[:, k, tok(t)], w_out[:, k, 512 * f:512 * f + 512],
                                       start=(k == 0), stop=(k == KD - 1))
                mm.then_inc(p8.step("mix", t), 1)

            pe.wait_ge(got_wo, 16)
            for i in range(NT + 3):
                if i < NT:
                    mix(i)
                t = i - 2
                if 0 <= t < NT:
                    pe.wait_ge(g8.sem, g8.after("sh", t))
                    if t:
                        pe.wait_ge(a8.sem, a8.after("h1", t - 1))
                    for k in range(KD):
                        mm = pe.transpose(bank[4 + k // 4][:, P * (k % 4):P * (k % 4) + P], h2[:, t % 3, P * k:P * k + P], ident)
                    mm.then_inc(p8.step("tr", t), 1)
                t = i - 3
                if t >= 0:
                    pe.wait_ge(a8.sem, a8.after("h1", t))
                    if t == 0:
                        pe.wait_ge(got8, 32)
                    for k in range(KD):
                        mm = pe.matmul(bank[6][:, 64 * t:64 * t + NG + NE], hT[:, k, tok(t)], w_r[:, k, :], start=(k == 0), stop=(k == KD - 1))
                    mm.then_inc(p8.step("lg", t), 1)

        @block.scalar
        def _(act):
            for i in range(NT + 2):
                t = i - 2
                if t >= 0:
                    act.wait_ge(p8.sem, p8.after("tr", t))
                    for f in range(2):
                        act.activation(hT[:, 4 * f:4 * f + 4, tok(t)], bank[4 + f][:, :].rearrange("p (k m) -> p k m", m=P),
                                       ACT.Copy).then_inc(a8.step(f"h{f}", t), 1)
                if i < NT:
                    act.wait_ge(v8.sem, v8.after("mv", i))
                    act.activation(rs8[:, 0, i:i + 1], mv8[:, 0, i, 1:2], ACT.Sqrt, bias=col(E_LN)).then_inc(a8.step("sqrt", i), 1)
                t = i - 1
                if 0 <= t < NT:
                    act.wait_ge(v8.sem, v8.after("mv2", t))
                    act.activation(rs8[:, 1, t:t + 1], mv8[:, 1, t, 1:2], ACT.Sqrt, bias=col(E_LN)).then_inc(a8.step("sqrt2", t), 1)

        @block.gpsimd
        def _(pool):
            pool.wait_ge(got_x2, 48)
            for t in range(1, NT):
                pool.tensor_tensor(x1[:, t, :], x1[:, t, :], pos2[:, t - 1, :], ALU.add).then_inc(g8.step("pos", t), 1)
            pool.wait_ge(got8, 32)
            for i in range(NT + 1):
                if i < NT:
                    pool.wait_ge(v8.sem, v8.after("xn", i))
                    pool.tensor_tensor(x1[:, i, :], x1[:, i, :], lnr[:, 0, :], ALU.mult).then_inc(g8.step("lg", i), 1)
                    pool.wait_ge(g8.sem, g8.after("lg", i))
                    pool.tensor_tensor(x1[:, i, :], x1[:, i, :], lnr[:, 1, :], ALU.add).then_inc(g8.step("lb", i), 1)
                t = i - 1
                if t >= 0:
                    c, m_ = 1 if t else 0, h2[:, t % 3, :]
                    pool.wait_ge(v8.sem, v8.after("xn2", t))
                    pool.tensor_tensor(m_, m_, rows[:, 3, c, :], ALU.mult).then_inc(g8.step("sc", t), 1)
                    pool.wait_ge(g8.sem, g8.after("sc", t))
                    pool.tensor_tensor(m_, m_, rows[:, 2, c, :], ALU.add).then_inc(g8.step("sh", t), 1)

        @block.vector
        def _(dve):
            def residual(t):
                c = 1 if t else 0
                m_ = h2[:, t % 3, :]
                if t >= 3:
                    dve.wait_ge(p8.sem, p8.after("tr", t - 3))
                    dve.wait_ge(sent8[t % 3], 16 * (t // 3))
                dve.wait_ge(p8.sem, p8.after("mix", t))
                for f in range(2):
                    fs = slice(512 * f, 512 * f + 512)
                    dve.tensor_tensor(m_[:, fs], bank[2 * (t % 2) + f][:, :], rows[:, 1, c, fs], ALU.mult).then_inc(v8.step(f"g{f}", t), 1)
                dve.wait_ge(v8.sem, v8.after("g1", t))
                if t:
                    dve.wait_ge(g8.sem, g8.after("pos", t))
                dve.scalar_tensor_tensor(x1[:, t, :], x1[:, t, :], ALPHA, m_, ALU.mult, ALU.add).then_inc(v8.step("res", t), 1)
                dve.wait_ge(v8.sem, v8.after("res", t))
                for i in range(2):
                    dve.bn_stats(st8[:, 0, i, :], x1[:, t, 512 * i:512 * i + 512]).then_inc(v8.step(f"s{i}", t), 1)
                dve.wait_ge(v8.sem, v8.after("s1", t))
                dve.bn_aggr(mv8[:, 0, t, :], st8[:, 0, :, :]).then_inc(v8.step("mv", t), 1)

            def norm(t):
                dve.wait_ge(a8.sem, a8.after("sqrt", t))
                dve.reciprocal(rs8[:, 0, t:t + 1], rs8[:, 0, t:t + 1]).then_inc(v8.step("rec", t), 1)
                dve.wait_ge(v8.sem, v8.after("rec", t))
                dve.tensor_scalar(x1[:, t, :], x1[:, t, :], mv8[:, 0, t, 0:1], rs8[:, 0, t:t + 1], ALU.subtract,
                                  ALU.mult).then_inc(v8.step("xn", t), 1)

            def moments2(t):
                dve.wait_ge(g8.sem, g8.after("lb", t))
                for i in range(2):
                    dve.bn_stats(st8[:, 1, i, :], x1[:, t, 512 * i:512 * i + 512]).then_inc(v8.step(f"t{i}", t), 1)
                dve.wait_ge(v8.sem, v8.after("t1", t))
                dve.bn_aggr(mv8[:, 1, t, :], st8[:, 1, :, :]).then_inc(v8.step("mv2", t), 1)

            def norm2(t):
                dve.wait_ge(a8.sem, a8.after("sqrt2", t))
                dve.reciprocal(rs8[:, 1, t:t + 1], rs8[:, 1, t:t + 1]).then_inc(v8.step("rec2", t), 1)
                dve.wait_ge(v8.sem, v8.after("rec2", t))
                dve.tensor_scalar(h2[:, t % 3, :], x1[:, t, :], mv8[:, 1, t, 0:1], rs8[:, 1, t:t + 1], ALU.subtract,
                                  ALU.mult).then_inc(v8.step("xn2", t), 1)

            dve.wait_ge(got_x2, 48)
            for i in range(NT + 1):
                if i < NT:
                    residual(i)
                if i:
                    moments2(i - 1)
                if i < NT:
                    norm(i)
                if i:
                    norm2(i - 1)
    if stop <= 8:
        return dict(locals())

    NX = 2 * T // P
    NU = NE + NX
    EW = KD * 2 * DE + 2 * D
    cursor[0] = rows_off + 2 * D * 4
    ew = sb("ew", [P, 4, EW])
    route_base = cursor[0]
    lgt = sb("lgt", [P, NT, NG + NE])
    lw = sb("lw", [P, NT, NG, EPG])
    ohg = sb("ohg", [P, NT, NG])
    ohk = sb("ohk", [P, 2, NT, EPG])
    w8 = sb("w8", [P, 5, NT, EPG])
    w1s = sb("w1s", [P, 12, NT])
    mk = sb("mk", [P, 2, NT, NE])
    mall = sb("mall", [P, NT, NE])
    rk = sb("rk", [P, 2, NT])
    rkj = sb("rkj", [P, 2, NT])
    unit = sb("unit", [P, 2, NT])
    mku = sb("mku", [P, 2, NT, NU])
    rhs = sb("rhs", [P, 2, NT, 3, NU])
    oneh = nc.alloc_sbuf_tensor_at("oneh", [P, 2 * NT, P], F32, offset=hT_off)
    tmp = sb("tmp", [P, NT, 2, NE])
    more = sb("more", [P, 3, NE])
    whose = sb("whose", [P, NX, NE])
    tab = sb("tab", [P, 2, 2, NU])
    cursor[0] = base0 - RING * 4096 * 4
    idx = sb("idx", [P, 2, NU], I32)
    gate = sb("gate", [P, NU])
    extra = sb("extra", [P, 1 + NX], I32)
    moe_keep = cursor[0]
    got_e = [nc.alloc_semaphore(f"got_expert{x}") for x in range(4)]
    G_MAX, G_MIN, G_SUM, G_P, T_M1, T_M2, T_MN, T_E, T_S, W_1, W_2, _ = range(12)
    lv9 = ["lgt", "gmax", "geq", "gv", "gmin", "goh", "gsub", "gsum", "gp", "lsel0", "lsel1", "m1", "eq1", "v1", "mn1", "oh1", "le2",
           "m2", "eq2", "v2", "mn2", "oh2", "dm", "s", "r", "w1", "w2", "w2b", "mk1", "mk2", "mall"]
    lv9 += [("rank", k) for k in range(2)] + [("rank1", k) for k in range(2)] + [(x, j) for j in range(1, NT) for x in ("more", "rkj")]
    lv9 += ["rkl"] + [("oneh", n) for n in range(2 * NT)] + ["upto", "before"]
    lv9 += [("off", k) for k in range(2)] + [("off1", k) for k in range(2)] + ["u0", "u1", "u2"]
    lv9 += [(x, k) for k in range(2) for x in ("mku", "mkx")] + [("rhs", k, i) for k in range(2) for i in range(3)]
    lv9 += ["whose", "whose1", "extra", "n_extra", "gate", "tab", "tmp", "idx"]
    v9 = Steps(nc, "route_vector", [x if isinstance(x, tuple) else (x,) for x in lv9])
    a9, p9 = Steps(nc, "route_scalar", [("gexp",), ("dexp",)]), Steps(nc, "route_tensor", [("rank",), ("tab",)])
    EXPERT = lambda n: A["experts"][bass.ds(n, 1)].rearrange("a p n -> (a p) n")
    with nc.Block("route", no_gpsimd_drain=True) as block:
        @block.sync
        def _(sp):
            for x in range(4):
                sp.dma_start(ew[:, x, :], A["experts"][x]).then_inc(got_e[x], 16)

        @block.scalar
        def _(act):
            act.wait_ge(v9.sem, v9.after("gsub"))
            act.activation(w8[:, 0, :, 0:NG], w8[:, 0, :, 0:NG], ACT.Exp).then_inc(a9.step("gexp"), 1)
            act.wait_ge(v9.sem, v9.after("dm"))
            act.activation(w1s[:, T_E, :], w1s[:, T_E, :], ACT.Exp).then_inc(a9.step("dexp"), 1)

        @block.tensor
        def _(pe):
            pe.wait_ge(v9.sem, v9.after("mall"))
            su = cst[:, C_SU:C_SU + P]
            for t in range(NT):
                for t2 in range(t + 1):
                    pe.matmul(bank[0][:, NE * t:NE * t + NE], su if t2 == t else ones, mall[:, t2, :], start=(t2 == 0), stop=(t2 == t))
            for t in range(NT):
                mm = pe.matmul(bank[0][:, NE * NT:NE * NT + NE], ones, mall[:, t, :], start=(t == 0), stop=(t == NT - 1))
            mm.then_inc(p9.step("rank"), 1)
            pe.wait_ge(v9.sem, v9.after("rhs", 1, 2))
            for t in range(NT):
                for k in range(2):
                    mm = pe.matmul(bank[1][:, 0:3 * NU], oneh[:, 2 * t + k, :], rhs[:, k, t, :, :].rearrange("p a e -> p (a e)"),
                                   start=(t == 0 and k == 0), stop=(t == NT - 1 and k == 1))
            mm.then_inc(p9.step("tab"), 1)

        @block.vector
        def _(dve):
            s1 = lambda x: w1s[:, x, :]
            b_ = lambda ap, n: bc(ap.unsqueeze(2), P, NT, n)
            iota = lambda n: bc(cst[:, C_IOTA:C_IOTA + n].unsqueeze(1), P, NT, n)
            dve.tensor_tensor(lgt[:], bank[6][:, 0:64 * NT].rearrange("p (t x) -> p t x", x=64)[:, :, 0:NG + NE],
                                  bc(row[:, R_BRG:R_BRG + NG + NE].unsqueeze(1), P, NT, NG + NE), ALU.add).then_inc(v9.step("lgt"), 1)
            dve.wait_ge(v9.sem, v9.after("lgt"))
            lg, le = lgt[:, :, 0:NG], lgt[:, :, NG:].rearrange("p t (g e) -> p t g e", g=NG)

            def first_max(x, n, best, low, work, out, names):
                dve.tensor_reduce(s1(best), x, AX, ALU.max).then_inc(v9.step(names[0]), 1)
                dve.wait_ge(v9.sem, v9.after(names[0]))
                dve.tensor_tensor(work, x, b_(s1(best), n), ALU.is_equal).then_inc(v9.step(names[1]), 1)
                dve.wait_ge(v9.sem, v9.after(names[1]))
                dve.scalar_tensor_tensor(work, work, -64.0, iota(n), ALU.mult, ALU.add).then_inc(v9.step(names[2]), 1)
                dve.wait_ge(v9.sem, v9.after(names[2]))
                dve.tensor_reduce(s1(low), work, AX, ALU.min).then_inc(v9.step(names[3]), 1)
                dve.wait_ge(v9.sem, v9.after(names[3]))
                dve.tensor_tensor(out, work, b_(s1(low), n), ALU.is_equal).then_inc(v9.step(names[4]), 1)
                dve.wait_ge(v9.sem, v9.after(names[4]))

            first_max(lg, NG, G_MAX, G_MIN, w8[:, 1, :, 0:NG], ohg[:], ("gmax", "geq", "gv", "gmin", "goh"))
            dve.tensor_tensor(w8[:, 0, :, 0:NG], lg, b_(s1(G_MAX), NG), ALU.subtract).then_inc(v9.step("gsub"), 1)
            dve.wait_ge(v9.sem, v9.after("gsub"))
            dve.wait_ge(a9.sem, a9.after("gexp"))
            dve.tensor_reduce(s1(G_SUM), w8[:, 0, :, 0:NG], AX, ALU.add).then_inc(v9.step("gsum"), 1)
            dve.wait_ge(v9.sem, v9.after("gsum"))
            dve.reciprocal(s1(G_P), s1(G_SUM)).then_inc(v9.step("gp"), 1)
            dve.wait_ge(v9.sem, v9.after("gp"))
            dve.tensor_tensor(lw[:], le, bc(ohg[:].unsqueeze(3), P, NT, NG, EPG), ALU.mult).then_inc(v9.step("lsel0"), 1)
            dve.wait_ge(v9.sem, v9.after("lsel0"))
            dve.tensor_reduce(w8[:, 2, :, :], lw[:].rearrange("p t g e -> p t e g"), AX, ALU.add).then_inc(v9.step("lsel1"), 1)
            dve.wait_ge(v9.sem, v9.after("lsel1"))
            first_max(w8[:, 2, :, :], EPG, T_M1, T_MN, w8[:, 3, :, :], ohk[:, 0, :, :], ("m1", "eq1", "v1", "mn1", "oh1"))
            dve.scalar_tensor_tensor(w8[:, 4, :, :], ohk[:, 0, :, :], NEG, w8[:, 2, :, :], ALU.mult, ALU.add).then_inc(v9.step("le2"), 1)
            dve.wait_ge(v9.sem, v9.after("le2"))
            first_max(w8[:, 4, :, :], EPG, T_M2, T_MN, w8[:, 3, :, :], ohk[:, 1, :, :], ("m2", "eq2", "v2", "mn2", "oh2"))
            dve.tensor_tensor(s1(T_E), s1(T_M2), s1(T_M1), ALU.subtract).then_inc(v9.step("dm"), 1)
            dve.wait_ge(v9.sem, v9.after("dm"))
            dve.wait_ge(a9.sem, a9.after("dexp"))
            dve.tensor_scalar(s1(T_S), s1(T_E), 1.0, None, ALU.add).then_inc(v9.step("s"), 1)
            dve.wait_ge(v9.sem, v9.after("s"))
            dve.reciprocal(s1(T_S), s1(T_S)).then_inc(v9.step("r"), 1)
            dve.wait_ge(v9.sem, v9.after("r"))
            dve.tensor_tensor(s1(W_1), s1(T_S), s1(G_P), ALU.mult).then_inc(v9.step("w1"), 1)
            dve.wait_ge(v9.sem, v9.after("w1"))
            dve.tensor_tensor(s1(W_2), s1(W_1), s1(T_E), ALU.mult).then_inc(v9.step("w2"), 1)
            dve.wait_ge(v9.sem, v9.after("w2"))
            dve.tensor_copy(s1(T_S), s1(W_2)).then_inc(v9.step("w2b"), 1)
            dve.wait_ge(v9.sem, v9.after("w2b"))
            for k in range(2):
                dve.tensor_tensor(mk[:, k, :, :].rearrange("p t (g e) -> p t g e", g=NG), bc(ohg[:].unsqueeze(3), P, NT, NG, EPG),
                                      bc(ohk[:, k, :, :].unsqueeze(2), P, NT, NG, EPG), ALU.mult).then_inc(v9.step(f"mk{k + 1}"), 1)
                dve.wait_ge(v9.sem, v9.after(f"mk{k + 1}"))
            dve.tensor_tensor(mall[:], mk[:, 0, :, :], mk[:, 1, :, :], ALU.add).then_inc(v9.step("mall"), 1)
            dve.wait_ge(v9.sem, v9.after("mall"))
            dve.wait_ge(p9.sem, p9.after("rank"))
            rank = bank[0][:, 0:NE * NT].rearrange("p (t e) -> p t e", e=NE)
            for k in range(2):
                dve.tensor_tensor(tmp[:, :, k, :], mk[:, k, :, :], rank, ALU.mult).then_inc(v9.step("rank", k), 1)
                dve.wait_ge(v9.sem, v9.after("rank", k))
            for k in range(2):
                dve.tensor_reduce(rk[:, k, :], tmp[:, :, k, :], AX, ALU.add).then_inc(v9.step("rank1", k), 1)
                dve.wait_ge(v9.sem, v9.after("rank1", k))
            count = bank[0][:, NE * NT:NE * NT + NE]
            for j in range(1, NT):
                if j == 1:
                    dve.tensor_scalar(more[:, 0, :], count, float(P), None, ALU.is_gt).then_inc(v9.step("more", j), 1)
                    dve.tensor_scalar(rkj[:], rk[:], float(P), None, ALU.is_ge).then_inc(v9.step("rkj", j), 1)
                else:
                    dve.scalar_tensor_tensor(more[:, 0, :], count, float(P * j), more[:, 0, :], ALU.is_gt, ALU.add).then_inc(v9.step("more", j), 1)
                    dve.scalar_tensor_tensor(rkj[:], rk[:], float(P * j), rkj[:], ALU.is_ge, ALU.add).then_inc(v9.step("rkj", j), 1)
                dve.wait_ge(v9.sem, v9.after("rkj", j))
            dve.scalar_tensor_tensor(rk[:], rkj[:], -float(P), rk[:], ALU.mult, ALU.add).then_inc(v9.step("rkl"), 1)
            dve.wait_ge(v9.sem, v9.after("rkl"))
            for n in range(2 * NT):
                dve.tensor_scalar(oneh[:, n, :], cst[:, C_IOTA:C_IOTA + P], rk[:, n % 2, n // 2:n // 2 + 1], None,
                                  ALU.is_equal).then_inc(v9.step("oneh", n), 1)
            dve.tensor_tensor_scan(more[:, 1, :], ones[:, 0:NE], more[:, 0, :], 0.0, ALU.mult, ALU.add).then_inc(v9.step("upto"), 1)
            dve.wait_ge(v9.sem, v9.after("upto"))
            dve.tensor_tensor(more[:, 2, :], more[:, 1, :], more[:, 0, :], ALU.subtract).then_inc(v9.step("before"), 1)
            dve.wait_ge(v9.sem, v9.after("before"))
            for k in range(2):
                dve.tensor_tensor(tmp[:, :, k, :], mk[:, k, :, :], bc(more[:, 2, :].unsqueeze(1), P, NT, NE), ALU.mult).then_inc(v9.step("off", k), 1)
            dve.wait_ge(v9.sem, v9.after("off", 1))
            for k in range(2):
                dve.tensor_reduce(unit[:, k, :], tmp[:, :, k, :], AX, ALU.add).then_inc(v9.step("off1", k), 1)
            dve.wait_ge(v9.sem, v9.after("off1", 1))
            dve.tensor_tensor(unit[:], unit[:], rkj[:], ALU.add).then_inc(v9.step("u0"), 1)
            dve.wait_ge(v9.sem, v9.after("u0"))
            dve.scalar_tensor_tensor(unit[:], rkj[:], 0.0, unit[:], ALU.is_gt, ALU.mult).then_inc(v9.step("u1"), 1)
            dve.wait_ge(v9.sem, v9.after("u1"))
            dve.tensor_scalar(unit[:], unit[:], -1.0, None, ALU.add).then_inc(v9.step("u2"), 1)
            dve.wait_ge(v9.sem, v9.after("u2"))
            for k in range(2):
                dve.scalar_tensor_tensor(mku[:, k, :, 0:NE], b_(rkj[:, k, :], NE), 0.0, mk[:, k, :, :], ALU.is_equal, ALU.mult).then_inc(v9.step("mku", k), 1)
                dve.tensor_tensor(mku[:, k, :, NE:NU], iota(NX), b_(unit[:, k, :], NX), ALU.is_equal).then_inc(v9.step("mkx", k), 1)
            dve.wait_ge(v9.sem, v9.after("mkx", 1))
            for k in range(2):
                for i in range(2):
                    c = C_TOKP if k and i else C_TOK1
                    dve.tensor_tensor(rhs[:, k, :, i, :], mku[:, k, :, :], b_(cst[:, c:c + NT], NU), ALU.mult).then_inc(v9.step("rhs", k, i), 1)
                dve.scalar_tensor_tensor(rhs[:, k, :, 2, :], mku[:, k, :, :], 0.5, b_(s1(W_1 + k), NU), ALU.mult,
                                         ALU.mult).then_inc(v9.step("rhs", k, 2), 1)
            sums = bc(more[:, 1, :].unsqueeze(1), P, NX, NE)
            dve.tensor_tensor(whose[:], sums, bc(cst[:, C_IOTA:C_IOTA + NX].unsqueeze(2), P, NX, NE), ALU.is_le).then_inc(v9.step("whose"), 1)
            dve.wait_ge(v9.sem, v9.after("whose"))
            dve.tensor_reduce(tmp[:, 0, 0, 0:NX], whose[:], AX, ALU.add).then_inc(v9.step("whose1"), 1)
            dve.wait_ge(v9.sem, v9.after("whose1"))
            dve.tensor_scalar(extra[:, 1:1 + NX], tmp[:, 0, 0, 0:NX], float(NE - 1), None, ALU.min).then_inc(v9.step("extra"), 1)
            dve.tensor_scalar(extra[:, 0:1], more[:, 1, NE - 1:NE], 1.0, None, ALU.mult).then_inc(v9.step("n_extra"), 1)
            dve.wait_ge(p9.sem, p9.after("tab"))
            slots = bank[1][:, 0:2 * NU].rearrange("p (a e) -> p a e", a=2)
            dve.tensor_scalar(gate[:], bank[1][:, 2 * NU:3 * NU], 1.0, None, ALU.mult).then_inc(v9.step("gate"), 1)
            dve.tensor_scalar(tab[:, 0, :, :], slots, -1.0, None, ALU.add).then_inc(v9.step("tab"), 1)
            dve.wait_ge(v9.sem, v9.after("tab"))
            dve.tensor_scalar(tab[:, 1, :, :], tab[:, 0, :, :], 0.0, 65536.0, ALU.is_lt, ALU.mult).then_inc(v9.step("tmp"), 1)
            dve.wait_ge(v9.sem, v9.after("tmp"))
            dve.tensor_tensor(idx[:], tab[:, 0, :, :], tab[:, 1, :, :], ALU.add).then_inc(v9.step("idx"), 1)
    if stop <= 9:
        return dict(locals())

    xg = nc.alloc_sbuf_tensor_at("xg", [P, 4, D], F32, offset=hT_off)
    xgT = nc.alloc_sbuf_tensor_at("xgT", [P, 2, KD, P], F32, offset=yA_off + 2 * H * T * 4)
    cursor[0] = route_base
    uh = sb("uh", [P, 2, DE])
    hid = sb("hid", [P, 2, DE])
    hidT = sb("hidT", [P, 2, 2 * P])
    cursor[0] = moe_keep
    yo = sb("yo", [P, 4, D])
    ig = sb("ig", [P, 4, 1], I32)
    isc = sb("isc", [P, 4, 1], I32)
    gsc = sb("gsc", [P, 4, 1])
    gathered = [nc.alloc_semaphore(f"gathered{i}") for i in range(4)]
    scattered = [nc.alloc_semaphore(f"scattered{i}") for i in range(4)]
    zeroed = nc.alloc_semaphore("gather_zeroed")

    class Marks:
        def __init__(self, name, labels):
            self.sem = {x: nc.alloc_semaphore(f"{name}_{x}") for x in labels}

    pt_m = Marks("te", ("xT", "hT", "f1", "f2"))
    ac_m = Marks("se", ("x", "tanh", "h", "y"))
    ve_m = Marks("ve", ("x", "u", "hid", "y"))
    po_m = Marks("pe", ("small", "rows", "gather", "scatter"))

    def sync_units(sp):
        with sp.Fori(0, NE // 4 - 1) as i:
            for x in range(4):
                sp.wait_ge(pt_m.sem["f2"], 4 * i + x + 1)
                sp.dma_start(ew[:, x, :], EXPERT(4 * i + (x + 4))).then_inc(got_e[x], 16)
        units = sp.value_load(extra[0:1, 0:1], min_val=0, max_val=NX)
        for u in range(NX):
            n = NE + u
            with sp.If(units > u):
                sp.wait_ge(pt_m.sem["f2"], n - 4 + 1)
                expert = sp.value_load(extra[0:1, 1 + u:2 + u], min_val=0, max_val=NE - 1)
                sp.dma_start(ew[:, n % 4, :], EXPERT(expert)).then_inc(got_e[n % 4], 16)

    last_row = []

    def pool_units(pool):
        def prepare(n, x):
            if not (isinstance(n, int) and n < 4):
                pool.wait_ge(pt_m.sem["xT"], n - 4 + 1)
                pool.wait_ge(ve_m.sem["hid"], n - 4 + 1)
            pool.tensor_copy(ig[:, x, :], idx[:, 0, bass.ds(n, 1)])
            pool.tensor_copy(gsc[:, x, :], gate[:, bass.ds(n, 1)]).then_inc(po_m.sem["small"], 1)
            pool.wait_ge(po_m.sem["small"], n + 1)
            pool.sem_inc(po_m.sem["gather"], 1)
            pool.indirect_dma_start(xg[:, x, :], None, h2d, bass.IndirectOffsetOnAxis(ig[:, x, :], 0),
                                    bounds_check=last_row[0], oob_is_err=False).then_inc(gathered[x], 16)

        def scatter(n, x):
            if not (isinstance(n, int) and n < 4):
                pool.wait_ge(scattered[x], quarter16(n, x) - 16)
            pool.tensor_copy(isc[:, x, :], idx[:, 1, bass.ds(n, 1)]).then_inc(po_m.sem["rows"], 1)
            pool.wait_ge(po_m.sem["rows"], n + 1)
            pool.wait_ge(ac_m.sem["y"], n + 1)
            pool.wait_ge(ve_m.sem["y"], n + 1)
            pool.sem_inc(po_m.sem["scatter"], 1)
            pool.indirect_dma_start(yd, bass.IndirectOffsetOnAxis(isc[:, x, :], 0), yo[:, x, :], None,
                                    bounds_check=last_row[1], oob_is_err=False).then_inc(scattered[x], 16)

        for x in range(4):
            prepare(x, x)
        for x in range(4):
            prepare(x + 4, x)
            scatter(x, x)
        with pool.Fori(1, NE // 4 - 1) as i:
            for x in range(4):
                prepare(4 * i + (x + 4), x)
                scatter(4 * i + x, x)
        for x in range(4):
            scatter(NE - 4 + x, x)
        for x in range(4):
            pool.wait_ge(scattered[x], quarter16(NE - 4 + x, x))
        units = pool.value_load(extra[0:1, 0:1], min_val=0, max_val=NX)
        for u in range(-1, NX):
            n = NE + u
            if u + 1 < NX:
                with pool.If(units > u + 1):
                    prepare(n + 1, (n + 1) % 4)
                    pool.nop()
            if u >= 0:
                with pool.If(units > u):
                    scatter(n, n % 4)
                    pool.wait_ge(scattered[n % 4], quarter16(n, n % 4))
                    pool.nop()

    def pe_units(pe):
        def xT(n, x):
            pe.wait_ge(gathered[x], quarter16(n, x))
            if not (isinstance(n, int) and n < 1):
                pe.wait_ge(ac_m.sem["x"], n - 1 + 1)
                pe.wait_ge(ve_m.sem["x"], n - 1 + 1)
            for k in range(KD):
                mm = pe.transpose(bank[k // 4][:, P * (k % 4):P * (k % 4) + P], xg[:, x, P * k:P * k + P], ident)
            mm.then_inc(pt_m.sem["xT"], 1)

        def hT_(n, x):
            pe.wait_ge(ve_m.sem["hid"], n + 1)
            for k in range(2):
                mm = pe.transpose(bank[4][:, P * k:P * k + P], hid[:, x % 2, P * k:P * k + P], ident)
            mm.then_inc(pt_m.sem["hT"], 1)

        def ffn1(n, x):
            pe.wait_ge(got_e[x], quarter16(n, x))
            pe.wait_ge(ac_m.sem["x"], n + 1)
            pe.wait_ge(ve_m.sem["x"], n + 1)
            if not (isinstance(n, int) and n < 2):
                pe.wait_ge(ve_m.sem["hid"], n - 2 + 1)
            for k in range(KD):
                mm = pe.matmul(bank[2 + x % 2][:, :], xgT[:, x % 2, k, :], ew[:, x, 2 * DE * k:2 * DE * (k + 1)], start=(k == 0), stop=(k == KD - 1))
            mm.then_inc(pt_m.sem["f1"], 1)

        def ffn2(n, x):
            pe.wait_ge(ac_m.sem["h"], n + 1)
            if not (isinstance(n, int) and n < 1):
                pe.wait_ge(ac_m.sem["y"], n - 1 + 1)
                pe.wait_ge(ve_m.sem["y"], n - 1 + 1)
            for f in range(2):
                for k in range(2):
                    at = KD * 2 * DE + D * k + 512 * f
                    mm = pe.matmul(bank[5 + f][:, :], hidT[:, x % 2, P * k:P * k + P], ew[:, x, at:at + 512], start=(k == 0), stop=(k == 1))
            mm.then_inc(pt_m.sem["f2"], 1)

        def step(n, x, more=True):
            hT_(n - 1, (x - 1) % 4)
            ffn1(n, x)
            if more:
                xT(n + 1, (x + 1) % 4)
            ffn2(n - 1, (x - 1) % 4)

        xT(0, 0)
        ffn1(0, 0)
        xT(1, 1)
        step(1, 1)
        with pe.Fori(0, NE // 4 - 1) as i:
            for x in range(4):
                step(4 * i + (2 + x), (2 + x) % 4)
        step(NE - 2, 2)
        step(NE - 1, 3, more=False)
        hT_(NE - 1, 3)
        ffn2(NE - 1, 3)
        units = pe.value_load(extra[0:1, 0:1], min_val=0, max_val=NX)
        for n in range(NE, NU):
            with pe.If(units > n - NE):
                xT(n, n % 4)
                ffn1(n, n % 4)
                hT_(n, n % 4)
                ffn2(n, n % 4)
                pe.nop()

    def act_units(act):
        def x_(n, x):
            act.wait_ge(pt_m.sem["xT"], n + 1)
            if not (isinstance(n, int) and n < 2):
                act.wait_ge(pt_m.sem["f1"], n - 2 + 1)
            act.activation(xgT[:, x % 2, 0:4, :], bank[0][:, :].rearrange("p (k m) -> p k m", m=P), ACT.Copy).then_inc(ac_m.sem["x"], 1)

        def h_(n, x):
            act.wait_ge(pt_m.sem["hT"], n + 1)
            if not (isinstance(n, int) and n < 2):
                act.wait_ge(pt_m.sem["f2"], n - 2 + 1)
            act.activation(hidT[:, x % 2, :], bank[4][:, 0:2 * P], ACT.Copy).then_inc(ac_m.sem["h"], 1)

        def tanh(n, x):
            act.wait_ge(pt_m.sem["f1"], n + 1)
            if not (isinstance(n, int) and n < 2):
                act.wait_ge(ve_m.sem["hid"], n - 2 + 1)
            act.activation(uh[:, x % 2, :], bank[2 + x % 2][:, 0:DE], ACT.Tanh, scale=0.5).then_inc(ac_m.sem["tanh"], 1)

        def y_(n, x):
            act.wait_ge(pt_m.sem["f2"], n + 1)
            if not (isinstance(n, int) and n < 4):
                act.wait_ge(scattered[x], quarter16(n, x) - 16)
            act.activation(yo[:, x, 0:512], bank[5][:, :], ACT.Copy).then_inc(ac_m.sem["y"], 1)

        def step(n, x, more=True):
            h_(n - 1, (x - 1) % 4)
            tanh(n, x)
            if more:
                x_(n + 1, (x + 1) % 4)
            y_(n - 1, (x - 1) % 4)

        x_(0, 0)
        tanh(0, 0)
        x_(1, 1)
        for n in range(1, 5):
            step(n, n % 4)
        with act.Fori(0, NE // 4 - 2) as i:
            for x in range(4):
                step(4 * i + (5 + x), (1 + x) % 4)
        for n in range(NE - 3, NE):
            step(n, n % 4, more=(n < NE - 1))
        h_(NE - 1, 3)
        y_(NE - 1, 3)
        units = act.value_load(extra[0:1, 0:1], min_val=0, max_val=NX)
        for n in range(NE, NU):
            with act.If(units > n - NE):
                x_(n, n % 4)
                tanh(n, n % 4)
                h_(n, n % 4)
                y_(n, n % 4)
                act.nop()

    def dve_units(dve):
        def x_(n, x):
            dve.wait_ge(pt_m.sem["xT"], n + 1)
            if not (isinstance(n, int) and n < 2):
                dve.wait_ge(pt_m.sem["f1"], n - 2 + 1)
            dve.tensor_copy(xgT[:, x % 2, 4:8, :], bank[1][:, :].rearrange("p (k m) -> p k m", m=P)).then_inc(ve_m.sem["x"], 1)

        def hid_(n, x):
            dve.wait_ge(ac_m.sem["tanh"], n + 1)
            if not (isinstance(n, int) and n < 2):
                dve.wait_ge(pt_m.sem["hT"], n - 2 + 1)
            b = bank[2 + x % 2]
            dve.scalar_tensor_tensor(uh[:, x % 2, :], uh[:, x % 2, :], 1.0, b[:, 0:DE], ALU.add, ALU.mult).then_inc(ve_m.sem["u"], 1)
            dve.wait_ge(ve_m.sem["u"], n + 1)
            dve.wait_ge(po_m.sem["small"], n + 1)
            dve.scalar_tensor_tensor(hid[:, x % 2, :], uh[:, x % 2, :], gsc[:, x, :], b[:, DE:2 * DE], ALU.mult,
                                     ALU.mult).then_inc(ve_m.sem["hid"], 1)

        def y_(n, x):
            dve.wait_ge(pt_m.sem["f2"], n + 1)
            if not (isinstance(n, int) and n < 4):
                dve.wait_ge(scattered[x], quarter16(n, x) - 16)
            dve.tensor_copy(yo[:, x, 512:D], bank[6][:, :]).then_inc(ve_m.sem["y"], 1)

        def step(n, x, more=True):
            hid_(n, x)
            if more:
                x_(n + 1, (x + 1) % 4)
            y_(n - 1, (x - 1) % 4)

        x_(0, 0)
        hid_(0, 0)
        x_(1, 1)
        for n in range(1, 5):
            step(n, n % 4)
        with dve.Fori(0, NE // 4 - 2) as i:
            for x in range(4):
                step(4 * i + (5 + x), (1 + x) % 4)
        for n in range(NE - 3, NE):
            step(n, n % 4, more=(n < NE - 1))
        y_(NE - 1, 3)
        units = dve.value_load(extra[0:1, 0:1], min_val=0, max_val=NX)
        for n in range(NE, NU):
            with dve.If(units > n - NE):
                x_(n, n % 4)
                hid_(n, n % 4)
                y_(n, n % 4)
                dve.nop()

    def quarter16(n, x):
        return (n - x) * 4 + 16

    with nc.Block("experts", no_gpsimd_drain=True) as block:
        @block.sync
        def _(sp):
            sync_units(sp)

        @block.gpsimd
        def _(pool):
            last_row.extend([pool.to_reg(T - 1), pool.to_reg(2 * T - 1)])
            pool.memset(xg[:], 0.0).then_inc(zeroed, 1)
            pool.wait_ge(zeroed, 1)
            pool_units(pool)

        @block.tensor
        def _(pe):
            pe_units(pe)

        @block.scalar
        def _(act):
            act_units(act)

        @block.vector
        def _(dve):
            dve_units(dve)
    if stop <= 10:
        return dict(locals())

    cursor[0] = route_base - 4 * EW * 4
    yt = sb("yt", [P, NT, 2, D])
    lnr2 = sb("lnr2", [P, 2, D])
    st11 = sb("st11", [P, 2, 6])
    mv11 = sb("mv11", [P, NT, 2])
    rs11 = sb("rs11", [P, NT])
    got_y = [nc.alloc_semaphore(f"got_y{i}") for i in range(NT)]
    got_l2 = nc.alloc_semaphore("got_ln2_rows")
    out_sent = nc.alloc_semaphore("out_sent")
    v11 = Steps(nc, "final_vector", turns8(NT + 1, (0, ("sum", "gate", "res", "s0", "s1", "mv")), (1, ("rec", "xn"))))
    a11 = Steps(nc, "final_scalar", [("sqrt", t) for t in range(NT)])
    g11 = Steps(nc, "final_gpsimd", [(x, t) for t in range(NT) for x in ("lg", "lb")])
    with nc.Block("final", no_gpsimd_drain=True) as block:
        @block.sync
        def _(sp):
            for t in range(NT):
                sp.dma_start(yt[:, t, :, :], yd.rearrange("(k r) d -> r k d", k=2)[t * P:t * P + P]).then_inc(got_y[t], 16)
                if t == 0:
                    sp.dma_start(lnr2[:], A["ln"][2 * D:4 * D].partition_broadcast(P).rearrange("p (a d) -> p a d", a=2)).then_inc(got_l2, 16)
            for t in range(NT):
                sp.wait_ge(g11.sem, g11.after("lb", t))
                sp.dma_start(O["y"][t * P:t * P + P, :], x1[:, t, :]).then_inc(out_sent, 16)
            sp.wait_ge(out_sent, 16 * NT)

        @block.gpsimd
        def _(pool):
            pool.wait_ge(got_l2, 16)
            for t in range(NT):
                pool.wait_ge(v11.sem, v11.after("xn", t))
                pool.tensor_tensor(x1[:, t, :], x1[:, t, :], lnr2[:, 0, :], ALU.mult).then_inc(g11.step("lg", t), 1)
                pool.wait_ge(g11.sem, g11.after("lg", t))
                pool.tensor_tensor(x1[:, t, :], x1[:, t, :], lnr2[:, 1, :], ALU.add).then_inc(g11.step("lb", t), 1)

        @block.scalar
        def _(act):
            for t in range(NT):
                act.wait_ge(v11.sem, v11.after("mv", t))
                act.activation(rs11[:, t:t + 1], mv11[:, t, 1:2], ACT.Sqrt, bias=col(E_LN)).then_inc(a11.step("sqrt", t), 1)

        @block.vector
        def _(dve):
            def residual(t):
                dve.wait_ge(got_y[t], 16)
                dve.tensor_tensor(yt[:, t, 0, :], yt[:, t, 0, :], yt[:, t, 1, :], ALU.add).then_inc(v11.step("sum", t), 1)
                dve.wait_ge(v11.sem, v11.after("sum", t))
                dve.tensor_tensor(yt[:, t, 0, :], yt[:, t, 0, :], rows[:, 0, 1 if t else 0, :], ALU.mult).then_inc(v11.step("gate", t), 1)
                dve.wait_ge(v11.sem, v11.after("gate", t))
                dve.scalar_tensor_tensor(x1[:, t, :], x1[:, t, :], ALPHA, yt[:, t, 0, :], ALU.mult, ALU.add).then_inc(v11.step("res", t), 1)
                dve.wait_ge(v11.sem, v11.after("res", t))
                for i in range(2):
                    dve.bn_stats(st11[:, i, :], x1[:, t, 512 * i:512 * i + 512]).then_inc(v11.step(f"s{i}", t), 1)
                dve.wait_ge(v11.sem, v11.after("s1", t))
                dve.bn_aggr(mv11[:, t, :], st11[:]).then_inc(v11.step("mv", t), 1)

            def norm(t):
                dve.wait_ge(a11.sem, a11.after("sqrt", t))
                dve.reciprocal(rs11[:, t:t + 1], rs11[:, t:t + 1]).then_inc(v11.step("rec", t), 1)
                dve.wait_ge(v11.sem, v11.after("rec", t))
                dve.tensor_scalar(x1[:, t, :], x1[:, t, :], mv11[:, t, 0:1], rs11[:, t:t + 1], ALU.subtract, ALU.mult).then_inc(v11.step("xn", t), 1)

            for i in range(NT + 1):
                if i < NT:
                    residual(i)
                if i:
                    norm(i - 1)
    return dict(locals())


def host_layout(i):
    import numpy as np

    f = {k: np.asarray(v) for k, v in i.items()}
    out = {}
    rows = lambda *names: [f[n].reshape(-1, P) for n in names]
    out["vecs"] = np.ascontiguousarray(np.concatenate(rows(
        "b_mod", "conv_a", "conv_b_w", "conv_b_b", "lru_ba", "lru_bx", "lru_lambda", "delta_norm", "mlstm_norm",
        "state_lru", "state_mlstm_n")).T)
    out["rows"] = np.concatenate([f[n].reshape(-1) for n in (
        "delta_a_log", "delta_dt_bias", "mlstm_bi", "mlstm_bf", "state_mlstm_m", "b_rg", "b_re")])
    out["cond"] = np.ascontiguousarray(np.stack([f["c_ctx"].reshape(KD, P).T, f["c"].reshape(KD, P).T], axis=2))
    out["xp"], out["xs"] = f["x_prompt"][0], f["x_sample"][0]
    w_in, w_mod = f["w_in"][0], f["w_mod"][0]
    at = {0: 1536, 1: 2576, 2: 0, 3: 512, 4: 1024, 5: 2048, 6: 3088, 7: 3600, 8: 4112, 9: 4624}
    blocks = np.empty((len(BLOCKS), P, 4096), w_in.dtype)
    for n, (kind, m) in enumerate(BLOCKS):
        w = w_mod[:, 512 * m:512 * m + 512] if kind == "mod" else w_in[:, at[m]:at[m] + 512]
        blocks[n].reshape(P, KD, 512)[:] = w.reshape(KD, P, 512).transpose(1, 0, 2)
    out["blocks"] = blocks
    small = np.concatenate([w_in[:, 2560:2576], w_in[:, 5136:5152]], axis=1)
    out["w_small"] = np.ascontiguousarray(small.reshape(KD, P, 32).transpose(1, 0, 2))
    out["w_lru"] = np.ascontiguousarray(np.stack([f["lru_wa"][0], f["lru_wx"][0]]).transpose(3, 0, 1, 2, 4))
    out["s_delta"] = np.ascontiguousarray(f["state_delta"][0, 0].transpose(0, 2, 1, 3).reshape(2, P, H * HD))
    out["s_mc"] = np.ascontiguousarray(f["state_mlstm_C"][0, 0].transpose(0, 2, 1, 3).reshape(2, P, H * HD))
    merge = np.empty((KD, P, 3, KD + 4, P), w_in.dtype)
    for b, name in enumerate(("w_pa", "w_pb", "w_pc")):
        gate = w_in[:, 5152 + D * b:5152 + D * (b + 1)].reshape(KD, P, KD, P)
        merge[:, :, b, 0:KD] = gate.transpose(2, 1, 0, 3)
        merge[:, :, b, KD:] = f[name][0].reshape(4, P, KD, P).transpose(2, 1, 0, 3)
    out["merge"] = merge.reshape(KD, P, -1)
    out["w_out"] = np.ascontiguousarray(f["w_out"][0].reshape(KD, P, D).transpose(1, 0, 2))
    out["w_r"] = np.ascontiguousarray(np.concatenate([f["w_rg"][0], f["w_re"][0]], axis=1).reshape(KD, P, NG + NE).transpose(1, 0, 2))
    out["ln"] = np.concatenate([f[n].reshape(-1) for n in ("ln1_g", "ln1_b", "ln2_g", "ln2_b")])
    experts = np.empty((NE, P, KD * 2 * DE + 2 * D), w_in.dtype)
    first = experts[:, :, :KD * 2 * DE].reshape(NE, P, KD, 2, DE)
    for b, name in enumerate(("w_e1", "w_e3")):
        first[:, :, :, b] = f[name][0].reshape(NE, KD, P, DE).transpose(0, 2, 1, 3)
    experts[:, :, KD * 2 * DE:].reshape(NE, P, 2, D)[:] = f["w_e2"][0].reshape(NE, 2, P, D).transpose(0, 2, 1, 3)
    out["experts"] = experts
    out.update(shape_constants())
    return out


def shape_constants():
    import numpy as np

    p = np.arange(P)
    c = np.zeros((P, N_CONST), np.float32)
    c[:, C_ID:C_ID + P] = np.eye(P)
    c[:, C_TRI:C_TRI + P] = p[:, None] <= p[None]
    c[:, C_TRI + P:C_TRI + 2 * P] = p[:, None] >= p[None]
    c[:, C_ONE:C_ONE + P] = 1.0
    c[:, C_NEG:C_NEG + P] = np.where(p[None] <= p[:, None], 0.0, NEG)
    c[:, C_NEG + P:C_NEG + 2 * P] = np.where(p[None] >= p[:, None], 0.0, NEG)
    c[:, C_SU:C_SU + P] = p[:, None] < p[None]
    c[:, C_IOTA:C_IOTA + NT * P] = np.arange(NT * P)
    c[:, C_COL:C_COL + len(COLS)] = COLS
    c[:, C_TOK1:C_TOK1 + NT] = p[:, None] + P * np.arange(NT) + 1
    c[:, C_TOKP:C_TOKP + NT] = p[:, None] + P * np.arange(NT) + 1 + T
    lev = np.zeros((P, 2, LEVELS, P), np.int32)
    for n in range(LEVELS):
        s = 1 << n
        pair = (p[:, None] // (2 * s) == p[None] // (2 * s)) & (p[:, None] // s != p[None] // s)
        lev[:, 0, n] = pair & (p[:, None] > p[None])
        lev[:, 1, n] = pair & (p[:, None] < p[None])
    rows, grid = T_LAT // 64, 64
    freqs = np.exp(-math.log(10000.0) * np.arange(D // 4, dtype=np.float32) / (D // 4)).astype(np.float32)
    r, q = np.meshgrid(np.arange(rows, dtype=np.float32), np.arange(grid, dtype=np.float32), indexing="ij")
    ar, ac = r.reshape(-1, 1) * freqs, q.reshape(-1, 1) * freqs
    pos = np.concatenate([np.sin(ar), np.cos(ar), np.sin(ac), np.cos(ac)], axis=-1).astype(np.float32)
    return {"consts": c, "levels": lev, "pos": pos}


OUTPUTS = {"lru": (P, 8), "delta": (2, P, H * HD), "mc": (2, P, H * HD), "mn": (2, P, H), "mm": (8,), "y": (T, D)}


def build(nc, shapes, stop=99):
    A = {n: nc.dram_tensor(f"in_{n}", s, mybir.dt.from_np(d), kind="ExternalInput").ap() for n, (s, d) in shapes.items()}
    O = {n: nc.dram_tensor(f"out_{n}", s, F32, kind="ExternalOutput").ap() for n, s in OUTPUTS.items()}
    return program(nc, A, O, stop)


def unlay(o):
    import numpy as np

    per_head = lambda a: np.ascontiguousarray(a.reshape(2, P, H, HD).transpose(0, 2, 1, 3))[None, None]
    return (o["y"][:T_CTX][None], o["y"][T_CTX:][None], per_head(o["delta"]),
            np.ascontiguousarray(o["lru"].reshape(P, 2, 4).transpose(1, 2, 0)).reshape(1, 1, 2, 512), per_head(o["mc"]),
            np.ascontiguousarray(o["mn"].transpose(0, 2, 1))[None, None], o["mm"].reshape(1, 1, 2, H))


def kernel(**inputs):
    import concourse.bacc as bacc
    from concourse.bass_utils import run_bass_kernel_spmd

    arrays = host_layout(inputs)
    nc = bacc.Bacc("TRN2", target_bir_lowering=False, num_devices=1)
    build(nc, {n: (a.shape, a.dtype) for n, a in arrays.items()})
    r = run_bass_kernel_spmd(nc, [{f"in_{n}": a for n, a in arrays.items()}], core_ids=[0])
    return unlay({n: r.results[0][f"out_{n}"] for n in OUTPUTS})
```
